# Optimizing a Trainium2 kernel written in Bass

```python
import jax, jax.numpy as jnp
from jax import lax
import numpy as np
import math

D_MODEL = 1024
BATCH = 1
SEQ = 256
DEPTH = 2

A_HEADS = 16
A_KV_HEADS = 4
A_HEAD_DIM = 64
A_REP = A_HEADS // A_KV_HEADS
IDX_HEADS = 8
IDX_DIM = 64
IDX_TOPK_MAX = 256
Q_BLOCK = 128
A_Q = A_HEADS * A_HEAD_DIM
A_KV = A_KV_HEADS * A_HEAD_DIM
A_IN = A_Q + 2 * A_KV + IDX_HEADS * IDX_DIM + IDX_DIM + IDX_HEADS
A_SPLITS = (A_Q, A_Q + A_KV, A_Q + 2 * A_KV, A_Q + 2 * A_KV + IDX_HEADS * IDX_DIM,
            A_Q + 2 * A_KV + IDX_HEADS * IDX_DIM + IDX_DIM)

B_HEADS = 4
B_DK = D_MODEL // 2 // B_HEADS
B_DV = D_MODEL // B_HEADS
B_GATE_RANK = 16
B_GATE_TAU = 16.0
B_CHUNK = 64
B_QK = B_HEADS * B_DK
B_V = B_HEADS * B_DV
B_IN = 2 * B_QK + 2 * B_V + B_GATE_RANK
B_SPLITS = (B_QK, 2 * B_QK, 2 * B_QK + B_V, 2 * B_QK + 2 * B_V)

D_FF = 4 * D_MODEL

ROPE_THETA = 500000.0
ROT_DIM = A_HEAD_DIM // 4
LN_EPS = 1e-5
RMS_EPS = 1e-6
DN_ALPHA = (2 * DEPTH) ** 0.25
DN_BETA = (8 * DEPTH) ** -0.25
N_A_LAYERS = (DEPTH + 1) // 2
N_B_LAYERS = DEPTH // 2


def layer_norm(x, g, b):
    xf = x.astype(jnp.float32)
    mu = jnp.mean(xf, axis=-1, keepdims=True)
    var = jnp.mean(jnp.square(xf - mu), axis=-1, keepdims=True)
    return ((xf - mu) * lax.rsqrt(var + LN_EPS) * g + b).astype(x.dtype)

def rotary_tables(positions):
    inv = ROPE_THETA ** (-jnp.arange(0, ROT_DIM, 2, dtype=jnp.float32) / ROT_DIM)
    ang = positions.astype(jnp.float32)[..., None] * inv
    return jnp.cos(ang), jnp.sin(ang)

def partial_rotary(t, cos, sin):
    half = cos.shape[-1]
    shape = cos.shape[:2] + (1,) * (t.ndim - 3) + (half,)
    c = cos.reshape(shape)
    s = sin.reshape(shape)
    t1 = t[..., :half].astype(jnp.float32)
    t2 = t[..., half:2 * half].astype(jnp.float32)
    return jnp.concatenate([(t1 * c - t2 * s).astype(t.dtype),
                            (t2 * c + t1 * s).astype(t.dtype),
                            t[..., 2 * half:]], axis=-1)

def dsa_mixer(x, cos, sin, w_in, w_o):
    bsz, L, _ = x.shape
    top_k = min(IDX_TOPK_MAX, L // 4)
    proj = x @ w_in
    q, k, v, iq, ik, iw = jnp.split(proj, A_SPLITS, axis=-1)
    q = partial_rotary(q.reshape(bsz, L, A_HEADS, A_HEAD_DIM), cos, sin)
    k = partial_rotary(k.reshape(bsz, L, A_KV_HEADS, A_HEAD_DIM), cos, sin)
    v = v.reshape(bsz, L, A_KV_HEADS, A_HEAD_DIM)
    iq = partial_rotary(iq.reshape(bsz, L, IDX_HEADS, IDX_DIM), cos, sin)
    ik = partial_rotary(ik, cos, sin)
    iw = iw.astype(jnp.float32) * IDX_HEADS ** -0.5
    key_idx = jnp.arange(L)

    def block(i):
        start = i * Q_BLOCK
        q_idx = start + jnp.arange(Q_BLOCK)
        iq_b = lax.dynamic_slice_in_dim(iq, start, Q_BLOCK, axis=1)
        iw_b = lax.dynamic_slice_in_dim(iw, start, Q_BLOCK, axis=1)
        s = jnp.einsum('bqhd,bsd->bqhs', iq_b, ik, preferred_element_type=jnp.float32) * IDX_DIM ** -0.5
        score = jnp.einsum('bqh,bqhs->bqs', iw_b, jax.nn.relu(s))
        causal = key_idx[None, :] <= q_idx[:, None]
        score = jnp.where(causal[None], score, -jnp.inf)
        _, sel = lax.top_k(score, top_k)
        valid = sel <= q_idx[None, :, None]
        k_sel = jax.vmap(lambda kk, ii: kk[ii])(k, sel)
        v_sel = jax.vmap(lambda vv, ii: vv[ii])(v, sel)
        q_b = lax.dynamic_slice_in_dim(q, start, Q_BLOCK, axis=1).reshape(bsz, Q_BLOCK, A_KV_HEADS, A_REP, A_HEAD_DIM)
        logits = jnp.einsum('bqgrd,bqkgd->bqgrk', q_b, k_sel, preferred_element_type=jnp.float32) * A_HEAD_DIM ** -0.5
        logits = jnp.where(valid[:, :, None, None, :], logits, -jnp.inf)
        p = jax.nn.softmax(logits, axis=-1)
        o = jnp.einsum('bqgrk,bqkgd->bqgrd', p.astype(v.dtype), v_sel)
        return o.reshape(bsz, Q_BLOCK, A_Q)

    out = lax.map(block, jnp.arange(L // Q_BLOCK))
    out = out.transpose(1, 0, 2, 3).reshape(bsz, L, A_Q)
    return out @ w_o

def gla_mixer(x, w_in, w_a2, b_a, g_norm, w_o):
    bsz, L, _ = x.shape
    n_c = L // B_CHUNK
    proj = x @ w_in
    q, k, v, r, a_low = jnp.split(proj, B_SPLITS, axis=-1)
    log_a = jax.nn.log_sigmoid((a_low @ w_a2 + b_a).astype(jnp.float32)) / B_GATE_TAU

    def to_chunks(t, d):
        return t.astype(jnp.float32).reshape(bsz, n_c, B_CHUNK, B_HEADS, d).transpose(1, 0, 3, 2, 4)

    qc = to_chunks(q, B_DK) * B_DK ** -0.5
    kc = to_chunks(k, B_DK)
    vc = to_chunks(v, B_DV)
    gc = to_chunks(log_a, B_DK)
    mask = jnp.tril(jnp.ones((B_CHUNK, B_CHUNK), dtype=bool))

    def step(state, inp):
        qi, ki, vi, gi = inp
        b = jnp.cumsum(gi, axis=2)
        b_last = b[:, :, -1:, :]
        diff = jnp.where(mask[None, None, :, :, None], b[:, :, :, None, :] - b[:, :, None, :, :], -jnp.inf)
        attn = jnp.einsum('bhid,bhjd,bhijd->bhij', qi, ki, jnp.exp(diff))
        intra = jnp.einsum('bhij,bhje->bhie', attn, vi)
        inter = jnp.einsum('bhid,bhde->bhie', qi * jnp.exp(b), state)
        new_state = jnp.exp(b_last)[:, :, 0, :, None] * state + jnp.einsum('bhjd,bhje->bhde', ki * jnp.exp(b_last - b), vi)
        return new_state, intra + inter

    state0 = jnp.zeros((bsz, B_HEADS, B_DK, B_DV), jnp.float32)
    _, outs = lax.scan(step, state0, (qc, kc, vc, gc))
    o = outs.transpose(1, 0, 3, 2, 4).reshape(bsz, L, B_HEADS, B_DV)
    o = o * lax.rsqrt(jnp.mean(jnp.square(o), axis=-1, keepdims=True) + RMS_EPS) * g_norm
    gate = jax.nn.silu(r.astype(jnp.float32).reshape(bsz, L, B_HEADS, B_DV))
    y = (o * gate).reshape(bsz, L, B_V).astype(x.dtype)
    return y @ w_o

def squared_relu_mlp(x, w_up, w_down):
    return jnp.square(jax.nn.relu(x @ w_up)) @ w_down

def first_inputs(seed: int = 0) -> dict:
    key = jax.random.key(seed)
    ks = jax.random.split(key, 16)
    f32 = jnp.float32

    def nrm(k, shape, fan_in, scale=1.0):
        return jax.random.normal(k, shape, f32) * (scale * fan_in ** -0.5)

    x = jax.random.normal(ks[0], (BATCH, SEQ, D_MODEL), f32)
    positions = jnp.broadcast_to(jnp.arange(SEQ, dtype=jnp.int32), (BATCH, SEQ))
    a_w_in = nrm(ks[1], (N_A_LAYERS, D_MODEL, A_IN), D_MODEL)
    a_w_o = nrm(ks[2], (N_A_LAYERS, A_Q, D_MODEL), A_Q, DN_BETA)
    b_w_in = nrm(ks[3], (N_B_LAYERS, D_MODEL, B_IN), D_MODEL)
    b_w_a2 = nrm(ks[4], (N_B_LAYERS, B_GATE_RANK, B_QK), B_GATE_RANK)
    b_b_a = 0.1 * jax.random.normal(ks[5], (N_B_LAYERS, B_QK), f32)
    b_g_norm = 1.0 + 0.02 * jax.random.normal(ks[6], (N_B_LAYERS, B_DV), f32)
    b_w_o = nrm(ks[7], (N_B_LAYERS, B_V, D_MODEL), B_V, DN_BETA)
    ln_mix_g = 1.0 + 0.02 * jax.random.normal(ks[8], (DEPTH, D_MODEL), f32)
    ln_mix_b = 0.02 * jax.random.normal(ks[9], (DEPTH, D_MODEL), f32)
    mlp_w_up = nrm(ks[10], (DEPTH, D_MODEL, D_FF), D_MODEL)
    mlp_w_down = nrm(ks[11], (DEPTH, D_FF, D_MODEL), D_FF, DN_BETA)
    ln_mlp_g = 1.0 + 0.02 * jax.random.normal(ks[12], (DEPTH, D_MODEL), f32)
    ln_mlp_b = 0.02 * jax.random.normal(ks[13], (DEPTH, D_MODEL), f32)
    return {'x': x, 'positions': positions, 'a_w_in': a_w_in, 'a_w_o': a_w_o,
            'b_w_in': b_w_in, 'b_w_a2': b_w_a2, 'b_b_a': b_b_a, 'b_g_norm': b_g_norm, 'b_w_o': b_w_o,
            'ln_mix_g': ln_mix_g, 'ln_mix_b': ln_mix_b, 'mlp_w_up': mlp_w_up, 'mlp_w_down': mlp_w_down,
            'ln_mlp_g': ln_mlp_g, 'ln_mlp_b': ln_mlp_b}

def first_block(x, positions, a_w_in, a_w_o, b_w_in, b_w_a2, b_b_a, b_g_norm, b_w_o,
              ln_mix_g, ln_mix_b, mlp_w_up, mlp_w_down, ln_mlp_g, ln_mlp_b):
    cos, sin = rotary_tables(positions)
    h = x
    for i in range(DEPTH):
        j = i // 2
        if i % 2 == 0:
            mix = dsa_mixer(h, cos, sin, a_w_in[j], a_w_o[j])
        else:
            mix = gla_mixer(h, b_w_in[j], b_w_a2[j], b_b_a[j], b_g_norm[j], b_w_o[j])
        h = layer_norm(DN_ALPHA * h + mix, ln_mix_g[i], ln_mix_b[i])
        h = layer_norm(DN_ALPHA * h + squared_relu_mlp(h, mlp_w_up[i], mlp_w_down[i]), ln_mlp_g[i], ln_mlp_b[i])
    return h


DEPTH_2 = 1

CHUNK = 64
MEM_LEN = 256
HEAD_DIM = 64
BR_W = 512
N_BRANCH = 4
A_HEADS_2 = BR_W // (2 * HEAD_DIM)
F_HEADS = BR_W // HEAD_DIM
CONV_W = BR_W
CONV_K = 31
SC_W = BR_W
SC_K = 3
IN_COLS = 3 * BR_W + (3 * BR_W + F_HEADS) + 2 * CONV_W + 3 * SC_W
X_HEADS = 4
X_HEAD_DIM = 128
X_W = X_HEADS * X_HEAD_DIM
D_FF_2 = 2816
FFN_K = 3
EPS = 1e-6


def _rms_norm(x, g):
    xf = x.astype(jnp.float32)
    y = xf * lax.rsqrt(jnp.mean(xf * xf, axis=-1, keepdims=True) + EPS)
    return (y * g.astype(jnp.float32)).astype(x.dtype)

def _layer_norm(x, g, b):
    xf = x.astype(jnp.float32)
    mu = jnp.mean(xf, axis=-1, keepdims=True)
    var = jnp.mean(jnp.square(xf - mu), axis=-1, keepdims=True)
    y = (xf - mu) * lax.rsqrt(var + EPS)
    return (y * g.astype(jnp.float32) + b.astype(jnp.float32)).astype(x.dtype)

def _dwconv_causal(x, w):
    K, C = w.shape
    return lax.conv_general_dilated(x, w[:, None, :].astype(x.dtype), window_strides=(1,),
                                    padding=[(K - 1, 0)], dimension_numbers=('NWC', 'WIO', 'NWC'),
                                    feature_group_count=C)

def _diff_attention(q, k, v, lam, t_pos):
    B, S, H = q.shape[:3]
    nb = S // Q_BLOCK
    scale = HEAD_DIM ** -0.5
    qb = q.reshape(B, nb, Q_BLOCK, H, 2, HEAD_DIM).transpose(1, 0, 2, 3, 4, 5)
    tq = t_pos.reshape(nb, Q_BLOCK)
    k_chunk = t_pos // CHUNK

    def one(args):
        q_blk, tq_blk = args
        s = jnp.einsum('bqhcd,bkhcd->bhcqk', q_blk, k, preferred_element_type=jnp.float32) * scale
        mask = k_chunk[None, :] <= (tq_blk // CHUNK)[:, None]
        p = jax.nn.softmax(jnp.where(mask, s, -jnp.inf), axis=-1)
        a = p[:, :, 0] - lam * p[:, :, 1]
        return jnp.einsum('bhqk,bkhe->bqhe', a.astype(v.dtype), v)

    o = lax.map(one, (qb, tq))
    return o.transpose(1, 0, 2, 3, 4).reshape(B, S, H, 2 * HEAD_DIM)

def _forgetting_attention(q, k, v, log_f, t_pos):
    B, S, H = q.shape[:3]
    nb = S // Q_BLOCK
    scale = HEAD_DIM ** -0.5
    c = jnp.cumsum(log_f.astype(jnp.float32), axis=1)
    c_k = c.transpose(0, 2, 1)
    qb = q.reshape(B, nb, Q_BLOCK, H, HEAD_DIM).transpose(1, 0, 2, 3, 4)
    cb = c.reshape(B, nb, Q_BLOCK, H).transpose(1, 0, 3, 2)
    tq = t_pos.reshape(nb, Q_BLOCK)

    def one(args):
        q_blk, c_blk, tq_blk = args
        s = jnp.einsum('bqhd,bkhd->bhqk', q_blk, k, preferred_element_type=jnp.float32) * scale
        s = s + c_blk[..., None] - c_k[:, :, None, :]
        mask = t_pos[None, :] <= tq_blk[:, None]
        p = jax.nn.softmax(jnp.where(mask, s, -jnp.inf), axis=-1)
        return jnp.einsum('bhqk,bkhd->bqhd', p.astype(v.dtype), v)

    o = lax.map(one, (qb, cb, tq))
    return o.transpose(1, 0, 2, 3, 4).reshape(B, S, H * HEAD_DIM)

def second_inputs(seed: int = 0) -> dict:
    key = jax.random.key(seed)
    ks = iter(jax.random.split(key, 48))
    L, D = DEPTH_2, D_MODEL

    def nrm(shape, scale):
        return jax.random.normal(next(ks), shape, jnp.float32) * scale

    def gain(shape):
        return 1.0 + nrm(shape, 0.05)

    return {
        "x": nrm((BATCH, SEQ, D), 1.0),
        "mem": nrm((BATCH, MEM_LEN, D), 1.0),
        "norm_mix_pre": gain((L, D)),
        "norm_mix_post": gain((L, D)),
        "w_in": nrm((L, D, IN_COLS), D ** -0.5),
        "b_fgt": 2.0 + nrm((L, F_HEADS), 0.1),
        "lam_q1": nrm((L, HEAD_DIM), 0.1),
        "lam_k1": nrm((L, HEAD_DIM), 0.1),
        "lam_q2": nrm((L, HEAD_DIM), 0.1),
        "lam_k2": nrm((L, HEAD_DIM), 0.1),
        "diff_norm": gain((L, 2 * HEAD_DIM)),
        "b_glu": nrm((L, 2 * CONV_W), 0.02),
        "conv_dw": nrm((L, CONV_K, CONV_W), CONV_K ** -0.5),
        "conv_dw_b": nrm((L, CONV_W), 0.02),
        "conv_ln_g": gain((L, CONV_W)),
        "conv_ln_b": nrm((L, CONV_W), 0.02),
        "sc_w": nrm((L, SC_K, SC_W), SC_K ** -0.5),
        "w_branch": nrm((L, N_BRANCH, BR_W, D), BR_W ** -0.5),
        "w_gate": nrm((L, D, N_BRANCH * D), D ** -0.5),
        "b_gate": nrm((L, N_BRANCH * D), 0.02),
        "w_out": nrm((L, D, D), D ** -0.5),
        "norm_x_pre": gain((L, D)),
        "norm_x_post": gain((L, D)),
        "norm_mem": gain((L, D)),
        "w_xq": nrm((L, D, X_W), D ** -0.5),
        "w_xkv": nrm((L, D, 2 * X_W), D ** -0.5),
        "w_xo": nrm((L, X_W, D), X_W ** -0.5),
        "norm_ffn_pre": gain((L, D)),
        "norm_ffn_post": gain((L, D)),
        "w_up": nrm((L, D, 2 * D_FF_2), D ** -0.5),
        "ffn_dw": nrm((L, FFN_K, 2 * D_FF_2), FFN_K ** -0.5),
        "ffn_dw_b": nrm((L, 2 * D_FF_2), 0.02),
        "w_down": nrm((L, D_FF_2, D), D_FF_2 ** -0.5),
    }

def second_block(x, mem, norm_mix_pre, norm_mix_post, w_in, b_fgt, lam_q1, lam_k1, lam_q2, lam_k2,
              diff_norm, b_glu, conv_dw, conv_dw_b, conv_ln_g, conv_ln_b, sc_w, w_branch, w_gate,
              b_gate, w_out, norm_x_pre, norm_x_post, norm_mem, w_xq, w_xkv, w_xo, norm_ffn_pre,
              norm_ffn_post, w_up, ffn_dw, ffn_dw_b, w_down):
    B, S, D = x.shape
    t_pos = jnp.arange(S, dtype=jnp.int32)
    sizes = [BR_W, BR_W, BR_W, BR_W, BR_W, BR_W, F_HEADS, 2 * CONV_W, SC_W, SC_W, SC_W]
    cuts = [int(v) for v in np.cumsum(sizes)[:-1]]

    for l in range(DEPTH_2):
        h = _rms_norm(x, norm_mix_pre[l])
        (a_q, a_k, a_v, f_q, f_k, f_v, f_g, c_u, s_x, s_b, s_c) = jnp.split(h @ w_in[l], cuts, axis=-1)

        lambda_init = 0.8 - 0.6 * math.exp(-0.3 * l)
        lam = (jnp.exp(jnp.sum(lam_q1[l].astype(jnp.float32) * lam_k1[l].astype(jnp.float32)))
               - jnp.exp(jnp.sum(lam_q2[l].astype(jnp.float32) * lam_k2[l].astype(jnp.float32))) + lambda_init)
        ya = _diff_attention(a_q.reshape(B, S, A_HEADS_2, 2, HEAD_DIM), a_k.reshape(B, S, A_HEADS_2, 2, HEAD_DIM),
                             a_v.reshape(B, S, A_HEADS_2, 2 * HEAD_DIM), lam, t_pos)
        ya = (_rms_norm(ya, diff_norm[l]) * (1.0 - lambda_init)).reshape(B, S, BR_W)

        log_f = jax.nn.log_sigmoid(f_g.astype(jnp.float32) + b_fgt[l].astype(jnp.float32))
        yf = _forgetting_attention(f_q.reshape(B, S, F_HEADS, HEAD_DIM), f_k.reshape(B, S, F_HEADS, HEAD_DIM),
                                   f_v.reshape(B, S, F_HEADS, HEAD_DIM), log_f, t_pos)

        c_a, c_g = jnp.split(c_u + b_glu[l], 2, axis=-1)
        yc = _dwconv_causal(c_a * jax.nn.sigmoid(c_g), conv_dw[l]) + conv_dw_b[l]
        yc = jax.nn.silu(_layer_norm(yc, conv_ln_g[l], conv_ln_b[l]))

        ys = s_b * _dwconv_causal(s_c * s_x, sc_w[l])

        br = jnp.stack([ya, yf, yc, ys], axis=2)
        proj = jnp.einsum('bsnc,ncd->bsnd', br, w_branch[l])
        gates = jax.nn.sigmoid(h @ w_gate[l] + b_gate[l]).reshape(B, S, N_BRANCH, D)
        mixed = jnp.sum(gates * proj, axis=2) @ w_out[l]
        x = x + _rms_norm(mixed, norm_mix_post[l])

        hx = _rms_norm(x, norm_x_pre[l])
        m = _rms_norm(mem, norm_mem[l])
        xq = (hx @ w_xq[l]).reshape(B, S, X_HEADS, X_HEAD_DIM)
        xk, xv = jnp.split(m @ w_xkv[l], 2, axis=-1)
        xk = xk.reshape(B, MEM_LEN, X_HEADS, X_HEAD_DIM)
        xv = xv.reshape(B, MEM_LEN, X_HEADS, X_HEAD_DIM)
        sx = jnp.einsum('bqhd,bkhd->bhqk', xq, xk, preferred_element_type=jnp.float32) * (X_HEAD_DIM ** -0.5)
        px = jax.nn.softmax(sx, axis=-1).astype(xv.dtype)
        ox = jnp.einsum('bhqk,bkhd->bqhd', px, xv).reshape(B, S, X_W) @ w_xo[l]
        x = x + _rms_norm(ox, norm_x_post[l])

        hf = _rms_norm(x, norm_ffn_pre[l])
        u = _dwconv_causal(hf @ w_up[l], ffn_dw[l]) + ffn_dw_b[l]
        u_g, u_v = jnp.split(u, 2, axis=-1)
        yff = (jax.nn.silu(u_g) * u_v) @ w_down[l]
        x = x + _rms_norm(yff, norm_ffn_post[l])

    return x


def setup_inputs(seed=0):
    out = dict(first_inputs(seed))
    for name, value in second_inputs(seed + 1).items():
        if name != "x":
            out[name + "_2"] = value
    return out


def reference(
    x, positions, a_w_in, a_w_o, b_w_in, b_w_a2, b_b_a, b_g_norm, b_w_o, ln_mix_g, ln_mix_b,
    mlp_w_up, mlp_w_down, ln_mlp_g, ln_mlp_b, mem_2, norm_mix_pre_2, norm_mix_post_2, w_in_2,
    b_fgt_2, lam_q1_2, lam_k1_2, lam_q2_2, lam_k2_2, diff_norm_2, b_glu_2, conv_dw_2,
    conv_dw_b_2, conv_ln_g_2, conv_ln_b_2, sc_w_2, w_branch_2, w_gate_2, b_gate_2, w_out_2,
    norm_x_pre_2, norm_x_post_2, norm_mem_2, w_xq_2, w_xkv_2, w_xo_2, norm_ffn_pre_2,
    norm_ffn_post_2, w_up_2, ffn_dw_2, ffn_dw_b_2, w_down_2,
):
    x = first_block(
        x, positions, a_w_in, a_w_o, b_w_in, b_w_a2, b_b_a, b_g_norm, b_w_o, ln_mix_g, ln_mix_b,
        mlp_w_up, mlp_w_down, ln_mlp_g, ln_mlp_b,
    )
    return second_block(
        x, mem_2, norm_mix_pre_2, norm_mix_post_2, w_in_2, b_fgt_2, lam_q1_2, lam_k1_2,
        lam_q2_2, lam_k2_2, diff_norm_2, b_glu_2, conv_dw_2, conv_dw_b_2, conv_ln_g_2,
        conv_ln_b_2, sc_w_2, w_branch_2, w_gate_2, b_gate_2, w_out_2, norm_x_pre_2,
        norm_x_post_2, norm_mem_2, w_xq_2, w_xkv_2, w_xo_2, norm_ffn_pre_2, norm_ffn_post_2,
        w_up_2, ffn_dw_2, ffn_dw_b_2, w_down_2,
    )


_drawn_inputs = setup_inputs


def setup_inputs(seed=0):
    import zlib

    import numpy as np

    out = dict(_drawn_inputs(seed))
    spreads = {}
    factors = {'b_b_a': 4.426,
     'b_g_norm': 8.0,
     'b_fgt_2': 32.856,
     'lam_q1_2': 4.431,
     'lam_k1_2': 3.186,
     'lam_k2_2': 2.822,
     'diff_norm_2': 2.768,
     'b_glu_2': 7.302,
     'conv_dw_b_2': 3.971,
     'conv_ln_g_2': 2.797,
     'conv_ln_b_2': 8.0,
     'b_gate_2': 8.0,
     'ffn_dw_b_2': 3.892}
    for name, (base, spread) in spreads.items():
        noise = np.random.default_rng([zlib.crc32(name.encode()), seed]).standard_normal(out[name].shape)
        drawn = base * np.exp(spread * noise) if base else spread * noise
        out[name] = __import__('jax').numpy.asarray(drawn.astype(out[name].dtype))
    for name, factor in factors.items():
        out[name] = (out[name] * factor).astype(out[name].dtype)
    return out
```

```python
import numpy as np
import concourse.bass as bass
from concourse import mybir
from concourse.alu_op_type import AluOpType as ALU
from contextlib import ExitStack

P = 128
S = 256
D = 1024
DB = D // P
RING = 4
UT = 16
UW = UT * P
AHEAD = 3
NEG = -1.0e30
TAKEN = -3.0e38
TOPK = min(256, S // 4)
ALPHA = 4 ** 0.25
CONV_K = 31
CPAD = CONV_K - 1
FB = 22
FH = FB // 2

VECTORS = [("ln_mix_g", 16), ("ln_mix_b", 16), ("ln_mlp_g", 16), ("ln_mlp_b", 16), ("b_b_a", 4), ("b_g_norm", 2),
           ("norm_mix_pre_2", 8), ("norm_mix_post_2", 8), ("norm_x_pre_2", 8), ("norm_x_post_2", 8),
           ("norm_mem_2", 8), ("norm_ffn_pre_2", 8), ("norm_ffn_post_2", 8), ("diff_norm_2", 1), ("b_glu_2", 8),
           ("conv_dw_b_2", 4), ("conv_ln_g_2", 4), ("conv_ln_b_2", 4), ("b_gate_2", 32), ("ffn_dw_b_2", 44),
           ("conv_dw_2", 4 * CONV_K), ("sc_w_2", 12), ("ffn_dw_2", 3 * 44)]
COL = {}
for _name, _n in VECTORS:
    COL[_name] = sum(n for m, n in VECTORS[:len(COL)])
NV = sum(n for _, n in VECTORS)

UNITS = [("iq", 2, 16), ("k", 1, 16), ("v", 1, 16), ("q", 4, 16), ("ao", 4, 16),
         ("up00", 8, 16), ("dn00", 8, 16), ("up01", 8, 16), ("dn01", 8, 16),
         ("gq", 2, 16), ("gk", 2, 16), ("gv", 4, 16), ("gr", 4, 16), ("go", 4, 16),
         ("up10", 8, 16), ("dn10", 8, 16), ("up11", 8, 16), ("dn11", 8, 16),
         ("aq", 2, 16), ("ak", 2, 16), ("av", 2, 16), ("fq", 2, 16), ("fk", 2, 16), ("fv", 2, 16),
         ("c", 4, 16), ("s", 6, 16), ("gate0", 4, 16), ("br0", 2, 16), ("gate1", 4, 16), ("br1", 2, 16),
         ("gate3", 4, 16), ("br3", 2, 16), ("gate2", 4, 16), ("br2", 2, 16), ("out", 4, 16),
         ("xk", 2, 16), ("xv", 2, 16), ("xq", 2, 16), ("xo", 2, 16),
         ("fu0", FH, 16), ("fd0", 8, FH), ("fu1", FH, 16), ("fd1", 8, FH)]
U0 = {}
NU = 0
for _name, _n, _t in UNITS:
    U0[_name] = NU
    NU += _n


def plan():
    job, last, n = {}, {}, [0]

    def add(name, i=0, unit=None, banks=1):
        job[name, i] = n[0]
        n[0] += banks
        if unit:
            last[U0[unit] + i] = n[0] - 1

    def units(name, count, banks=1):
        for i in range(count):
            add(name, i, name, banks)

    def norm(name, mean):
        if mean:
            add(name + "_mean")
        add(name + "_sq")

    units("iq", 2); add("ik"); add("iw"); add("rope", 0); add("rope", 1); add("rope", 2)
    units("k", 1); units("v", 1); add("rope", 3)
    for i in range(6):
        add("idx", i)
    units("q", 4)
    for i in range(4):
        add("rope", 4 + i)
    units("ao", 4); norm("ln0", True)
    for layer in range(2):
        for half in range(2):
            units(f"up{layer}{half}", 8); units(f"dn{layer}{half}", 8)
        norm(f"ln{2 * layer + 1}", True)
        if layer == 0:
            units("gq", 2); units("gk", 2); add("alow"); add("gate_a", 0); add("gate_a", 1)
            units("gv", 4)
            for i in range(4):
                add("gr", i, "gr"); add("level", i)
            for i in range(4, 7):
                add("level", i)
            add("kd", 0); add("kd", 1)
            for c in range(4):
                add("gla_o", c)
                if c < 3:
                    add("state", 2 * c); add("state", 2 * c + 1)
            add("gla_sq", 0); add("gla_sq", 1)
            units("go", 4); norm("ln2", True)
    add("pre_mix_sq")
    add("fg")
    for name in ("aq", "ak", "av", "fq", "fk", "fv", "c", "s"):
        units(name, dict((a, b) for a, b, _ in UNITS)[name])
    add("gate0", 0, "gate0"); add("ya_sq", 0); add("ya_sq", 1)
    for i in range(1, 4):
        add("gate0", i, "gate0")
    units("br0", 2, 2); units("gate1", 4); units("br1", 2, 2)
    units("gate3", 4); units("br3", 2, 2); add("conv_mean"); add("conv_sq"); units("gate2", 4); units("br2", 2, 2)
    units("out", 4); add("mem_sq"); add("post_mix_sq"); units("xk", 2); add("xv", 0, "xv"); add("pre_x_sq")
    add("xv", 1, "xv"); units("xq", 2); units("xo", 2, 2); add("post_x_sq"); add("pre_ffn_sq")
    for half in range(2):
        units(f"fu{half}", FH); units(f"fd{half}", 8)
    add("post_ffn_sq")
    return job, last


JOB, LAST = plan()

CONSTS = [("ident", P), ("ones", S), ("causal", S), ("chunk", S), ("perm", P), ("level", 7 * 64), ("scan", S),
          ("inv", 1), ("rot", 1), ("norot", 1), ("ln_eps", 1), ("rms_eps", 1), ("one", 1), ("zero", 1)]
CC = {}
for _name, _n in CONSTS:
    CC[_name] = sum(n for m, n in CONSTS[:len(CC)])
NC = sum(n for _, n in CONSTS)


def shape_constants():
    c = np.zeros((P, NC), np.float32)

    def put(name, a):
        c[:, CC[name]:CC[name] + a.shape[1]] = a

    i = np.arange(P)
    put("ident", np.eye(P))
    put("ones", np.ones((P, S)))
    put("causal", np.concatenate([np.zeros((P, P)), np.where(i[None] <= i[:, None], 0.0, NEG)], 1))
    put("chunk", np.concatenate([np.zeros((P, P)), np.where(i[None] // 64 <= i[:, None] // 64, 0.0, NEG)], 1))
    perm = np.zeros((P, P))
    for head in range(0, P, 64):
        for d in range(8):
            perm[head + d + 8, head + d] = -1.0
            perm[head + d, head + d + 8] = 1.0
    put("perm", perm)
    j, t = i[:, None] % 64, np.arange(64)[None]
    levels = []
    for l in range(6):
        half = 32 >> l
        levels.append((j // (2 * half) == t // (2 * half)) & (j // half % 2 == 0) & (t // half % 2 == 1))
    levels.append(j == t)
    put("level", np.concatenate(levels, 1).astype(np.float32))
    put("scan", np.broadcast_to((np.arange(S) % 64 != 0).astype(np.float32), (P, S)))
    rot = (i % 64 < 16).astype(np.float32)
    inv = np.float32(500000.0) ** (-np.arange(0, 16, 2, dtype=np.float32) / np.float32(16))
    put("inv", (rot * inv[i % 8])[:, None])
    put("rot", rot[:, None])
    put("norot", 1.0 - rot[:, None])
    put("ln_eps", np.full((P, 1), 1e-5))
    put("rms_eps", np.full((P, 1), 1e-6))
    put("one", np.ones((P, 1)))
    return c


def build(nc, units_d, x_d, mem_d, pos_d, vec_d, const_d, narrow_a_d, narrow_b_d, narrow_f_d, w_a2_d, b_fgt_d, lam_d, out_d):
    f32, f32r = mybir.dt.float32, mybir.dt.float32r
    i32 = mybir.dt.int32
    ACT, AX = mybir.ActivationFunctionType, mybir.AxisListType
    ctx = ExitStack()
    with ctx:
        def sem(name):
            return ctx.enter_context(nc.semaphore(name))

        def sbuf(name, shape, dt=f32, where=ctx):
            return where.enter_context(nc.sbuf_tensor(name, shape, dt))

        raw = [sbuf(f"raw{i}", [P, UW]) for i in range(RING)]
        whi = [sbuf(f"whi{i}", [P, UW], f32r) for i in range(RING)]
        wlo = [sbuf(f"wlo{i}", [P, UW], f32r) for i in range(RING)]
        h = sbuf("h", [P, DB, S])
        z = sbuf("z", [P, DB, S])
        xh = sbuf("xh", [P, DB, S], f32r)
        xl = sbuf("xl", [P, DB, S], f32r)
        consts = sbuf("consts", [P, NC])
        vec = sbuf("vec", [P, NV])
        hvec = sbuf("hvec", [P, 32 + 8 + 1])
        std = sbuf("std", [P, S])
        rstd = sbuf("rstd", [P, S])

        def const(name, a=0, b=None):
            n = dict(CONSTS)[name]
            return consts[:, CC[name] + a:CC[name] + (n if b is None else b)]

        def vcol(name, i=0):
            return vec[:, COL[name] + i:COL[name] + i + 1]

        ident, ones = const("ident"), const("ones", 0, P)

        lg = sbuf("lg", [P, 2, S])
        pr = [sbuf(f"pr{i}", [P, 2, S]) for i in range(2)]
        pT = [sbuf(f"pT{i}", [P, 4, P]) for i in range(2)]
        nmax = sbuf("nmax", [P, 2, 2])
        rsum = sbuf("rsum", [P, 2, 2])
        rinv = sbuf("rinv", [P, 2])

        def stage(*tensors):
            with ExitStack() as own:
                return [sbuf(t[0], t[1], t[2] if len(t) > 2 else f32, own) for t in tensors]

        (narrow_a, qT, kT, kswap, v_tok, iqT, ikT, cosT, sinT, ang, turns, posi, iw, work, selbias, rbuf0, rbuf1, rtmp,
         top8) = stage(
            ("narrow_a", [P, DB, 136]), ("qT", [P, 8, S]), ("kT", [P, 2, S]), ("kswap", [P, 2, S]),
            ("v_tok", [P, 2, S]), ("iqT", [P, 4, S]), ("ikT", [P, 1, S]), ("cosT", [P, S]), ("sinT", [P, S]),
            ("ang", [P, S]), ("turns", [P, S]), ("posi", [P, S], i32), ("iw", [P, 2, 8]), ("work", [P, 2, S]),
            ("selbias", [P, 2, S]), ("rbuf0", [P, 512]), ("rbuf1", [P, 512]), ("rtmp", [P, 2, S]), ("top8", [P, 8]))
        rbuf = [rbuf0, rbuf1]
        fh, fl, relu0, relu1, sqr0, sqr1 = stage(
            ("fh", [P, 16, S], f32r), ("fl", [P, 16, S], f32r), ("relu0", [P, 2, S]), ("relu1", [P, 2, S]),
            ("sqr0", [P, 2, S]), ("sqr1", [P, 2, S]))
        relu, sqr = [relu0, relu1], [sqr0, sqr1]
        narrow_b, w_a2, alow, gqT, gkT, gv_tok, rgate, gtmp, bcum, decay, qk, attnT, state = stage(
            ("narrow_b", [P, DB, 16]), ("w_a2", [16, 512]), ("alow", [16, S]), ("gqT", [P, 4, S]), ("gkT", [P, 4, S]),
            ("gv_tok", [P, 2, D]), ("rgate", [P, 8, S]), ("gtmp", [P, 4, S]), ("bcum", [P, 4, S]), ("decay", [P, 4, S]),
            ("qk", [P, 8, S]), ("attnT", [P, 8, 64]), ("state", [P, 4, S]))
        (narrow_f, aqT, gate, fqT, fkT, fv_tok, upad, conv, scpad, sgate, mtmp0, mtmp1, bhi, blo, lamv, lamt, fgt, fc,
         bfg) = stage(
            ("narrow_f", [P, DB, 8]), ("aqT", [P, 4, S]), ("gate", [P, 8, S]), ("fqT", [P, 4, S]), ("fkT", [P, 4, S]),
            ("fv_tok", [P, 2, 512]), ("upad", [P, 4, CPAD + S]), ("conv", [P, 4, S]), ("scpad", [P, 2, 2 + S]),
            ("sgate", [P, 4, S]), ("mtmp0", [P, 2, S]), ("mtmp1", [P, 2, S]), ("bhi", [P, 4, S], f32r),
            ("blo", [P, 4, S], f32r), ("lamv", [P, 4, 64]), ("lamt", [P, 8]), ("fgt", [8, S]), ("fc", [8, S]),
            ("bfg", [8, 1]))
        akT = gate[:, 0:4, :]
        av_tok = gate[:, 4:8, :].rearrange("p (t a) s -> p t (a s)", t=2)
        mtmp = [mtmp0, mtmp1]
        memT, xkT, xv_tok, xqT = stage(
            ("memT", [P, DB, S]), ("xkT", [P, 4, S]), ("xv_tok", [P, 2, 512]), ("xqT", [P, 4, S]))
        gh, gl, fpad0, fpad1, fconv, fth, fy = stage(
            ("gh", [P, FH, S], f32r), ("gl", [P, FH, S], f32r), ("fpad0", [P, 2, 2 + S]), ("fpad1", [P, 2, 2 + S]),
            ("fconv", [P, 2, 2, S]), ("fth", [P, 2, S]), ("fy", [P, 2, S]))
        fpad = [fpad0, fpad1]

        lin = [ctx.enter_context(nc.psum_tensor(f"lin{i}", [P, 2, S], f32)) for i in range(RING)]
        att = [ctx.enter_context(nc.psum_tensor(f"att{i}", [P, 512], f32)) for i in range(4)]

        raw_full = [sem(f"raw_full{i}") for i in range(RING)]
        hi_ready = sem("hi_ready")
        lo_ready = sem("lo_ready")
        job_done = sem("job_done")
        evac = [sem(f"evac{i}") for i in range(RING)]
        x_loaded, consts_loaded, vec_loaded = sem("x_loaded"), sem("consts_loaded"), sem("vec_loaded")
        pos_loaded, narrow_a_loaded, gla_loaded = sem("pos_loaded"), sem("narrow_a_loaded"), sem("gla_loaded")
        mix_loaded, mem_loaded, out_stored = sem("mix_loaded"), sem("mem_loaded"), sem("out_stored")
        split_hi, split_lo = sem("split_hi"), sem("split_lo")
        reduced, trig = sem("reduced"), sem("trig")
        roped, kswapped = sem("roped"), sem("kswapped")
        idx_acc, selected = sem("idx_acc"), sem("selected")
        lg_ready, neg_ready, exp_done, p_ready = sem("lg_ready"), sem("neg_ready"), sem("exp_done"), sem("p_ready")
        pT_psum, pT_sb, pv_psum, o_done = sem("pT_psum"), sem("pT_sb"), sem("pv_psum"), sem("o_done")
        centered, squared, sq_used, normed = sem("centered"), sem("squared"), sem("sq_used"), sem("normed")
        relu_done, sqr_done, fhi, flo = sem("relu_done"), sem("sqr_done"), sem("fhi"), sem("flo")
        softplus = sem("softplus")
        gr_tanh, lvl_arg, lvl_exp, lvl_qk, attn_acc = sem("gr_tanh"), sem("lvl_arg"), sem("lvl_exp"), sem("lvl_qk"), sem("attn_acc")
        kd_ready, q_decayed, gla_squared, gla_y = sem("kd_ready"), sem("q_decayed"), sem("gla_squared"), sem("gla_y")
        fg_soft, fc_ready = sem("fg_soft"), sem("fc_ready")
        lam_dot, lam_exp = sem("lam_dot"), sem("lam_exp")
        ya_squared, b_y, b_hi, b_lo = sem("ya_squared"), sem("b_y"), sem("b_hi"), sem("b_lo")
        mixed, conv_done, conv_normed, conv_tanh = sem("mixed"), sem("conv_done"), sem("conv_normed"), sem("conv_tanh")
        ff_conv, ff_tanh, ff_y, ff_hi, ff_lo = sem("ff_conv"), sem("ff_tanh"), sem("ff_y"), sem("ff_hi"), sem("ff_lo")
        dve_step, act_step = sem("dve_step"), sem("act_step")

        def counts(events):
            n, out = 0, {}
            for name, k in events:
                out[name] = n
                n += k
            return out

        SPLIT = counts([(e, 4) for e in ("x", "ao", "mlp0", "gla", "go", "mlp1", "mix", "out", "mem", "xq")] + [("xo", 2), ("ffn", 4)])
        NORMED = counts([(e, 4) for e in ("ln0", "ln1", "ln2", "ln3", "pre_mix", "mem", "post_mix", "pre_x", "post_x", "pre_ffn", "post_ffn")])
        SQ = counts([(e, 1) for e in ("ln0", "ln1", "ln2", "ln3", "pre_mix", "conv", "mem", "post_mix", "pre_x", "post_x", "pre_ffn", "post_ffn")])
        CENTERED = {"ln0": 0, "ln1": 4, "ln2": 8, "ln3": 12, "conv": 16}

        def squares_before(name):
            return sum(2 if n == "conv" else 4 for n in SQ if SQ[n] < SQ[name])

        def used_before(name):
            return sum(1 if n == "conv" else 3 for n in SQ if SQ[n] < SQ[name])

        def per(n, g, step):
            return n if g is None else n + g * step

        def evacuated(eng, j, g=None):
            eng.wait_ge(evac[j % RING], per(j // RING + 1, g, 1))

        def filled(eng, j, g=None):
            eng.wait_ge(job_done, per(j + 1, g, RING))

        class Chain:

            def __init__(self, eng, s):
                self.eng, self.sem, self.n, self.g, self.step = eng, s, 0, None, 0

            def link(self, ins):
                ins.then_inc(self.sem, 1)
                self.n += 1
                self.eng.wait_ge(self.sem, per(self.n, self.g, self.step))

            def enter(self, g, step):
                self.g, self.step, self.first = g, step, self.n

            def leave(self, times):
                assert self.n - self.first == self.step, (self.n - self.first, self.step)
                self.n, self.g = self.first + times * self.step, None

        UNITS_ATT = [("A", j, t) for j in range(8) for t in range(2)] + [("D", j, t) for j in range(4) for t in range(2)] \
            + [("F", j, t) for j in range(4) for t in range(2)] + [("X", j, t) for j in range(4) for t in range(2)]
        ATT0 = {k: [u[0] for u in UNITS_ATT].index(k) for k in "ADFX"}

        def att_keys(u):
            k, j, t = UNITS_ATT[u]
            return S if k == "X" else P * (t + 1)

        def att_mats(u):
            return 1 if UNITS_ATT[u][0] == "X" else 2

        def att_out(u):
            k, j, t = UNITS_ATT[u]
            return {"A": qT, "D": aqT, "F": fqT, "X": xqT}[k][:, j, t * P:(t + 1) * P]

        block = ctx.enter_context(nc.Block())
        SEGMENTS = []
        for name, n, tiles in UNITS:
            if SEGMENTS and SEGMENTS[-1][2] == tiles:
                SEGMENTS[-1][1] += n
            else:
                SEGMENTS.append([U0[name], n, tiles])

        @block.sync
        def _(sp):
            def load(u, tiles, g=None):
                if u >= RING:
                    sp.wait_ge(lo_ready, per(u - RING + 1, g, RING))
                w = tiles * P
                sp.dma_start(raw[u % RING][:, 0:w], units_d[per(u, g, RING), :, 0:w]).then_inc(raw_full[u % RING], 16)

            sp.dma_start(h[:], x_d).then_inc(x_loaded, 16)
            for u in range(RING):
                load(u, UT)
            for start, n, tiles in SEGMENTS:
                if start == 0:
                    start, n = RING, n - RING
                if n >= RING:
                    with sp.Fori(0, n // RING) as g:
                        for j in range(RING):
                            load(start + j, tiles, g)
                for u in range(start + n // RING * RING, start + n):
                    load(u, tiles)
            for c in range(4):
                sp.wait_ge(normed, NORMED["post_ffn"] + c + 1)
                sp.dma_start(out_d[:, 2 * c:2 * c + 2, :], h[:, 2 * c:2 * c + 2, :]).then_inc(out_stored, 16)
            sp.wait_ge(out_stored, 64)

        @block.gpsimd
        def _(pool):
            def low_part(u, tiles, g=None):
                pool.wait_ge(hi_ready, per(u + 1, g, RING))
                w = tiles * P
                nc.gpsimd.tensor_tensor(wlo[u % RING][:, 0:w], raw[u % RING][:, 0:w],
                                        whi[u % RING][:, 0:w].bitcast(f32), ALU.subtract).then_inc(lo_ready, 1)

            for start, n, tiles in SEGMENTS:
                if n >= RING:
                    with pool.Fori(0, n // RING) as g:
                        for j in range(RING):
                            low_part(start + j, tiles, g)
                for u in range(start + n // RING * RING, start + n):
                    low_part(u, tiles)

        @block.tensor
        def _(pe):
            mm = nc.tensor.matmul

            def bank(j, g=None):
                if j >= RING:
                    evacuated(pe, j - RING, g)
                return lin[j % RING]

            def three(out, w, a, first, last):
                mm(out, w[0], a[0], start=first, stop=False)
                mm(out, w[0], a[1], start=False, stop=False)
                return mm(out, w[1], a[0], start=False, stop=last)

            def tile(u, i, n=1):
                return (whi[u % RING][:, i * P:(i + n) * P], wlo[u % RING][:, i * P:(i + n) * P])

            def arrived(u, g=None):
                pe.wait_ge(lo_ready, per(u + 1, g, RING))

            def unit_up(u, j, g=None):
                arrived(u, g)
                o = bank(j, g)
                for m in range(2):
                    for k in range(DB):
                        last = three(o[:, m, :], tile(u, m * DB + k), (xh[:, k, :], xl[:, k, :]), k == 0, k == DB - 1)
                last.then_inc(job_done, 1)

            def unit_down(u, j, a, n, g=None):
                arrived(u, g)
                o = bank(j, g)
                for k in range(n):
                    last = three(o[:, 0, :], tile(u, k), (a[0][:, k, :], a[1][:, k, :]), k == 0, k == n - 1)
                last.then_inc(job_done, 1)

            def unit_tok(u, j):
                arrived(u)
                o = bank(j)
                for t in range(2):
                    for k in range(DB):
                        at = slice(t * P, (t + 1) * P)
                        last = three(o[:, t, :], (xh[:, k, at], xl[:, k, at]), tile(u, 2 * k, 2), k == 0, k == DB - 1)
                last.then_inc(job_done, 1)

            def unit_wide(u, j, a):
                arrived(u)
                for b in range(2):
                    o = bank(j + b)
                    for m in range(2):
                        for k in range(4):
                            last = three(o[:, m, :], tile(u, (2 * b + m) * 4 + k), (a[0][:, k, :], a[1][:, k, :]), k == 0, k == 3)
                    last.then_inc(job_done, 1)

            def ups(name, i0=0, i1=None):
                n = dict((a, b) for a, b, _ in UNITS)[name]
                for i in range(i0, n if i1 is None else i1):
                    unit_up(U0[name] + i, JOB[name, i])

            def have(event, n=4):
                pe.wait_ge(split_lo, SPLIT[event] + n)

            def mean_sum(name, j, src, blocks, ready):
                o = bank(j)
                for m in range(blocks):
                    ready(m)
                    last = mm(o[:, 0, :], ones, src[:, m, :], start=m == 0, stop=m == blocks - 1)
                last.then_inc(job_done, 1)

            def square_sum(name, j, blocks=DB):
                o = bank(j)
                for c in range(blocks // 2):
                    pe.wait_ge(squared, squares_before(name) + c + 1)
                    for i in range(2):
                        last = mm(o[:, 0, :], ones, pr[c % 2][:, i, :], start=c == i == 0, stop=c == blocks // 2 - 1 and i == 1)
                    last.then_inc(job_done if c == blocks // 2 - 1 else sq_used, 1)

            def att_logits(u):
                k, j, t = UNITS_ATT[u]
                at, w = slice(t * P, (t + 1) * P), att_keys(u)
                if u:
                    pe.wait_ge(neg_ready, u)
                for m in range(att_mats(u)):
                    r, o = slice(64 * m, 64 * m + 64), att[m][:, 0:w]
                    if k == "A":
                        keys = kT if j // 2 % 2 == m else kswap
                        last = mm(o, qT[r, j, at], keys[r, j // 4, 0:w], start=True, stop=True)
                    elif k == "D":
                        last = mm(o, aqT[r, j, at], akT[r, j, 0:w], start=True, stop=True)
                    elif k == "F":
                        mm(o, fqT[r, j, at], fkT[r, j, 0:w], start=True, stop=False)
                        last = mm(o, ident[0:8, 2 * j + m:2 * j + m + 1].broadcast_to([8, P]), fc[:, 0:w], start=False, stop=True)
                    else:
                        last = mm(o, xqT[:, j, at], xkT[:, j, :], start=True, stop=True)
                last.then_inc(lg_ready, 1)

            def att_transpose(u):
                pe.wait_ge(p_ready, u + 1)
                if u:
                    pe.wait_ge(pT_sb, u)
                mats = 1 if UNITS_ATT[u][0] in "DX" else 2
                kb = att_keys(u) // P
                for m in range(mats):
                    for b in range(kb):
                        i = m * kb + b
                        last = nc.tensor.transpose(att[2][:, i * P:(i + 1) * P], pr[u % 2][:, m, b * P:(b + 1) * P], ident)
                last.then_inc(pT_psum, 1)

            def att_values(u):
                k, j, t = UNITS_ATT[u]
                pe.wait_ge(pT_sb, u + 1)
                if u:
                    pe.wait_ge(o_done, u)
                kb = att_keys(u) // P
                for m in range(1 if k in "DX" else 2):
                    for b in range(kb):
                        if k == "A":
                            v, o = v_tok[:, b, 64 * (j // 2):64 * (j // 2) + 64], att[3][64 * m:64 * m + 64, 0:P]
                        elif k == "F":
                            v, o = fv_tok[:, b, 64 * (2 * j + m):64 * (2 * j + m) + 64], att[3][64 * m:64 * m + 64, 0:P]
                        else:
                            v, o = (av_tok if k == "D" else xv_tok)[:, b, j * P:(j + 1) * P], att[3][:, 0:P]
                        last = mm(o, v, pT[u % 2][:, m * kb + b, :], start=b == 0, stop=b == kb - 1)
                last.then_inc(pv_psum, 1)

            def att_step(s, u0, n):
                if s < n:
                    att_logits(u0 + s)
                if 2 <= s < n + 2:
                    att_transpose(u0 + s - 2)
                if 3 <= s < n + 3:
                    att_values(u0 + s - 3)

            pe.wait_ge(consts_loaded, 16)
            pe.wait_ge(narrow_a_loaded, 16)
            have("x")
            ups("iq")
            o = bank(JOB["ik", 0])
            for k in range(DB):
                last = mm(o[:, 0, :], narrow_a[:, k, 0:P], h[:, k, :], start=k == 0, stop=k == DB - 1)
            last.then_inc(job_done, 1)
            o = bank(JOB["iw", 0])
            for t in range(2):
                for k in range(DB):
                    last = mm(o[:, t, 0:8], h[:, k, t * P:(t + 1) * P], narrow_a[:, k, P:P + 8], start=k == 0, stop=k == DB - 1)
            last.then_inc(job_done, 1)

            def rope(r, raw_jobs, src):
                for j in raw_jobs:
                    evacuated(pe, j)
                o = bank(JOB["rope", r])
                n = src.shape[1]
                mm(o[:, 0:n, :], const("perm"), src, start=True, stop=True).then_inc(job_done, 1)

            rope(0, [JOB["iq", 0]], iqT[:, 0:2, :])
            rope(1, [JOB["iq", 1]], iqT[:, 2:4, :])
            rope(2, [JOB["ik", 0]], ikT[:])
            ups("k")
            unit_tok(U0["v"], JOB["v", 0])
            rope(3, [JOB["k", 0]], kT[:])
            pe.wait_ge(roped, 3)
            for i in range(6):
                o = bank(JOB["idx", i])
                t, heads = (0, range(i, 8, 2)) if i < 2 else (1, [(0, 2), (4, 6), (1, 3), (5, 7)][i - 2])
                w = P * (t + 1)
                for n, hd in enumerate(heads):
                    r = slice(64 * (hd % 2), 64 * (hd % 2) + 64)
                    last = mm(o[:].rearrange("p a s -> p (a s)")[:, n * w:(n + 1) * w], iqT[r, hd // 2, t * P:(t + 1) * P], ikT[r, 0, 0:w], start=True, stop=True)
                last.then_inc(job_done, 1)
            ups("q")
            for i in range(4):
                rope(4 + i, [JOB["q", i]], qT[:, 2 * i:2 * i + 2, :])
            pe.wait_ge(roped, 8)
            pe.wait_ge(kswapped, 2)
            evacuated(pe, JOB["v", 0])
            for s in range(16 + 3):
                att_step(s, ATT0["A"], 16)
            have("ao")
            ups("ao")

            def ln_sums(name, owner):
                mean_sum(name, JOB[name + "_mean", 0], z, DB, lambda m: evacuated(pe, owner(m)))
                square_sum(name, JOB[name + "_sq", 0])

            ln_sums("ln0", lambda m: JOB["ao", m // 2])

            def mlp(layer):
                have(f"mlp{layer}")
                for half in range(2):
                    up, dn = f"up{layer}{half}", f"dn{layer}{half}"
                    with pe.Fori(0, 2) as g:
                        for i in range(RING):
                            unit_up(U0[up] + i, JOB[up, i], g)
                    pe.wait_ge(flo, 8 * (2 * layer + half + 1))
                    with pe.Fori(0, 2) as g:
                        for i in range(RING):
                            unit_down(U0[dn] + i, JOB[dn, i], (fh, fl), 16, g)
                ln_sums(f"ln{2 * layer + 1}", lambda m: JOB[f"dn{layer}1", m])

            mlp(0)

            have("gla")
            pe.wait_ge(gla_loaded, 32)
            ups("gq")
            ups("gk")
            o = bank(JOB["alow", 0])
            for k in range(DB):
                last = mm(o[0:16, 0, :], narrow_b[:, k, :], h[:, k, :], start=k == 0, stop=k == DB - 1)
            last.then_inc(job_done, 1)
            evacuated(pe, JOB["alow", 0])
            for i in range(2):
                o = bank(JOB["gate_a", i])
                for n in range(2):
                    hd = 2 * i + n
                    last = mm(o[:, n, :], w_a2[:, hd * P:(hd + 1) * P], alow[:], start=True, stop=True)
                last.then_inc(job_done, 1)
            for i in range(4):
                unit_tok(U0["gv"] + i, JOB["gv", i])

            def level(l):
                if l < 6:
                    pe.wait_ge(lvl_qk, l + 1)
                o = bank(JOB["level", l])[:].rearrange("p a (b s) -> p (a b) s", s=64)
                for hd in range(4):
                    for c in range(4):
                        at = slice(c * 64, c * 64 + 64)
                        keys, queries = (qk[:, 4 + hd, at], qk[:, hd, at]) if l < 6 else (gkT[:, hd, at], gqT[:, hd, at])
                        last = mm(o[64 * (c % 2):64 * (c % 2) + 64, hd * 2 + c // 2, :], keys, queries, start=True, stop=True)
                last.then_inc(job_done, 1)

            for i in range(4):
                unit_up(U0["gr"] + i, JOB["gr", i])
                level(i)
            for i in range(4, 7):
                level(i)
            pe.wait_ge(kd_ready, 1)
            for t in range(2):
                o = bank(JOB["kd", t])[:].rearrange("p a s -> p (a s)")
                for hd in range(4):
                    last = nc.tensor.transpose(o[:, hd * P:(hd + 1) * P], qk[:, 4 + hd, t * P:(t + 1) * P], ident)
                last.then_inc(job_done, 1)
            kd_tok = gtmp[:].rearrange("p (t a) s -> p t (a s)", t=2)
            pe.wait_ge(attn_acc, 6)
            pe.wait_ge(q_decayed, 1)
            for t in range(2):
                evacuated(pe, JOB["kd", t])
            for i in range(4):
                evacuated(pe, JOB["gv", i])
            for c in range(4):
                t, r = c // 2, slice(64 * (c % 2), 64 * (c % 2) + 64)
                if c:
                    evacuated(pe, JOB["state", 2 * c - 2])
                    evacuated(pe, JOB["state", 2 * c - 1])
                o = bank(JOB["gla_o", c])[:].rearrange("p a (b s) -> p (a b) s", s=64)
                for hd in range(4):
                    for dv in range(2):
                        at = slice(hd * S + dv * P, hd * S + dv * P + P)
                        if c:
                            mm(o[:, 2 * hd + dv, :], state[:, hd, dv * P:(dv + 1) * P], gqT[:, hd, c * 64:c * 64 + 64], start=True, stop=False)
                        last = mm(o[:, 2 * hd + dv, :], gv_tok[r, t, at], attnT[r, hd * 2 + t, :], start=c == 0, stop=True)
                last.then_inc(job_done, 1)
                if c < 3:
                    for i in range(2):
                        o = bank(JOB["state", 2 * c + i])
                        for n in range(2):
                            hd = 2 * i + n
                            last = mm(o[:, n, :], kd_tok[r, t, hd * P:(hd + 1) * P], gv_tok[r, t, hd * S:(hd + 1) * S], start=True, stop=True)
                        last.then_inc(job_done, 1)
            for i in range(2):
                o = bank(JOB["gla_sq", i])
                for n in range(2):
                    hd = 2 * i + n
                    pe.wait_ge(gla_squared, hd + 1)
                    for b in range(2):
                        last = mm(o[:, n, :], ones, z[:, 2 * hd + b, :], start=b == 0, stop=b == 1)
                last.then_inc(job_done, 1)
            have("go")
            ups("go")
            ln_sums("ln2", lambda m: JOB["go", m // 2])
            mlp(1)

            square_sum("pre_mix", JOB["pre_mix_sq", 0])
            have("mix")
            pe.wait_ge(mix_loaded, 48)
            o = bank(JOB["fg", 0])
            for k in range(DB):
                last = mm(o[0:8, 0, :], narrow_f[:, k, :], z[:, k, :], start=k == 0, stop=k == DB - 1)
            last.then_inc(job_done, 1)
            for name in ("aq", "ak"):
                ups(name)
            for i in range(2):
                unit_tok(U0["av"] + i, JOB["av", i])
            for name in ("fq", "fk"):
                ups(name)
            for i in range(2):
                unit_tok(U0["fv"] + i, JOB["fv", i])
            pe.wait_ge(fc_ready, 1)
            for i in range(2):
                for name in ("aq", "ak", "av", "fq", "fk", "fv"):
                    evacuated(pe, JOB[name, i])
            fill = [("c", i) for i in range(4)] + [("s", i) for i in range(6)]
            for s, (name, i) in enumerate(fill):
                unit_up(U0[name] + i, JOB[name, i])
                att_step(s, ATT0["D"], 16)
            unit_up(U0["gate0"], JOB["gate0", 0])
            att_step(10, ATT0["D"], 16)
            pe.wait_ge(ya_squared, 2)
            for i in range(2):
                mm(bank(JOB["ya_sq", i])[:], ones, z[:, 2 * i:2 * i + 2, :], start=True, stop=True).then_inc(job_done, 1)
            for i in range(1, 4):
                unit_up(U0["gate0"] + i, JOB["gate0", i])
                att_step(10 + i, ATT0["D"], 16)
            pe.wait_ge(b_lo, 2)
            for i in range(2):
                unit_wide(U0["br0"] + i, JOB["br0", i], (bhi, blo))
                att_step(14 + i, ATT0["D"], 16)
            for i in range(4):
                unit_up(U0["gate1"] + i, JOB["gate1", i])
                att_step(16 + i, ATT0["D"], 16)
            for n, b in enumerate((1, 3, 2)):
                if b != 1:
                    if b == 2:
                        o = bank(JOB["conv_mean", 0])
                        pe.wait_ge(conv_done, 1)
                        for m in range(4):
                            last = mm(o[:, 0, :], ones, conv[:, m, :], start=m == 0, stop=m == 3)
                        last.then_inc(job_done, 1)
                        square_sum("conv", JOB["conv_sq", 0], 4)
                    ups(f"gate{b}")
                pe.wait_ge(b_lo, 2 * n + 4)
                for i in range(2):
                    unit_wide(U0[f"br{b}"] + i, JOB[f"br{b}", i], (bhi, blo))
            have("out")
            ups("out")

            square_sum("mem", JOB["mem_sq", 0])
            square_sum("post_mix", JOB["post_mix_sq", 0])
            have("mem")
            ups("xk")
            unit_tok(U0["xv"], JOB["xv", 0])
            square_sum("pre_x", JOB["pre_x_sq", 0])
            unit_tok(U0["xv"] + 1, JOB["xv", 1])
            have("xq")
            ups("xq")
            for i in range(2):
                for name in ("xk", "xv", "xq"):
                    evacuated(pe, JOB[name, i])
            for s in range(8 + 3):
                att_step(s, ATT0["X"], 8)
            have("xo", 2)
            for i in range(2):
                unit_wide(U0["xo"] + i, JOB["xo", i], (xh, xl))
            square_sum("post_x", JOB["post_x_sq", 0])

            square_sum("pre_ffn", JOB["pre_ffn_sq", 0])
            have("ffn")
            for half in range(2):
                ups(f"fu{half}")
                pe.wait_ge(ff_lo, FH * (half + 1))
                with pe.Fori(0, 2) as g:
                    for i in range(RING):
                        unit_down(U0[f"fd{half}"] + i, JOB[f"fd{half}", i], (gh, gl), FH, g)
            square_sum("post_ffn", JOB["post_ffn_sq", 0])

        @block.scalar
        def _(act):
            f = nc.scalar.activation
            chain = Chain(act, act_step)
            eps_ln, eps_rms, one = const("ln_eps"), const("rms_eps"), const("one")

            def two(t, c):
                return t[:, 2 * c:2 * c + 2, :]

            def high_part(u, g=None, used=None):
                if u >= NU:
                    return
                tiles = [t for s, n, t in SEGMENTS if s <= u < s + n][0]
                act.wait_ge(raw_full[u % RING], per(16 * (u // RING + 1), g, 16))
                if u >= RING:
                    act.wait_ge(job_done, per(LAST[u - RING] + 1 if used is None else used, g, RING))
                f(whi[u % RING][:, 0:tiles * P], raw[u % RING][:, 0:tiles * P], ACT.Copy).then_inc(hi_ready, 1)

            def unit(name, i):
                high_part(U0[name] + i + AHEAD)
                filled(act, JOB[name, i])

            def passed(name):
                for i in range(dict((a, b) for a, b, _ in UNITS)[name]):
                    high_part(U0[name] + i + AHEAD)

            def copy(name, i, dst, scale=1.0):
                unit(name, i)
                j = JOB[name, i]
                f(dst, lin[j % RING][:], ACT.Copy, scale=scale).then_inc(evac[j % RING], 1)

            def split(event, src, ready, n=4):
                for c in range(n):
                    ready(c)
                    f(two(xh, c), two(src, c), ACT.Copy).then_inc(split_hi, 1)

            def squares(name, src, ready, n=4):
                for c in range(n):
                    ready(c)
                    if c >= 2:
                        act.wait_ge(sq_used, used_before(name) + c - 1)
                    f(pr[c % 2][:], two(src, c), ACT.Square).then_inc(squared, 1)

            def deviation(j, width, eps):
                filled(act, j)
                f(std[:], lin[j % RING][:, 0, :], ACT.Sqrt, scale=1.0 / width, bias=eps).then_inc(evac[j % RING], 1)

            def is_normed(name):
                return lambda c: act.wait_ge(normed, NORMED[name] + c + 1)

            def layer_norm(name, event):
                squares(name, z, lambda c: act.wait_ge(centered, CENTERED[name] + c + 1))
                deviation(JOB[name + "_sq", 0], D, eps_ln)
                if event:
                    split(event, h, is_normed(name))

            def att_exp(u):
                act.wait_ge(neg_ready, u + 1)
                if u >= 2:
                    act.wait_ge(pT_psum, u - 1)
                w = att_keys(u)
                for m in range(att_mats(u)):
                    last = f(pr[u % 2][:, m, 0:w], lg[:, m, 0:w], ACT.Exp, scale=-1.0, bias=nmax[:, u % 2, m:m + 1],
                             accum_out=rsum[:, u % 2, m:m + 1])
                last.then_inc(exp_done, 1)

            def att_transposed(u):
                act.wait_ge(pT_psum, u + 1)
                if u >= 2:
                    act.wait_ge(pv_psum, u - 1)
                n = (1 if UNITS_ATT[u][0] in "DX" else 2) * att_keys(u) // P
                f(pT[u % 2][:, 0:n, :], att[2][:, 0:n * P].rearrange("p (n q) -> p n q", q=P), ACT.Copy).then_inc(pT_sb, 1)

            def att_result(u):
                act.wait_ge(pv_psum, u + 1)
                f(att_out(u), att[3][:, 0:P], ACT.Copy).then_inc(o_done, 1)

            def att_step(s, u0, n):
                if s < n:
                    att_exp(u0 + s)
                if 2 <= s < n + 2:
                    att_transposed(u0 + s - 2)
                if 3 <= s < n + 3:
                    att_result(u0 + s - 3)

            act.dma_start(consts[:], const_d).then_inc(consts_loaded, 16)
            act.dma_start(posi[:], pos_d.partition_broadcast(P)).then_inc(pos_loaded, 16)
            act.dma_start(narrow_a[:], narrow_a_d).then_inc(narrow_a_loaded, 16)
            act.dma_start(vec[:], vec_d).then_inc(vec_loaded, 16)
            split("x", h, lambda c: act.wait_ge(x_loaded, 16))
            for u in range(AHEAD):
                high_part(u)
            act.wait_ge(reduced, 2)
            f(sinT[:], sinT[:], ACT.Sin).then_inc(trig, 1)
            f(cosT[:], cosT[:], ACT.Sin).then_inc(trig, 1)
            for i in range(2):
                copy("iq", i, two(iqT, i))
            j = JOB["ik", 0]
            filled(act, j)
            f(ikT[:, 0, :], lin[j % RING][:, 0, :], ACT.Copy).then_inc(evac[j % RING], 1)
            copy("k", 0, kT[:])
            copy("v", 0, v_tok[:])
            for i in range(6):
                j = JOB["idx", i]
                filled(act, j)
                if i >= 2:
                    act.wait_ge(idx_acc, i - 1)
                f(rbuf[i % 2][:], lin[j % RING][:].rearrange("p a s -> p (a s)"), ACT.Relu, scale=64 ** -0.5).then_inc(evac[j % RING], 1)
            for i in range(4):
                copy("q", i, two(qT, i))
            for s in range(16 + 3):
                att_step(s, ATT0["A"], 16)
            split("ao", qT, lambda c: act.wait_ge(o_done, 4 * c + 4))
            passed("ao")
            layer_norm("ln0", "mlp0")

            def mlp(layer):
                for half in range(2):
                    up, dn = f"up{layer}{half}", f"dn{layer}{half}"
                    base = 8 * (2 * layer + half)
                    with act.Fori(0, 2) as g:
                        for i in range(RING):
                            j = JOB[up, i]
                            high_part(U0[up] + i + AHEAD, g, j)
                            filled(act, j, g)
                            f(relu[i % 2][:], lin[j % RING][:], ACT.Relu).then_inc(evac[j % RING], 1)
                            act.wait_ge(sqr_done, per(base + i + 1, g, RING))
                            f(fh[:, bass.ds(g * 8 + 2 * i, 2), :], sqr[i % 2][:], ACT.Copy).then_inc(fhi, 1)
                    with act.Fori(0, 2) as g:
                        for i in range(RING):
                            high_part(U0[dn] + i + AHEAD, g, JOB[dn, i])
                layer_norm(f"ln{2 * layer + 1}", "gla" if layer == 0 else None)

            mlp(0)

            act.dma_start(narrow_b[:], narrow_b_d).then_inc(gla_loaded, 16)
            act.dma_start(w_a2[:], w_a2_d).then_inc(gla_loaded, 16)
            for i in range(2):
                copy("gq", i, two(gqT, i), 128 ** -0.5)
            for i in range(2):
                copy("gk", i, two(gkT, i))
            j = JOB["alow", 0]
            filled(act, j)
            f(alow[:], lin[j % RING][0:16, 0, :], ACT.Copy).then_inc(evac[j % RING], 1)
            for i in range(2):
                evacuated(act, JOB["gate_a", i])
            chain.link(f(decay[:], gtmp[:], ACT.Abs))
            chain.link(f(decay[:], decay[:], ACT.Exp, scale=-1.0))
            f(decay[:], decay[:], ACT.Ln, bias=one).then_inc(softplus, 1)
            for i in range(4):
                copy("gv", i, gv_tok[:, :, i * S:(i + 1) * S])

            def level_decay(l):
                act.wait_ge(lvl_arg, l + 1)
                chain.link(f(decay[:], gtmp[:], ACT.Abs))
                f(decay[:], decay[:], ACT.Exp, scale=-1.0 / 16).then_inc(lvl_exp, 1)

            level_decay(0)
            for i in range(4):
                unit("gr", i)
                j = JOB["gr", i]
                f(two(rgate, i), lin[j % RING][:], ACT.Tanh, scale=0.5).then_inc(gr_tanh, 1)
                level_decay(i + 1)
            level_decay(5)
            act.wait_ge(lvl_arg, 7)
            f(decay[:], bcum[:], ACT.Exp, scale=1.0 / 16).then_inc(lvl_exp, 1)
            f(gtmp[:], gtmp[:], ACT.Exp, scale=-1.0 / 16).then_inc(lvl_exp, 1)
            act.wait_ge(kd_ready, 1)
            kd_tok = gtmp[:].rearrange("p (t a) s -> p t (a s)", t=2)
            for t in range(2):
                j = JOB["kd", t]
                filled(act, j)
                f(kd_tok[:, t, :], lin[j % RING][:].rearrange("p a s -> p (a s)"), ACT.Copy).then_inc(evac[j % RING], 1)
            for c in range(4):
                j = JOB["gla_o", c]
                filled(act, j)
                f(qk[:, :, c * 64:(c + 1) * 64], lin[j % RING][:].rearrange("p a (b s) -> p (a b) s", s=64), ACT.Copy).then_inc(evac[j % RING], 1)
            for hd in range(4):
                if hd == 0:
                    evacuated(act, JOB["gla_o", 3])
                    act.wait_ge(attn_acc, 6)
                f(two(z, hd), two(qk, hd), ACT.Square).then_inc(gla_squared, 1)
            for i in range(2):
                j = JOB["gla_sq", i]
                filled(act, j)
                f(two(decay, i), lin[j % RING][:], ACT.Sqrt, scale=1.0 / S, bias=eps_rms).then_inc(evac[j % RING], 1)
            split("go", qk, lambda c: act.wait_ge(gla_y, c + 1))
            passed("go")
            layer_norm("ln2", "mlp1")
            mlp(1)

            squares("pre_mix", h, is_normed("ln3"))
            deviation(JOB["pre_mix_sq", 0], D, eps_rms)
            act.dma_start(narrow_f[:], narrow_f_d).then_inc(mix_loaded, 16)
            act.dma_start(lamv[:], lam_d.partition_broadcast(P)).then_inc(mix_loaded, 16)
            act.dma_start(bfg[:], b_fgt_d).then_inc(mix_loaded, 16)
            split("mix", z, is_normed("pre_mix"))
            evacuated(act, JOB["fg", 0])
            chain.link(f(fc[:], fgt[:], ACT.Abs))
            chain.link(f(fc[:], fc[:], ACT.Exp, scale=-1.0))
            f(fc[:], fc[:], ACT.Ln, bias=one[0:8, :]).then_inc(fg_soft, 1)
            act.wait_ge(lam_dot, 2)
            f(lamt[:, 2:4], lamt[:, 0:2], ACT.Exp).then_inc(lam_exp, 1)
            for name, dst in (("aq", aqT), ("ak", akT)):
                for i in range(2):
                    copy(name, i, two(dst, i))
            for i in range(2):
                copy("av", i, av_tok[:, :, i * S:(i + 1) * S])
            for name, dst in (("fq", fqT), ("fk", fkT)):
                for i in range(2):
                    copy(name, i, two(dst, i))
            for i in range(2):
                copy("fv", i, fv_tok[:, :, i * S:(i + 1) * S])

            def branch_split(n, src, ready):
                for c in range(2):
                    ready(c)
                    f(two(bhi, c), two(src, c), ACT.Copy).then_inc(b_hi, 1)

            def gates(b, i):
                unit(f"gate{b}", i)
                j = JOB[f"gate{b}", i]
                for m in range(2):
                    col = b * 8 + 2 * i + m
                    last = f(gate[:, 2 * i + m, :], lin[j % RING][:, m, :], ACT.Tanh, scale=0.5, bias=hvec[:, col:col + 1])
                last.then_inc(evac[j % RING], 1)

            for s in range(10):
                if s < 4:
                    unit("c", s)
                    j = JOB["c", s]
                    if s % 2 == 0:
                        if s:
                            evacuated(act, JOB["c", s - 1])
                        for m in range(2):
                            last = f(mtmp[0][:, m, :], lin[j % RING][:, m, :], ACT.Tanh, scale=0.5, bias=hvec[:, 36 + s + m:37 + s + m])
                        last.then_inc(evac[j % RING], 1)
                else:
                    i = s - 4
                    unit("s", i)
                    j = JOB["s", i]
                    if i % 3 == 0:
                        if i:
                            evacuated(act, JOB["s", i - 2])
                        f(mtmp[1][:], lin[j % RING][:], ACT.Copy).then_inc(evac[j % RING], 1)
                    elif i % 3 == 2:
                        f(two(sgate, i // 3), lin[j % RING][:], ACT.Copy).then_inc(evac[j % RING], 1)
                att_step(s, ATT0["D"], 16)
            att_step(10, ATT0["D"], 16)
            gates(0, 0)
            for i in range(2):
                j = JOB["ya_sq", i]
                filled(act, j)
                f(z[:, 4 + 2 * i:6 + 2 * i, :], lin[j % RING][:], ACT.Sqrt, scale=1.0 / P, bias=eps_rms).then_inc(evac[j % RING], 1)
            for i in range(1, 4):
                gates(0, i)
                att_step(10 + i, ATT0["D"], 16)
            branch_split(0, aqT, lambda c: act.wait_ge(b_y, c + 1))
            for i in range(2):
                high_part(U0["br0"] + i + AHEAD)
                att_step(14 + i, ATT0["D"], 16)
            for i in range(4):
                if i < 2:
                    act.wait_ge(mixed, 2 * i + 2)
                gates(1, i)
                att_step(16 + i, ATT0["D"], 16)
            branch_split(1, fqT, lambda c: act.wait_ge(o_done, 32))
            passed("br1")
            for i in range(4):
                if i < 2:
                    act.wait_ge(mixed, 4 + 2 * i + 2)
                gates(3, i)
            branch_split(2, sgate, lambda c: act.wait_ge(b_y, 2 + c + 1))
            passed("br3")
            squares("conv", conv, lambda c: act.wait_ge(centered, CENTERED["conv"] + c + 1), 2)
            deviation(JOB["conv_sq", 0], 512, eps_rms)
            for i in range(2):
                act.wait_ge(conv_normed, i + 1)
                if i == 0:
                    act.wait_ge(mixed, 12)
                f(mtmp[i][:], two(conv, i), ACT.Tanh, scale=0.5).then_inc(conv_tanh, 1)
            for i in range(4):
                gates(2, i)
            branch_split(3, conv, lambda c: act.wait_ge(b_y, 4 + c + 1))
            passed("br2")
            split("out", z, lambda c: act.wait_ge(mixed, 16))
            act.dma_start(memT[:], mem_d).then_inc(mem_loaded, 16)
            for i in range(4):
                copy("out", i, two(z, i))

            squares("mem", memT, lambda c: act.wait_ge(mem_loaded, 16))
            deviation(JOB["mem_sq", 0], D, eps_rms)
            squares("post_mix", z, lambda c: evacuated(act, JOB["out", c]))
            split("mem", memT, is_normed("mem"))
            act.wait_ge(normed, NORMED["mem"] + 4)
            deviation(JOB["post_mix_sq", 0], D, eps_rms)
            for i in range(2):
                copy("xk", i, two(xkT, i))
            copy("xv", 0, xv_tok[:, :, 0:S])
            squares("pre_x", h, is_normed("post_mix"))
            deviation(JOB["pre_x_sq", 0], D, eps_rms)
            copy("xv", 1, xv_tok[:, :, S:2 * S])
            split("xq", z, is_normed("pre_x"))
            for i in range(2):
                copy("xq", i, two(xqT, i))
            for s in range(8 + 3):
                att_step(s, ATT0["X"], 8)
            split("xo", xqT, lambda c: act.wait_ge(o_done, ATT0["X"] + 4 * c + 4), 2)
            passed("xo")
            for c in range(4):
                j = JOB["xo", 0] + c
                filled(act, j)
                f(two(z, c), lin[j % RING][:], ACT.Copy).then_inc(evac[j % RING], 1)
            squares("post_x", z, lambda c: evacuated(act, JOB["xo", 0] + c))
            deviation(JOB["post_x_sq", 0], D, eps_rms)

            squares("pre_ffn", h, is_normed("post_x"))
            deviation(JOB["pre_ffn_sq", 0], D, eps_rms)
            split("ffn", z, is_normed("pre_ffn"))
            for half in range(2):
                u0 = FH * half
                for s in range(FH + 2):
                    if s < FH:
                        u = u0 + s
                        unit(f"fu{half}", s)
                        if u >= 2:
                            act.wait_ge(ff_conv, u - 1)
                        j = JOB[f"fu{half}", s]
                        f(fpad[u % 2][:, :, 2:], lin[j % RING][:], ACT.Copy).then_inc(evac[j % RING], 1)
                    if 1 <= s < FH + 1:
                        u = u0 + s - 1
                        act.wait_ge(ff_conv, u + 1)
                        if u >= 2:
                            act.wait_ge(ff_y, u - 1)
                        f(fth[:, u % 2, :], fconv[:, u % 2, 0, :], ACT.Tanh, scale=0.5).then_inc(ff_tanh, 1)
                    if s >= 2:
                        u = u0 + s - 2
                        act.wait_ge(ff_y, u + 1)
                        f(gh[:, s - 2, :], fy[:, u % 2, :], ACT.Copy).then_inc(ff_hi, 1)
                for i in range(8):
                    high_part(U0[f"fd{half}"] + i + AHEAD)
            squares("post_ffn", z, lambda c: evacuated(act, JOB["fd1", 2 * c + 1]))
            deviation(JOB["post_ffn_sq", 0], D, eps_rms)

        @block.vector
        def _(dve):
            v = nc.vector
            chain = Chain(dve, dve_step)
            link = chain.link

            def two(t, c):
                return t[:, 2 * c:2 * c + 2, :]

            def over(row, n=2):
                return row[:, None, :].broadcast_to([P, n, S])

            def psum(j, g=None):
                filled(dve, j, g)
                return lin[j % RING]

            def read_out(ins, j):
                ins.then_inc(evac[j % RING], 1)

            def low(event, src, c):
                dve.wait_ge(split_hi, SPLIT[event] + c + 1)
                v.tensor_tensor(two(xl, c), two(src, c), two(xh, c).bitcast(f32), ALU.subtract).then_inc(split_lo, 1)

            def layer_norm(name, i, event, g_name, b_name):
                j = JOB[name + "_mean", 0]
                read_out(v.tensor_scalar(rstd[:], psum(j)[:, 0, :], -1.0 / D, None, ALU.mult), j)
                evacuated(dve, j)
                for c in range(4):
                    v.tensor_tensor(two(z, c), two(z, c), over(rstd), ALU.add).then_inc(centered, 1)
                evacuated(dve, JOB[name + "_sq", 0])
                link(v.reciprocal(rstd[:], std[:]))
                dve.wait_ge(centered, CENTERED[name] + 4)
                for c in range(4):
                    link(v.tensor_tensor(two(z, c), two(z, c), over(rstd), ALU.mult))
                    for m in (2 * c, 2 * c + 1):
                        last = v.tensor_scalar(h[:, m, :], z[:, m, :], vcol(g_name, 8 * i + m), vcol(b_name, 8 * i + m), ALU.mult, ALU.add)
                    last.then_inc(normed, 1)
                    if event and c:
                        low(event, h, c - 1)
                if event:
                    low(event, h, 3)

            def rms(name, src, dst, g_name, event=None):
                evacuated(dve, JOB[name + "_sq", 0])
                link(v.reciprocal(rstd[:], std[:]))
                for c in range(4):
                    for m in (2 * c, 2 * c + 1):
                        last = v.scalar_tensor_tensor(out=dst[:, m, :], in0=src[:, m, :], scalar=vcol(g_name, m), in1=rstd[:], op0=ALU.mult, op1=ALU.mult)
                    last.then_inc(normed, 1)
                    if event and c:
                        low(event, dst, c - 1)
                if event:
                    low(event, dst, 3)

            def rms_residual(name, g_name):
                evacuated(dve, JOB[name + "_sq", 0])
                link(v.reciprocal(rstd[:], std[:]))
                for c in range(4):
                    for m in (2 * c, 2 * c + 1):
                        link(v.scalar_tensor_tensor(out=z[:, m, :], in0=z[:, m, :], scalar=vcol(g_name, m), in1=rstd[:], op0=ALU.mult, op1=ALU.mult))
                    v.tensor_tensor(two(h, c), two(h, c), two(z, c), ALU.add).then_inc(normed, 1)

            def residual(name, n, g=None, i=0, blocks=2):
                j = JOB[name, i]
                read_out(v.scalar_tensor_tensor(out=two(z, i), in0=two(h, i), scalar=ALPHA, in1=psum(j)[:], op0=ALU.mult, op1=ALU.add), j)

            def att_neg(u):
                k, j, t = UNITS_ATT[u]
                w = att_keys(u)
                dve.wait_ge(lg_ready, u + 1)
                if u:
                    dve.wait_ge(exp_done, u)
                for m in range(att_mats(u)):
                    if k == "A":
                        mask = selbias[:, t, 0:w]
                    elif k == "X":
                        mask = const("zero").broadcast_to([P, S])
                    else:
                        mask = const("chunk" if k == "D" else "causal", P * (1 - t), S)
                    last = v.tensor_tensor_reduce(out=lg[:, m, 0:w], in0=att[m][:, 0:w], in1=mask, scale=-(128 if k == "X" else 64) ** -0.5,
                                                  scalar=3.0e38, op0=ALU.add, op1=ALU.min, accum_out=nmax[:, u % 2, m:m + 1])
                last.then_inc(neg_ready, 1)

            def att_scale(u):
                k, j, t = UNITS_ATT[u]
                n, w = att_mats(u), att_keys(u)
                dve.wait_ge(exp_done, u + 1)
                if u:
                    dve.wait_ge(p_ready, u)
                link(v.reciprocal(rinv[:, 0:n], rsum[:, u % 2, 0:n]))
                p0, p1 = pr[u % 2][:, 0, 0:w], pr[u % 2][:, 1, 0:w]
                if k == "D":
                    link(v.tensor_tensor(rinv[:, 1:2], rinv[:, 1:2], lamt[:, 4:5], ALU.mult))
                    link(v.tensor_scalar(p1, p1, rinv[:, 1:2], None, ALU.mult))
                    last = v.scalar_tensor_tensor(out=p0, in0=p0, scalar=rinv[:, 0:1], in1=p1, op0=ALU.mult, op1=ALU.subtract)
                else:
                    last = v.tensor_scalar(p0, p0, rinv[:, 0:1], None, ALU.mult)
                    if n == 2:
                        last = v.tensor_scalar(p1, p1, rinv[:, 1:2], None, ALU.mult)
                last.then_inc(p_ready, 1)

            def att_step(s, u0, n):
                if s < n:
                    att_neg(u0 + s)
                if 1 <= s < n + 1:
                    att_scale(u0 + s - 1)

            dve.wait_ge(pos_loaded, 16)
            dve.wait_ge(consts_loaded, 16)
            link(v.tensor_copy(ang[:], posi[:]))
            link(v.tensor_scalar(ang[:], ang[:], const("inv"), None, ALU.mult))
            TURN, MAGIC = 2 * np.pi, 12582912.0
            for quarter, dst in ((0.0, sinT), (0.25, cosT)):
                link(v.tensor_scalar(turns[:], ang[:], 1 / TURN, quarter, ALU.mult, ALU.add))
                link(v.tensor_scalar(turns[:], turns[:], MAGIC, None, ALU.add))
                link(v.tensor_scalar(turns[:], turns[:], MAGIC, None, ALU.subtract))
                link(v.scalar_tensor_tensor(out=dst[:], in0=turns[:], scalar=-6.28125, in1=ang[:], op0=ALU.mult, op1=ALU.add))
                link(v.scalar_tensor_tensor(out=dst[:], in0=turns[:], scalar=-(TURN - 6.28125), in1=dst[:], op0=ALU.mult, op1=ALU.add))
                link(v.tensor_scalar(dst[:], dst[:], quarter * TURN, 3.1415925, ALU.add, ALU.min))
                v.tensor_scalar(dst[:], dst[:], -3.1415925, None, ALU.max).then_inc(reduced, 1)
            for c in range(4):
                low("x", h, c)
            dve.wait_ge(vec_loaded, 16)
            link(v.tensor_scalar(hvec[:, 0:32], vec[:, COL["b_gate_2"]:COL["b_gate_2"] + 32], 0.5, None, ALU.mult))
            link(v.tensor_scalar(hvec[:, 32:40], vec[:, COL["b_glu_2"]:COL["b_glu_2"] + 8], 0.5, None, ALU.mult))
            link(v.tensor_scalar(hvec[:, 40:41], vcol("diff_norm_2"), 0.8, None, ALU.mult))
            dve.wait_ge(trig, 2)
            link(v.tensor_scalar(cosT[:], cosT[:], const("rot"), const("norot"), ALU.mult, ALU.add))

            def rope(r, dst):
                j = JOB["rope", r]
                n = dst.shape[1]
                p = psum(j)
                read_out(v.tensor_tensor(rtmp[:, 0:n, :], p[:, 0:n, :], over(sinT, n), ALU.mult), j)
                link(v.tensor_tensor(dst, dst, over(cosT, n), ALU.mult))
                evacuated(dve, j)
                v.tensor_tensor(dst, dst, rtmp[:, 0:n, :], ALU.add).then_inc(roped, 1)
                dve.wait_ge(roped, r + 1)

            j = JOB["iw", 0]
            read_out(v.tensor_scalar(iw[:], psum(j)[:, :, 0:8], 8 ** -0.5, None, ALU.mult), j)
            rope(0, two(iqT, 0))
            rope(1, two(iqT, 1))
            rope(2, ikT[:])
            rope(3, kT[:])
            v.tensor_copy(kswap[0:64, :, :], kT[64:128, :, :]).then_inc(kswapped, 1)
            v.tensor_copy(kswap[64:128, :, :], kT[0:64, :, :]).then_inc(kswapped, 1)
            for i in range(6):
                evacuated(dve, JOB["idx", i])
                t, heads = (0, range(i, 8, 2)) if i < 2 else (1, [(0, 2), (4, 6), (1, 3), (5, 7)][i - 2])
                w = P * (t + 1)
                for n, hd in enumerate(heads):
                    first = i in (0, 2) and n == 0
                    ins = v.scalar_tensor_tensor(out=work[:, t, 0:w], in0=rbuf[i % 2][:, n * w:(n + 1) * w], scalar=iw[:, t, hd:hd + 1],
                                                 in1=const("causal", P * (1 - t), S) if first else work[:, t, 0:w], op0=ALU.mult, op1=ALU.add)
                    if n < len(heads) - 1:
                        link(ins)
                ins.then_inc(idx_acc, 1)
                dve.wait_ge(idx_acc, i + 1)
            for t in range(2):
                w = P * (t + 1)
                for _ in range(TOPK // 8):
                    link(v.max(top8[:], work[:, t, 0:w]))
                    link(v.match_replace(work[:, t, 0:w], top8[:], work[:, t, 0:w], TAKEN))
                link(v.tensor_scalar(selbias[:, t, 0:w], work[:, t, 0:w], TAKEN, NEG, ALU.not_equal, ALU.mult))
                link(v.tensor_tensor(selbias[:, t, 0:w], selbias[:, t, 0:w], const("causal", P * (1 - t), S), ALU.add))
            for i in range(4):
                rope(4 + i, two(qT, i))
            for s in range(16 + 1):
                att_step(s, ATT0["A"], 16)
            for c in range(4):
                low("ao", qT, c)
            for i in range(4):
                residual("ao", 4, i=i)
            layer_norm("ln0", 0, "mlp0", "ln_mix_g", "ln_mix_b")

            def mlp(layer):
                for half in range(2):
                    up, dn = f"up{layer}{half}", f"dn{layer}{half}"
                    base = 8 * (2 * layer + half)
                    with dve.Fori(0, 2) as g:
                        for i in range(RING):
                            evacuated(dve, JOB[up, i], g)
                            v.tensor_tensor(sqr[i % 2][:], relu[i % 2][:], relu[i % 2][:], ALU.mult).then_inc(sqr_done, 1)
                            dve.wait_ge(fhi, per(base + i + 1, g, RING))
                            at = bass.ds(g * 8 + 2 * i, 2)
                            v.tensor_tensor(fl[:, at, :], sqr[i % 2][:], fh[:, at, :].bitcast(f32), ALU.subtract).then_inc(flo, 1)
                    with dve.Fori(0, 2) as g:
                        for i in range(RING):
                            j = JOB[dn, i]
                            p = psum(j, g)
                            m = bass.ds(g * 4 + i, 1)
                            if half == 0:
                                ins = v.scalar_tensor_tensor(out=z[:, m, :], in0=h[:, m, :], scalar=ALPHA, in1=p[:, 0:1, :], op0=ALU.mult, op1=ALU.add)
                            else:
                                ins = v.tensor_tensor(z[:, m, :], z[:, m, :], p[:, 0:1, :], ALU.add)
                            read_out(ins, j)
                layer_norm(f"ln{2 * layer + 1}", layer, "gla" if layer == 0 else None, "ln_mlp_g", "ln_mlp_b")

            mlp(0)

            for i in range(2):
                j = JOB["gate_a", i]
                p = psum(j)
                for n in range(2):
                    ins = v.tensor_scalar(gtmp[:, 2 * i + n, :], p[:, n, :], vcol("b_b_a", 2 * i + n), None, ALU.add)
                read_out(ins, j)
            evacuated(dve, JOB["gate_a", 0])
            evacuated(dve, JOB["gate_a", 1])
            dve.wait_ge(softplus, 1)
            link(v.tensor_scalar(gtmp[:], gtmp[:], 0.0, None, ALU.min))
            link(v.tensor_tensor(gtmp[:], gtmp[:], decay[:], ALU.subtract))
            for hd in range(4):
                ins = v.tensor_tensor_scan(out=bcum[:, hd, :], data0=const("scan"), data1=gtmp[:, hd, :], initial=0.0, op0=ALU.mult, op1=ALU.add)
                link(ins)
            flat_b = bcum[:].rearrange("p a s -> p (a s)")
            flat_t = gtmp[:].rearrange("p a s -> p (a s)")
            masked = z[:, 0:2, :].rearrange("p a (b s) -> p (a b) s", s=64)

            def level_args(l):
                half = 32 >> l
                if l:
                    dve.wait_ge(lvl_exp, l)
                b = flat_b.rearrange("p (n w) -> p n w", w=2 * half)
                v.tensor_tensor(flat_t.rearrange("p (n w) -> p n w", w=2 * half), b,
                                b[:, :, half - 1:half].broadcast_to([P, 4 * S // (2 * half), 2 * half]), ALU.subtract).then_inc(lvl_arg, 1)

            def level_pairs(l):
                dve.wait_ge(lvl_exp, l + 1)
                if l:
                    filled(dve, JOB["level", l - 1])
                v.tensor_tensor(qk[:, 0:4, :], gqT[:], decay[:], ALU.mult)
                v.tensor_tensor(qk[:, 4:8, :], gkT[:], decay[:], ALU.mult).then_inc(lvl_qk, 1)

            def level_sum(l):
                j = JOB["level", l]
                p = psum(j)[:].rearrange("p a (b s) -> p (a b) s", s=64)
                mask = const("level", 64 * l, 64 * l + 64)[:, None, :].broadcast_to([P, 8, 64])
                if l == 0:
                    read_out(v.tensor_tensor(attnT[:], p, mask, ALU.mult), j)
                    evacuated(dve, j)
                    return
                read_out(v.tensor_tensor(masked, p, mask, ALU.mult), j)
                evacuated(dve, j)
                v.tensor_tensor(attnT[:], attnT[:], masked, ALU.add).then_inc(attn_acc, 1)
                dve.wait_ge(attn_acc, l)

            level_args(0)
            for i in range(2):
                evacuated(dve, JOB["gq", i])
                evacuated(dve, JOB["gk", i])
            for l in range(6):
                level_pairs(l)
                if l < 5:
                    level_args(l + 1)
                if l < 4:
                    j = JOB["gr", l]
                    dve.wait_ge(gr_tanh, l + 1)
                    read_out(v.scalar_tensor_tensor(out=two(rgate, l), in0=two(rgate, l), scalar=1.0, in1=lin[j % RING][:], op0=ALU.add, op1=ALU.mult), j)
                if l:
                    level_sum(l - 1)
            level_sum(5)
            b = flat_b.rearrange("p (n w) -> p n w", w=64)
            v.tensor_tensor(flat_t.rearrange("p (n w) -> p n w", w=64), b, b[:, :, 63:64].broadcast_to([P, 16, 64]), ALU.subtract).then_inc(lvl_arg, 1)
            level_sum(6)
            dve.wait_ge(lvl_exp, 8)
            v.tensor_tensor(qk[:, 4:8, :], gkT[:], gtmp[:], ALU.mult).then_inc(kd_ready, 1)
            v.tensor_tensor(gqT[:], gqT[:], decay[:], ALU.mult).then_inc(q_decayed, 1)
            for c in range(3):
                for i in range(2):
                    j = JOB["state", 2 * c + i]
                    p = psum(j)
                    if c == 0:
                        read_out(v.tensor_copy(two(state, i), p[:]), j)
                        continue
                    evacuated(dve, JOB["state", 2 * c - 2 + i])
                    for n in range(2):
                        hd = 2 * i + n
                        ins = v.scalar_tensor_tensor(out=state[:, hd, :], in0=state[:, hd, :], scalar=decay[:, hd, c * 64 + 63:c * 64 + 64],
                                                     in1=p[:, n, :], op0=ALU.mult, op1=ALU.add)
                    read_out(ins, j)
            for i in range(2):
                evacuated(dve, JOB["gla_sq", i])
                link(v.reciprocal(two(decay, i), two(decay, i)))
                for hd in (2 * i, 2 * i + 1):
                    for dv in range(2):
                        m = 2 * hd + dv
                        link(v.scalar_tensor_tensor(out=qk[:, m, :], in0=qk[:, m, :], scalar=vcol("b_g_norm", dv), in1=decay[:, hd, :], op0=ALU.mult, op1=ALU.mult))
                    v.scalar_tensor_tensor(out=two(qk, hd), in0=two(rgate, hd), scalar=0.5, in1=two(qk, hd), op0=ALU.mult, op1=ALU.mult).then_inc(gla_y, 1)
            for c in range(4):
                low("go", qk, c)
            for i in range(4):
                residual("go", 4, i=i)
            layer_norm("ln2", 1, "mlp1", "ln_mix_g", "ln_mix_b")
            mlp(1)

            rms("pre_mix", h, z, "norm_mix_pre_2", "mix")
            dve.wait_ge(mix_loaded, 48)
            for i in range(2):
                v.tensor_tensor_reduce(out=pr[0][:, i, 0:64], in0=lamv[:, 2 * i, :], in1=lamv[:, 2 * i + 1, :], scale=1.0, scalar=0.0,
                                       op0=ALU.mult, op1=ALU.add, accum_out=lamt[:, i:i + 1]).then_inc(lam_dot, 1)
            link(v.memset(upad[:, :, 0:CPAD], 0.0))
            link(v.memset(scpad[:, :, 0:2], 0.0))
            j = JOB["fg", 0]
            read_out(v.tensor_scalar(fgt[:], psum(j)[0:8, 0, :], bfg[:], None, ALU.add), j)
            dve.wait_ge(fg_soft, 1)
            link(v.tensor_scalar(fgt[:], fgt[:], 0.0, None, ALU.min))
            link(v.tensor_tensor(fgt[:], fgt[:], fc[:], ALU.subtract))
            link(v.tensor_tensor_scan(out=fc[:], data0=const("ones")[0:8, :], data1=fgt[:], initial=0.0, op0=ALU.mult, op1=ALU.add))
            v.tensor_scalar(fc[:], fc[:], -8.0, None, ALU.mult).then_inc(fc_ready, 1)
            dve.wait_ge(lam_exp, 1)
            link(v.tensor_tensor(lamt[:, 4:5], lamt[:, 2:3], lamt[:, 3:4], ALU.subtract))
            link(v.tensor_scalar(lamt[:, 4:5], lamt[:, 4:5], 0.8 - 0.6, None, ALU.add))

            def conv_taps(n0, n1):
                for n in range(n0, min(n1, 4 * CONV_K)):
                    k, b = n // 4, n % 4
                    x, w = upad[:, b, k:k + S], vcol("conv_dw_2", 4 * k + b)
                    if k == 0:
                        ins = v.tensor_scalar(conv[:, b, :], x, w, vcol("conv_dw_b_2", b), ALU.mult, ALU.add)
                    else:
                        ins = v.scalar_tensor_tensor(out=conv[:, b, :], in0=x, scalar=w, in1=conv[:, b, :], op0=ALU.mult, op1=ALU.add)
                    if n == 4 * CONV_K - 1:
                        ins.then_inc(conv_done, 1)
                    else:
                        link(ins)

            def short_conv(i):
                evacuated(dve, JOB["s", 3 * i + 2])
                evacuated(dve, JOB["s", 3 * i + 1])
                for m in range(2):
                    b = 2 * i + m
                    acc = mtmp[1][:, m, :]
                    link(v.tensor_scalar(acc, scpad[:, m, 0:S], vcol("sc_w_2", b), None, ALU.mult))
                    for k in (1, 2):
                        link(v.scalar_tensor_tensor(out=acc, in0=scpad[:, m, k:k + S], scalar=vcol("sc_w_2", 4 * k + b), in1=acc, op0=ALU.mult, op1=ALU.add))
                v.tensor_tensor(two(sgate, i), two(sgate, i), mtmp[1][:], ALU.mult).then_inc(b_y, 1)

            def branch_low(n, src):
                for c in range(2):
                    dve.wait_ge(b_hi, 2 * n + c + 1)
                    v.tensor_tensor(two(blo, c), two(src, c), two(bhi, c).bitcast(f32), ALU.subtract).then_inc(b_lo, 1)

            def branch_sum(n, b, i):
                for c in (2 * i, 2 * i + 1):
                    j = JOB[f"br{b}", 0] + c
                    t = mtmp[c % 2]
                    read_out(v.scalar_tensor_tensor(out=t[:], in0=two(gate, c), scalar=1.0, in1=psum(j)[:], op0=ALU.add, op1=ALU.mult), j)
                    evacuated(dve, j)
                    if n == 0:
                        ins = v.tensor_scalar(two(z, c), t[:], 0.5, None, ALU.mult)
                    else:
                        ins = v.scalar_tensor_tensor(out=two(z, c), in0=t[:], scalar=0.5, in1=two(z, c), op0=ALU.mult, op1=ALU.add)
                    ins.then_inc(mixed, 1)
                    dve.wait_ge(mixed, 4 * n + c + 1)

            TAPS = 8
            for s in range(10):
                if s < 4 and s % 2:
                    j = JOB["c", s]
                    evacuated(dve, JOB["c", s - 1])
                    link(v.tensor_scalar(mtmp[0][:], mtmp[0][:], 0.5, 0.5, ALU.mult, ALU.add))
                    p = psum(j)
                    for m in range(2):
                        b = s - 1 + m
                        ins = v.scalar_tensor_tensor(out=upad[:, b, CPAD:], in0=p[:, m, :], scalar=vcol("b_glu_2", b), in1=mtmp[0][:, m, :], op0=ALU.add, op1=ALU.mult)
                    read_out(ins, j)
                elif s >= 4 and (s - 4) % 3 == 1:
                    i = s - 4
                    j = JOB["s", i]
                    evacuated(dve, JOB["s", i - 1])
                    read_out(v.tensor_tensor(scpad[:, :, 2:], mtmp[1][:], psum(j)[:], ALU.mult), j)
                elif s >= 4 and (s - 4) % 3 == 2:
                    short_conv((s - 4) // 3)
                att_step(s, ATT0["D"], 16)
                if s == 4:
                    evacuated(dve, JOB["c", 1])
                    evacuated(dve, JOB["c", 3])
                if s >= 4:
                    conv_taps(TAPS * (s - 4), TAPS * (s - 3))
            att_step(10, ATT0["D"], 16)
            dve.wait_ge(o_done, 24)
            for i in range(2):
                v.tensor_tensor(two(z, i), two(aqT, i), two(aqT, i), ALU.mult).then_inc(ya_squared, 1)
            for i in range(1, 4):
                att_step(10 + i, ATT0["D"], 16)
                conv_taps(TAPS * (5 + i), TAPS * (6 + i))
                if i == 1:
                    for c in range(2):
                        evacuated(dve, JOB["ya_sq", c])
                        link(v.reciprocal(z[:, 4 + 2 * c:6 + 2 * c, :], z[:, 4 + 2 * c:6 + 2 * c, :]))
                        for hd in (2 * c, 2 * c + 1):
                            ins = v.scalar_tensor_tensor(out=aqT[:, hd, :], in0=aqT[:, hd, :], scalar=hvec[:, 40:41], in1=z[:, 4 + hd, :], op0=ALU.mult, op1=ALU.mult)
                        ins.then_inc(b_y, 1)
            branch_low(0, aqT)
            for i in range(2):
                att_step(14 + i, ATT0["D"], 16)
                branch_sum(0, 0, i)
            for i in range(4):
                att_step(16 + i, ATT0["D"], 16)
                conv_taps(TAPS * (9 + i), TAPS * (10 + i))
            branch_low(1, fqT)
            for i in range(2):
                branch_sum(1, 1, i)
            branch_low(2, sgate)
            conv_taps(TAPS * 13, 4 * CONV_K)
            for i in range(2):
                branch_sum(2, 3, i)
            j = JOB["conv_mean", 0]
            read_out(v.tensor_scalar(rstd[:], psum(j)[:, 0, :], -1.0 / 512, None, ALU.mult), j)
            evacuated(dve, j)
            for c in range(2):
                v.tensor_tensor(two(conv, c), two(conv, c), over(rstd), ALU.add).then_inc(centered, 1)
            evacuated(dve, JOB["conv_sq", 0])
            link(v.reciprocal(rstd[:], std[:]))
            dve.wait_ge(centered, CENTERED["conv"] + 2)
            for c in range(2):
                link(v.tensor_tensor(two(conv, c), two(conv, c), over(rstd), ALU.mult))
                for b in (2 * c, 2 * c + 1):
                    ins = v.tensor_scalar(conv[:, b, :], conv[:, b, :], vcol("conv_ln_g_2", b), vcol("conv_ln_b_2", b), ALU.mult, ALU.add)
                ins.then_inc(conv_normed, 1)
            for c in range(2):
                dve.wait_ge(conv_tanh, c + 1)
                link(v.tensor_scalar(mtmp[c][:], mtmp[c][:], 0.5, 0.5, ALU.mult, ALU.add))
                v.tensor_tensor(two(conv, c), two(conv, c), mtmp[c][:], ALU.mult).then_inc(b_y, 1)
            branch_low(3, conv)
            for i in range(2):
                branch_sum(3, 2, i)
            for c in range(4):
                low("out", z, c)

            rms("mem", memT, memT, "norm_mem_2", "mem")
            rms_residual("post_mix", "norm_mix_post_2")
            rms("pre_x", h, z, "norm_x_pre_2", "xq")
            for s in range(8 + 1):
                att_step(s, ATT0["X"], 8)
            for c in range(2):
                low("xo", xqT, c)
            rms_residual("post_x", "norm_x_post_2")

            for i in range(2):
                link(v.memset(fpad[i][:, :, 0:2], 0.0))
            rms("pre_ffn", h, z, "norm_ffn_pre_2", "ffn")
            for half in range(2):
                u0 = FH * half
                for s in range(FH + 2):
                    if s < FH:
                        u = u0 + s
                        evacuated(dve, JOB[f"fu{half}", s])
                        for m in range(2):
                            x, acc, b = fpad[u % 2][:, m, :], fconv[:, u % 2, m, :], FB * m + u
                            link(v.tensor_scalar(acc, x[:, 0:S], vcol("ffn_dw_2", b), vcol("ffn_dw_b_2", b), ALU.mult, ALU.add))
                            link(v.scalar_tensor_tensor(out=acc, in0=x[:, 1:1 + S], scalar=vcol("ffn_dw_2", 2 * FB + b), in1=acc, op0=ALU.mult, op1=ALU.add))
                            ins = v.scalar_tensor_tensor(out=acc, in0=x[:, 2:2 + S], scalar=vcol("ffn_dw_2", 4 * FB + b), in1=acc, op0=ALU.mult, op1=ALU.add)
                            if m == 0:
                                link(ins)
                        ins.then_inc(ff_conv, 1)
                    if 1 <= s < FH + 1:
                        u = u0 + s - 1
                        dve.wait_ge(ff_tanh, u + 1)
                        if u >= 2:
                            dve.wait_ge(ff_lo, u - 1)
                        link(v.scalar_tensor_tensor(out=fy[:, u % 2, :], in0=fth[:, u % 2, :], scalar=1.0, in1=fconv[:, u % 2, 0, :], op0=ALU.add, op1=ALU.mult))
                        v.scalar_tensor_tensor(out=fy[:, u % 2, :], in0=fy[:, u % 2, :], scalar=0.5, in1=fconv[:, u % 2, 1, :], op0=ALU.mult, op1=ALU.mult).then_inc(ff_y, 1)
                    if s >= 2:
                        u = u0 + s - 2
                        dve.wait_ge(ff_hi, u + 1)
                        v.tensor_tensor(gl[:, s - 2, :], fy[:, u % 2, :], gh[:, s - 2, :].bitcast(f32), ALU.subtract).then_inc(ff_lo, 1)
                for i in range(8):
                    j = JOB[f"fd{half}", i]
                    p = psum(j)
                    if half == 0:
                        read_out(v.tensor_copy(z[:, i, :], p[:, 0, :]), j)
                    else:
                        read_out(v.tensor_tensor(z[:, i, :], z[:, i, :], p[:, 0, :], ALU.add), j)
            rms_residual("post_ffn", "norm_ffn_post_2")


def tiles_up(w, blocks):
    out = []
    for pair in blocks:
        cols = np.concatenate([np.arange(c, c + P) for c in pair])
        kb = w.shape[0] // P
        out.append(w[:, cols].reshape(kb, P, len(pair), P).transpose(1, 2, 0, 3).reshape(P, -1))
    return out


def pairs(start, n, step=P):
    return [(start + 2 * i * step, start + (2 * i + 1) * step) for i in range(n // 2)]


def tiles_tok(w, start, n):
    return [w[:, start + i * S:start + (i + 1) * S].reshape(DB, P, S).transpose(1, 0, 2).reshape(P, -1) for i in range(n)]


def tiles_wide(w):
    return tiles_up(w, [tuple(range(i * 512, i * 512 + 512, P)) for i in range(2)])


def tiles_down(w):
    return tiles_up(w, [(i * P,) for i in range(8)])


def weight_units(i):
    a, b, w2, br = i["a_w_in"][0], i["b_w_in"][0], i["w_in_2"][0], i["w_branch_2"][0]
    wg, up, dn = i["w_gate_2"][0], i["w_up_2"][0], i["w_down_2"][0]
    g = {"iq": tiles_up(a, pairs(1536, 4)), "k": tiles_up(a, pairs(1024, 2)), "v": tiles_tok(a, 1280, 1),
         "q": tiles_up(a, pairs(0, 8)), "ao": tiles_up(i["a_w_o"][0], pairs(0, 8)),
         "gq": tiles_up(b, pairs(0, 4)), "gk": tiles_up(b, pairs(512, 4)), "gv": tiles_tok(b, 1024, 4),
         "gr": tiles_up(b, pairs(2048, 8)), "go": tiles_up(i["b_w_o"][0], pairs(0, 8)),
         "aq": tiles_up(w2, pairs(0, 4)), "ak": tiles_up(w2, pairs(512, 4)), "av": tiles_tok(w2, 1024, 2),
         "fq": tiles_up(w2, pairs(1536, 4)), "fk": tiles_up(w2, pairs(2048, 4)), "fv": tiles_tok(w2, 2560, 2)}
    c0 = 3080
    g["c"] = tiles_up(w2, [p for n in range(2) for p in (pairs(c0 + 512 + 256 * n, 2) + pairs(c0 + 256 * n, 2))])
    s0 = c0 + 1024
    g["s"] = tiles_up(w2, [p for n in range(2) for at in (1024, 0, 512) for p in pairs(s0 + at + 256 * n, 2)])
    for layer in range(2):
        for half in range(2):
            g[f"up{layer}{half}"] = tiles_up(i["mlp_w_up"][layer], pairs(2048 * half, 16))
            g[f"dn{layer}{half}"] = tiles_down(i["mlp_w_down"][layer][2048 * half:2048 * half + 2048])
    for n in range(4):
        g[f"gate{n}"] = tiles_up(wg, pairs(D * n, 8))
        g[f"br{n}"] = tiles_wide(br[n])
    g["out"] = tiles_up(i["w_out_2"][0], pairs(0, 8))
    g["xq"] = tiles_up(i["w_xq_2"][0], pairs(0, 4))
    g["xk"] = tiles_up(i["w_xkv_2"][0], pairs(0, 4))
    g["xv"] = tiles_tok(i["w_xkv_2"][0], 512, 2)
    g["xo"] = tiles_wide(i["w_xo_2"][0])
    for half in range(2):
        g[f"fu{half}"] = tiles_up(up, [(P * b, P * (FB + b)) for b in range(FH * half, FH * half + FH)])
        g[f"fd{half}"] = tiles_down(dn[FH * P * half:FH * P * (half + 1)])
    out = np.zeros((NU, P, UW), np.float32)
    for name, n, tiles in UNITS:
        assert len(g[name]) == n, name
        for k, unit in enumerate(g[name]):
            assert unit.shape[1] == tiles * P, name
            out[U0[name] + k, :, 0:tiles * P] = unit
    return out


def by_partition(w):
    return np.ascontiguousarray(w.reshape(-1, P, w.shape[1]).transpose(1, 0, 2))


def kernel(**inputs):
    import concourse.bacc as bacc
    from concourse.bass_utils import run_bass_kernel_spmd

    i = {k: np.asarray(v) for k, v in inputs.items()}
    a, b, w2 = i["a_w_in"][0], i["b_w_in"][0], i["w_in_2"][0]
    ik = a[:, 2048:2112]
    arrays = {
        "units": weight_units(i),
        "x": by_partition(np.ascontiguousarray(i["x"][0].T)),
        "mem": by_partition(np.ascontiguousarray(i["mem_2"][0].T)),
        "pos": np.ascontiguousarray(i["positions"][0]),
        "vectors": np.ascontiguousarray(np.concatenate([i[n].reshape(-1, P) for n, _ in VECTORS]).T),
        "consts": shape_constants(),
        "narrow_a": by_partition(np.concatenate([ik, ik, a[:, 2112:2120]], 1)),
        "narrow_b": by_partition(b[:, 3072:3088]),
        "narrow_f": by_partition(w2[:, 3072:3080]),
        "w_a2": np.ascontiguousarray(i["b_w_a2"][0]),
        "b_fgt": np.ascontiguousarray(i["b_fgt_2"][0][:, None]),
        "lam": np.ascontiguousarray(np.stack([i[n + "_2"][0] for n in ("lam_q1", "lam_k1", "lam_q2", "lam_k2")])),
    }
    nc = bacc.Bacc("TRN2", target_bir_lowering=False, num_devices=1)
    args = [nc.dram_tensor(n + "_dram", v.shape, mybir.dt.from_np(v.dtype), kind="ExternalInput").ap() for n, v in arrays.items()]
    out = nc.dram_tensor("out_dram", (P, DB, S), mybir.dt.float32, kind="ExternalOutput").ap()
    build(nc, *args, out)
    r = run_bass_kernel_spmd(nc, [{n + "_dram": v for n, v in arrays.items()}], core_ids=[0])
    y = r.results[0]["out_dram"]
    return np.ascontiguousarray(y.transpose(2, 1, 0).reshape(1, S, D))
```

```python
import numpy as np
import concourse.bass as bass
from concourse import mybir
from concourse.alu_op_type import AluOpType as ALU
from contextlib import ExitStack

P = 128
S = 256
D = 1024
DB = D // P
RING = 4
UT = 16
UW = UT * P
AHEAD = 3
NEG = -1.0e30
TAKEN = -3.0e38
TOPK = min(256, S // 4)
ALPHA = 4 ** 0.25
CONV_K = 31
CPAD = CONV_K - 1
FB = 22

VECTORS = [("ln_mix_g", 16), ("ln_mix_b", 16), ("ln_mlp_g", 16), ("ln_mlp_b", 16), ("b_b_a", 4), ("b_g_norm", 2),
           ("norm_mix_pre_2", 8), ("norm_mix_post_2", 8), ("norm_x_pre_2", 8), ("norm_x_post_2", 8),
           ("norm_mem_2", 8), ("norm_ffn_pre_2", 8), ("norm_ffn_post_2", 8), ("diff_norm_2", 1), ("b_glu_2", 8),
           ("conv_dw_b_2", 4), ("conv_ln_g_2", 4), ("conv_ln_b_2", 4), ("b_gate_2", 32), ("ffn_dw_b_2", 44),
           ("conv_dw_2", 4 * CONV_K), ("sc_w_2", 12), ("ffn_dw_2", 3 * 44)]
COL = {}
for _name, _n in VECTORS:
    COL[_name] = sum(n for m, n in VECTORS[:len(COL)])
NV = sum(n for _, n in VECTORS)

UNITS = [("iq", 2), ("k", 1), ("v", 1), ("q", 4), ("ao", 4),
         ("up00", 8), ("dn00", 8), ("up01", 8), ("dn01", 8),
         ("gq", 2), ("gk", 2), ("gv", 4), ("gr", 4), ("go", 4),
         ("up10", 8), ("dn10", 8), ("up11", 8), ("dn11", 8),
         ("aq", 2), ("ak", 2), ("av", 2), ("fq", 2), ("fk", 2), ("fv", 2),
         ("c", 4), ("s", 6), ("gate0", 4), ("br0", 2), ("gate3", 4), ("br3", 2),
         ("gate1", 4), ("br1", 2), ("gate2", 4), ("br2", 2), ("out", 4),
         ("xk", 2), ("xv", 2), ("xq", 2), ("xo", 2),
         ("fu", FB), ("fd", DB * FB // UT)]
COUNT = dict(UNITS)
U0 = {}
NU = 0
for _name, _n in UNITS:
    U0[_name] = NU
    NU += _n


GLA_FILL = {0: ("gv", 2), 1: ("gv", 3), 2: ("gr", 0), 3: ("gr", 1), 5: ("gr", 2)}


def plan():
    job, last, n = {}, {}, [0]

    def add(name, i=0, unit=None, banks=1):
        job[name, i] = n[0]
        n[0] += banks
        if unit:
            last[U0[unit] + i] = n[0] - 1

    def units(name, count, banks=1):
        for i in range(count):
            add(name, i, name, banks)

    def norm(name, mean=False):
        if mean:
            add(name + "_mean")
        add(name + "_sq"); add(name + "_rstd")

    units("iq", 2); add("ik"); add("iw"); add("rope", 0); add("rope", 1); add("rope", 2)
    units("k", 1); units("v", 1); add("rope", 3)
    for i in range(6):
        add("idx", i)
    units("q", 4)
    for i in range(4):
        add("rope", 4 + i)
    units("ao", 4); norm("ln0", True)
    for layer in range(2):
        for half in range(2):
            units(f"up{layer}{half}", 8); units(f"dn{layer}{half}", 8)
        norm(f"ln{2 * layer + 1}", True)
        if layer == 0:
            units("gq", 2); units("gk", 2); add("alow"); add("gate_a", 0); add("gate_a", 1)
            add("gv", 0, "gv"); add("gv", 1, "gv")
            for l in range(7):
                if l in GLA_FILL:
                    add(*GLA_FILL[l], GLA_FILL[l][0])
                add("level", l)
            add("kd", 0); add("kd", 1)
            for c in range(4):
                add("gla_o", c)
                if c < 3:
                    add("state", 2 * c); add("state", 2 * c + 1)
                if c == 0:
                    add("gr", 3, "gr")
            add("gla_sq"); add("gla_rstd", 0); add("gla_rstd", 1)
            units("go", 4); norm("ln2", True)
    norm("pre_mix")
    add("fg")
    for name in ("aq", "ak", "av", "fq", "fk", "fv", "c", "s"):
        units(name, COUNT[name])
    add("gate0", 0, "gate0"); add("ya_sq"); add("gate0", 1, "gate0"); add("ya_rstd", 0); add("ya_rstd", 1)
    add("gate0", 2, "gate0"); add("gate0", 3, "gate0"); units("br0", 2, 2); units("gate3", 4); units("br3", 2, 2)
    add("gate1", 0, "gate1"); add("gate1", 1, "gate1"); add("conv_mean"); add("gate1", 2, "gate1"); add("conv_sq")
    add("gate1", 3, "gate1"); add("conv_rstd"); units("br1", 2, 2); units("gate2", 4); units("br2", 2, 2)
    units("out", 4); norm("mem"); add("post_mix_sq"); add("xk", 0, "xk"); add("post_mix_rstd"); add("xk", 1, "xk")
    add("xv", 0, "xv"); add("pre_x_sq"); add("xv", 1, "xv"); add("pre_x_rstd"); units("xq", 2); units("xo", 2, 2)
    norm("post_x"); norm("pre_ffn")
    units("fu", FB)
    for i in range(DB):
        add("fd", i)
    for u in range(COUNT["fd"]):
        last[U0["fd"] + u] = job["fd", (UT * u + UT - 1) // FB]
    norm("post_ffn")
    return job, last


JOB, LAST = plan()

CONSTS = [("ident", P), ("ones", S), ("causal", S), ("chunk", S), ("perm", P), ("level", 7 * 64), ("scan", S),
          ("inv", 1), ("rot", 1), ("norot", 1), ("ln_eps", 1), ("rms_eps", 1), ("one", 1), ("zero", 1)]
CC = {}
for _name, _n in CONSTS:
    CC[_name] = sum(n for m, n in CONSTS[:len(CC)])
NC = sum(n for _, n in CONSTS)


def shape_constants():
    c = np.zeros((P, NC), np.float32)

    def put(name, a):
        c[:, CC[name]:CC[name] + a.shape[1]] = a

    i = np.arange(P)
    put("ident", np.eye(P))
    put("ones", np.ones((P, S)))
    put("causal", np.concatenate([np.zeros((P, P)), np.where(i[None] <= i[:, None], 0.0, NEG)], 1))
    put("chunk", np.concatenate([np.zeros((P, P)), np.where(i[None] // 64 <= i[:, None] // 64, 0.0, NEG)], 1))
    perm = np.zeros((P, P))
    for head in range(0, P, 64):
        for d in range(8):
            perm[head + d + 8, head + d] = -1.0
            perm[head + d, head + d + 8] = 1.0
    put("perm", perm)
    j, t = i[:, None] % 64, np.arange(64)[None]
    levels = []
    for l in range(6):
        half = 32 >> l
        levels.append((j // (2 * half) == t // (2 * half)) & (j // half % 2 == 0) & (t // half % 2 == 1))
    levels.append(j == t)
    put("level", np.concatenate(levels, 1).astype(np.float32))
    put("scan", np.broadcast_to((np.arange(S) % 64 != 0).astype(np.float32), (P, S)))
    rot = (i % 64 < 16).astype(np.float32)
    inv = np.float32(500000.0) ** (-np.arange(0, 16, 2, dtype=np.float32) / np.float32(16))
    put("inv", (rot * inv[i % 8])[:, None])
    put("rot", rot[:, None])
    put("norot", 1.0 - rot[:, None])
    put("ln_eps", np.full((P, 1), 1e-5))
    put("rms_eps", np.full((P, 1), 1e-6))
    put("one", np.ones((P, 1)))
    return c


def build(nc, units_d, x_d, mem_d, pos_d, vec_d, const_d, narrow_a_d, narrow_b_d, narrow_f_d, w_a2_d, b_fgt_d, lam_d, out_d):
    f32, f32r = mybir.dt.float32, mybir.dt.float32r
    i32 = mybir.dt.int32
    ACT, AX = mybir.ActivationFunctionType, mybir.AxisListType
    ctx = ExitStack()
    with ctx:
        def sem(name):
            return ctx.enter_context(nc.semaphore(name))

        def sbuf(name, shape, dt=f32, where=ctx):
            return where.enter_context(nc.sbuf_tensor(name, shape, dt))

        raw = [sbuf(f"raw{i}", [P, UW]) for i in range(RING)]
        whi = [sbuf(f"whi{i}", [P, UW], f32r) for i in range(RING)]
        wlo = [sbuf(f"wlo{i}", [P, UW], f32r) for i in range(RING)]
        h = sbuf("h", [P, DB, S])
        z = sbuf("z", [P, DB, S])
        xh = sbuf("xh", [P, DB, S], f32r)
        xl = sbuf("xl", [P, DB, S], f32r)
        consts = sbuf("consts", [P, NC])
        vec = sbuf("vec", [P, NV])
        hvec = sbuf("hvec", [P, 32 + 8 + 1])
        zsum = sbuf("zsum", [P, S])
        dev = sbuf("dev", [P, 8])
        inv = sbuf("inv", [P, 8])

        def const(name, a=0, b=None):
            n = dict(CONSTS)[name]
            return consts[:, CC[name] + a:CC[name] + (n if b is None else b)]

        def vcol(name, i=0):
            return vec[:, COL[name] + i:COL[name] + i + 1]

        ident, ones = const("ident"), const("ones", 0, P)

        lg = [sbuf(f"lg{i}", [P, 2, S]) for i in range(2)]
        pr = [sbuf(f"pr{i}", [P, 2, S]) for i in range(2)]
        pT = [sbuf(f"pT{i}", [P, 4, P]) for i in range(2)]
        nmax = sbuf("nmax", [P, 2, 2])
        rsum = sbuf("rsum", [P, 2, 2])
        rinv = sbuf("rinv", [P, 2])
        squares_of = pr + lg

        def stage(*tensors):
            with ExitStack() as own:
                return [sbuf(t[0], t[1], t[2] if len(t) > 2 else f32, own) for t in tensors]

        (narrow_a, qT, kT, kswap, v_tok, iqT, ikT, cosT, sinT, ang, turns, posi, iw, work, selbias, rbuf0, rbuf1, rtmp,
         top8) = stage(
            ("narrow_a", [P, DB, 136]), ("qT", [P, 8, S]), ("kT", [P, 2, S]), ("kswap", [P, 2, S]),
            ("v_tok", [P, 2, S]), ("iqT", [P, 4, S]), ("ikT", [P, 1, S]), ("cosT", [P, S]), ("sinT", [P, S]),
            ("ang", [P, S]), ("turns", [P, S]), ("posi", [P, S], i32), ("iw", [P, 2, 8]), ("work", [P, 2, S]),
            ("selbias", [P, 2, S]), ("rbuf0", [P, 512]), ("rbuf1", [P, 512]), ("rtmp", [P, 2, S]), ("top8", [P, 8]))
        rbuf = [rbuf0, rbuf1]
        fh, fl, relu0, relu1, sqr0, sqr1 = stage(
            ("fh", [P, 16, S], f32r), ("fl", [P, 16, S], f32r), ("relu0", [P, 2, S]), ("relu1", [P, 2, S]),
            ("sqr0", [P, 2, S]), ("sqr1", [P, 2, S]))
        relu, sqr = [relu0, relu1], [sqr0, sqr1]
        narrow_b, w_a2, alow, gqT, gkT, gv_tok, rgate, gtmp, bcum, decay, qk, attnT, state = stage(
            ("narrow_b", [P, DB, 16]), ("w_a2", [16, 512]), ("alow", [16, S]), ("gqT", [P, 4, S]), ("gkT", [P, 4, S]),
            ("gv_tok", [P, 2, D]), ("rgate", [P, 8, S]), ("gtmp", [P, 4, S]), ("bcum", [P, 4, S]), ("decay", [P, 4, S]),
            ("qk", [P, 8, S]), ("attnT", [P, 8, 64]), ("state", [P, 4, S]))
        (narrow_f, aqT, gate, fqT, fkT, fv_tok, upad, conv, scpad, sgate, mtmp0, mtmp1, bhi, blo, lamv, lamt, fgt, fc,
         bfg) = stage(
            ("narrow_f", [P, DB, 8]), ("aqT", [P, 4, S]), ("gate", [P, 8, S]), ("fqT", [P, 4, S]), ("fkT", [P, 4, S]),
            ("fv_tok", [P, 2, 512]), ("upad", [P, 4, CPAD + S]), ("conv", [P, 4, S]), ("scpad", [P, 2, 2 + S]),
            ("sgate", [P, 4, S]), ("mtmp0", [P, 2, S]), ("mtmp1", [P, 2, S]), ("bhi", [P, 4, S], f32r),
            ("blo", [P, 4, S], f32r), ("lamv", [P, 4, 64]), ("lamt", [P, 8]), ("fgt", [8, S]), ("fc", [8, S]),
            ("bfg", [8, 1]))
        akT = gate[:, 0:4, :]
        av_tok = gate[:, 4:8, :].rearrange("p (t a) s -> p t (a s)", t=2)
        mtmp = [mtmp0, mtmp1]
        memT, xkT, xv_tok, xqT = stage(
            ("memT", [P, DB, S]), ("xkT", [P, 4, S]), ("xv_tok", [P, 2, 512]), ("xqT", [P, 4, S]))
        gh, gl, fpad0, fpad1, fconv, fth, fy = stage(
            ("gh", [P, FB, S], f32r), ("gl", [P, FB, S], f32r), ("fpad0", [P, 2, 2 + S]), ("fpad1", [P, 2, 2 + S]),
            ("fconv", [P, 2, 2, S]), ("fth", [P, 2, S]), ("fy", [P, 2, S]))
        fpad = [fpad0, fpad1]

        lin = [ctx.enter_context(nc.psum_tensor(f"lin{i}", [P, 2, S], f32)) for i in range(RING)]
        att = [ctx.enter_context(nc.psum_tensor(f"att{i}", [P, 512], f32)) for i in range(4)]

        raw_full = [sem(f"raw_full{i}") for i in range(RING)]
        hi_ready = sem("hi_ready")
        lo_ready = sem("lo_ready")
        job_done = sem("job_done")
        evac = [sem(f"evac{i}") for i in range(RING)]
        x_loaded, consts_loaded, vec_loaded = sem("x_loaded"), sem("consts_loaded"), sem("vec_loaded")
        pos_loaded, narrow_a_loaded, gla_loaded = sem("pos_loaded"), sem("narrow_a_loaded"), sem("gla_loaded")
        mix_loaded, mem_loaded, out_stored = sem("mix_loaded"), sem("mem_loaded"), sem("out_stored")
        split_hi, split_lo = sem("split_hi"), sem("split_lo")
        reduced, trig = sem("reduced"), sem("trig")
        roped, kswapped = sem("roped"), sem("kswapped")
        idx_acc, selected = sem("idx_acc"), sem("selected")
        lg_ready, neg_ready, exp_done, p_ready = sem("lg_ready"), sem("neg_ready"), sem("exp_done"), sem("p_ready")
        pT_psum, pT_sb, pv_psum, o_done = sem("pT_psum"), sem("pT_sb"), sem("pv_psum"), sem("o_done")
        z_summed, centered, squared, normed = sem("z_summed"), sem("centered"), sem("squared"), sem("normed")
        scaled, inv_ready = sem("scaled"), sem("inv_ready")
        relu_done, sqr_done, fhi, flo = sem("relu_done"), sem("sqr_done"), sem("fhi"), sem("flo")
        softplus = sem("softplus")
        gr_tanh, lvl_arg, lvl_exp, lvl_qk, attn_acc = sem("gr_tanh"), sem("lvl_arg"), sem("lvl_exp"), sem("lvl_qk"), sem("attn_acc")
        kd_ready, q_decayed, gla_squared, gla_y = sem("kd_ready"), sem("q_decayed"), sem("gla_squared"), sem("gla_y")
        fg_soft, fc_ready = sem("fg_soft"), sem("fc_ready")
        lam_dot, lam_exp = sem("lam_dot"), sem("lam_exp")
        ya_squared, b_y, b_hi, b_lo = sem("ya_squared"), sem("b_y"), sem("b_hi"), sem("b_lo")
        mixed, conv_done, conv_normed, conv_tanh = sem("mixed"), sem("conv_done"), sem("conv_normed"), sem("conv_tanh")
        ff_conv, ff_tanh, ff_y, ff_hi, ff_lo = sem("ff_conv"), sem("ff_tanh"), sem("ff_y"), sem("ff_hi"), sem("ff_lo")
        dve_step, act_step = sem("dve_step"), sem("act_step")

        def counts(events):
            n, out = 0, {}
            for name, k in events:
                out[name] = n
                n += k
            return out

        SPLIT = counts([(e, 4) for e in ("x", "ao", "mlp0", "gla", "go", "mlp1", "mix", "out", "mem", "xq")] + [("xo", 2), ("ffn", 4)])
        NORMED = counts([("ln0", 4), ("ln1", 4), ("ln2", 4), ("ln3", 4), ("post_mix", 4), ("post_x", 4), ("post_ffn", 4)])
        SCALED = counts([(e, 3) for e in ("ln0", "ln1", "ln2", "ln3", "pre_mix", "mem", "pre_x", "pre_ffn")])
        CENTERED = counts([(e, 3) for e in ("ln0", "ln1", "ln2", "ln3", "conv")])
        SQUARED = counts([("ln0", 4), ("ln1", 4), ("ln2", 4), ("ln3", 4), ("pre_mix", 4), ("conv", 2), ("mem", 4),
                          ("post_mix", 4), ("pre_x", 4), ("post_x", 4), ("pre_ffn", 4), ("post_ffn", 4)])
        INV = counts([(e, 1) for e in ("ln0", "ln1", "gla", "ln2", "ln3", "pre_mix", "ya", "conv", "mem", "post_mix", "pre_x",
                                       "post_x", "pre_ffn", "post_ffn")])
        SUMMED = {"ln0": 0, "ln1": 8, "ln2": 16, "ln3": 24}

        def per(n, g, step):
            return n if g is None else n + g * step

        def evacuated(eng, j, g=None):
            eng.wait_ge(evac[j % RING], per(j // RING + 1, g, 1))

        def filled(eng, j, g=None):
            eng.wait_ge(job_done, per(j + 1, g, RING))

        class Chain:

            def __init__(self, eng, s):
                self.eng, self.sem, self.n, self.g, self.step = eng, s, 0, None, 0

            def link(self, ins):
                ins.then_inc(self.sem, 1)
                self.n += 1
                self.eng.wait_ge(self.sem, per(self.n, self.g, self.step))

            def enter(self, g, step):
                self.g, self.step, self.first = g, step, self.n

            def leave(self, times):
                assert self.n - self.first == self.step, (self.n - self.first, self.step)
                self.n, self.g = self.first + times * self.step, None

        UNITS_ATT = [("A", i, None) for i in range(16)] + [("D", j, t) for j in range(4) for t in range(2)] \
            + [("F", i, None) for i in range(8)] + [("X", j, None) for j in range(4)]
        ATT0 = {k: [u[0] for u in UNITS_ATT].index(k) for k in "ADFX"}

        def att_keys(u, m):
            k, i, t = UNITS_ATT[u]
            return {"X": S, "D": P * ((t or 0) + 1)}.get(k, P * (m + 1))

        def att_blocks(u):
            return [(m, b) for m in range(1 if UNITS_ATT[u][0] == "D" else 2) for b in range(att_keys(u, m) // P)]

        def att_rows(u):
            k, i, t = UNITS_ATT[u]
            return slice(64 * (i % 2), 64 * (i % 2) + 64) if k in "AF" else slice(0, P)

        def att_cols(u):
            k, i, t = UNITS_ATT[u]
            return slice(P * t, P * t + P) if k == "D" else slice(0, S)

        def att_out(u):
            k, i, t = UNITS_ATT[u]
            return {"A": qT, "D": aqT, "F": fqT, "X": xqT}[k][att_rows(u), i // 2 if k in "AF" else i, att_cols(u)]

        def att_scores(u, m):
            bank, at = (m, 0) if UNITS_ATT[u][0] == "D" else (u % 2, S * m)
            return att[bank][:, at:at + att_keys(u, m)]

        def free_after(u, kinds):
            return u - 1 if u and UNITS_ATT[u][0] in kinds and UNITS_ATT[u - 1][0] in kinds else u

        block = ctx.enter_context(nc.Block())
        @block.sync
        def _(sp):
            def load(u, g=None):
                if u >= RING:
                    sp.wait_ge(lo_ready, per(u - RING + 1, g, RING))
                sp.dma_start(raw[u % RING][:], units_d[per(u, g, RING)]).then_inc(raw_full[u % RING], 16)

            sp.dma_start(h[:], x_d).then_inc(x_loaded, 16)
            for u in range(RING):
                load(u)
            with sp.Fori(0, NU // RING - 1) as g:
                for u in range(RING, 2 * RING):
                    load(u, g)
            for u in range(NU // RING * RING, NU):
                load(u)
            for c in range(4):
                sp.wait_ge(normed, NORMED["post_ffn"] + c + 1)
                sp.dma_start(out_d[:, 2 * c:2 * c + 2, :], h[:, 2 * c:2 * c + 2, :]).then_inc(out_stored, 16)
            sp.wait_ge(out_stored, 64)

        @block.gpsimd
        def _(pool):
            def low_part(u, g=None):
                pool.wait_ge(hi_ready, per(u + 1, g, RING))
                nc.gpsimd.tensor_tensor(wlo[u % RING][:], raw[u % RING][:], whi[u % RING][:].bitcast(f32), ALU.subtract).then_inc(lo_ready, 1)

            with pool.Fori(0, NU // RING) as g:
                for u in range(RING):
                    low_part(u, g)
            for u in range(NU // RING * RING, NU):
                low_part(u)

        @block.tensor
        def _(pe):
            mm = nc.tensor.matmul

            def bank(j, g=None):
                if j >= RING:
                    evacuated(pe, j - RING, g)
                return lin[j % RING]

            def three(out, w, a, first, last):
                mm(out, w[0], a[0], start=first, stop=False)
                mm(out, w[0], a[1], start=False, stop=False)
                return mm(out, w[1], a[0], start=False, stop=last)

            def tile(u, i, n=1):
                return (whi[u % RING][:, i * P:(i + n) * P], wlo[u % RING][:, i * P:(i + n) * P])

            def arrived(u, g=None):
                pe.wait_ge(lo_ready, per(u + 1, g, RING))

            def unit_up(u, j, g=None, event=None):
                arrived(u, g)
                o = bank(j, g)
                for m in range(2):
                    for k in range(DB):
                        if event and m == 0 and k % 2 == 0:
                            have(event, k // 2 + 1)
                        last = three(o[:, m, :], tile(u, m * DB + k), (xh[:, k, :], xl[:, k, :]), k == 0, k == DB - 1)
                last.then_inc(job_done, 1)

            def unit_down(u, j, first, g=None):
                arrived(u, g)
                o = bank(j, g)
                for k in range(UT):
                    if first is not None and k % 2 == 0:
                        pe.wait_ge(flo, first + k // 2 + 1)
                    last = three(o[:, 0, :], tile(u, k), (fh[:, k, :], fl[:, k, :]), k == 0, k == UT - 1)
                last.then_inc(job_done, 1)

            def unit_tok(u, j):
                arrived(u)
                o = bank(j)
                for t in range(2):
                    for k in range(DB):
                        at = slice(t * P, (t + 1) * P)
                        last = three(o[:, t, :], (xh[:, k, at], xl[:, k, at]), tile(u, 2 * k, 2), k == 0, k == DB - 1)
                last.then_inc(job_done, 1)

            def unit_wide(u, j, a):
                arrived(u)
                for b in range(2):
                    o = bank(j + b)
                    for m in range(2):
                        for k in range(4):
                            last = three(o[:, m, :], tile(u, (2 * b + m) * 4 + k), (a[0][:, k, :], a[1][:, k, :]), k == 0, k == 3)
                    last.then_inc(job_done, 1)

            def ups(name, event=None):
                for i in range(COUNT[name]):
                    unit_up(U0[name] + i, JOB[name, i], None, event if i == 0 else None)

            def have(event, n=4):
                pe.wait_ge(split_lo, SPLIT[event] + n)

            def token_sum(o, col, block, first, last):
                for t in range(2):
                    ins = mm(o[:, 0, col + t:col + t + 1], block[:, t * P:(t + 1) * P], ones[:, 0:1], start=first and t == 0, stop=last and t == 1)
                return ins

            def square_sum(name, blocks=DB):
                o = bank(JOB[name + "_sq", 0])
                for m in range(blocks):
                    if m % 2 == 0:
                        pe.wait_ge(squared, SQUARED[name] + m // 2 + 1)
                    last = token_sum(o, 0, squares_of[m // 2][:, m % 2, :], m == 0, m == blocks - 1)
                last.then_inc(job_done, 1)

            def spread(name, i=0, heads=1):
                pe.wait_ge(inv_ready, INV[name] + 1)
                o = bank(JOB[name + "_rstd", i])
                for n in range(heads):
                    for t in range(2):
                        col = 2 * (i * heads + n) + t
                        last = mm(o[:, n, t * P:(t + 1) * P], inv[:, col:col + 1].broadcast_to([P, P]), ident, start=True, stop=True)
                last.then_inc(job_done, 1)

            def norm(name):
                square_sum(name)
                spread(name)

            def layer_norm(name):
                pe.wait_ge(z_summed, SUMMED[name] + DB)
                mm(bank(JOB[name + "_mean", 0])[:, 0, :], ones, zsum[:], start=True, stop=True).then_inc(job_done, 1)
                norm(name)

            def att_logits(u):
                k, i, t = UNITS_ATT[u]
                if free_after(u, "AFX"):
                    pe.wait_ge(neg_ready, free_after(u, "AFX"))
                for m in range(2):
                    o = att_scores(u, m)
                    w = att_keys(u, m)
                    q = slice((m if t is None else t) * P, (m if t is None else t) * P + P)
                    r = att_rows(u)
                    if k == "A":
                        keys = kT if i // 4 % 2 == i % 2 else kswap
                        last = mm(o, qT[r, i // 2, q], keys[r, i // 8, 0:w], start=True, stop=True)
                    elif k == "D":
                        r = slice(64 * m, 64 * m + 64)
                        last = mm(o, aqT[r, i, q], akT[r, i, 0:w], start=True, stop=True)
                    elif k == "F":
                        mm(o, fqT[r, i // 2, q], fkT[r, i // 2, 0:w], start=True, stop=False)
                        last = mm(o, ident[0:8, i:i + 1].broadcast_to([8, P]), fc[:, 0:w], start=False, stop=True)
                    else:
                        last = mm(o, xqT[:, i, q], xkT[:, i, :], start=True, stop=True)
                last.then_inc(lg_ready, 1)

            def att_transpose(u):
                pe.wait_ge(p_ready, u + 1)
                if u:
                    pe.wait_ge(pT_sb, u)
                for n, (m, b) in enumerate(att_blocks(u)):
                    last = nc.tensor.transpose(att[2][:, n * P:(n + 1) * P], pr[u % 2][:, m, b * P:(b + 1) * P], ident)
                last.then_inc(pT_psum, 1)

            def att_values(u):
                k, i, t = UNITS_ATT[u]
                pe.wait_ge(pT_sb, u + 1)
                if free_after(u, "AF"):
                    pe.wait_ge(o_done, free_after(u, "AF"))
                for n, (m, b) in enumerate(att_blocks(u)):
                    o = att[3][att_rows(u), m * P:(m + 1) * P]
                    if k == "A":
                        v = v_tok[:, b, 64 * (i // 4):64 * (i // 4) + 64]
                    elif k == "F":
                        v = fv_tok[:, b, 64 * i:64 * i + 64]
                    else:
                        v = (av_tok if k == "D" else xv_tok)[:, b, i * P:(i + 1) * P]
                    last = mm(o, v, pT[u % 2][:, n, :], start=b == 0, stop=b == att_keys(u, m) // P - 1)
                last.then_inc(pv_psum, 1)

            def att_step(s, u0, n):
                if s < n:
                    att_logits(u0 + s)
                if 2 <= s < n + 2:
                    att_transpose(u0 + s - 2)
                if 3 <= s < n + 3:
                    att_values(u0 + s - 3)

            pe.wait_ge(consts_loaded, 16)
            pe.wait_ge(narrow_a_loaded, 16)
            ups("iq", "x")
            o = bank(JOB["ik", 0])
            for k in range(DB):
                last = mm(o[:, 0, :], narrow_a[:, k, 0:P], h[:, k, :], start=k == 0, stop=k == DB - 1)
            last.then_inc(job_done, 1)
            o = bank(JOB["iw", 0])
            for t in range(2):
                for k in range(DB):
                    last = mm(o[:, t, 0:8], h[:, k, t * P:(t + 1) * P], narrow_a[:, k, P:P + 8], start=k == 0, stop=k == DB - 1)
            last.then_inc(job_done, 1)

            def rope(r, raw_jobs, src):
                for j in raw_jobs:
                    evacuated(pe, j)
                o = bank(JOB["rope", r])
                n = src.shape[1]
                mm(o[:, 0:n, :], const("perm"), src, start=True, stop=True).then_inc(job_done, 1)

            rope(0, [JOB["iq", 0]], iqT[:, 0:2, :])
            rope(1, [JOB["iq", 1]], iqT[:, 2:4, :])
            rope(2, [JOB["ik", 0]], ikT[:])
            ups("k")
            unit_tok(U0["v"], JOB["v", 0])
            rope(3, [JOB["k", 0]], kT[:])
            pe.wait_ge(roped, 3)
            for i in range(6):
                o = bank(JOB["idx", i])
                t, heads = (0, range(i, 8, 2)) if i < 2 else (1, [(0, 2), (4, 6), (1, 3), (5, 7)][i - 2])
                w = P * (t + 1)
                for n, hd in enumerate(heads):
                    r = slice(64 * (hd % 2), 64 * (hd % 2) + 64)
                    last = mm(o[:].rearrange("p a s -> p (a s)")[:, n * w:(n + 1) * w], iqT[r, hd // 2, t * P:(t + 1) * P], ikT[r, 0, 0:w], start=True, stop=True)
                last.then_inc(job_done, 1)
            ups("q")
            for i in range(4):
                rope(4 + i, [JOB["q", i]], qT[:, 2 * i:2 * i + 2, :])
            pe.wait_ge(roped, 8)
            pe.wait_ge(kswapped, 2)
            evacuated(pe, JOB["v", 0])
            for s in range(16 + 3):
                att_step(s, ATT0["A"], 16)
            ups("ao", "ao")

            layer_norm("ln0")

            def mlp(layer):
                for half in range(2):
                    up, dn = f"up{layer}{half}", f"dn{layer}{half}"
                    with pe.Fori(0, 2) as g:
                        for i in range(RING):
                            unit_up(U0[up] + i, JOB[up, i], g, f"mlp{layer}" if half == i == 0 else None)
                    with pe.Fori(0, 2) as g:
                        for i in range(RING):
                            unit_down(U0[dn] + i, JOB[dn, i], None if i else 8 * (2 * layer + half), g)
                layer_norm(f"ln{2 * layer + 1}")

            mlp(0)

            ups("gq", "gla")
            ups("gk")
            pe.wait_ge(gla_loaded, 32)
            pe.wait_ge(normed, NORMED["ln1"] + 4)
            o = bank(JOB["alow", 0])
            for k in range(DB):
                last = mm(o[0:16, 0, :], narrow_b[:, k, :], h[:, k, :], start=k == 0, stop=k == DB - 1)
            last.then_inc(job_done, 1)
            evacuated(pe, JOB["alow", 0])
            for i in range(2):
                o = bank(JOB["gate_a", i])
                for n in range(2):
                    hd = 2 * i + n
                    last = mm(o[:, n, :], w_a2[:, hd * P:(hd + 1) * P], alow[:], start=True, stop=True)
                last.then_inc(job_done, 1)
            for i in range(2):
                unit_tok(U0["gv"] + i, JOB["gv", i])

            def level(l):
                if l < 6:
                    pe.wait_ge(lvl_qk, l + 1)
                o = bank(JOB["level", l])[:].rearrange("p a (b s) -> p (a b) s", s=64)
                for hd in range(4):
                    for c in range(4):
                        at = slice(c * 64, c * 64 + 64)
                        keys, queries = (qk[:, 4 + hd, at], qk[:, hd, at]) if l < 6 else (gkT[:, hd, at], gqT[:, hd, at])
                        last = mm(o[64 * (c % 2):64 * (c % 2) + 64, hd * 2 + c // 2, :], keys, queries, start=True, stop=True)
                last.then_inc(job_done, 1)

            for l in range(7):
                if l in GLA_FILL:
                    name, i = GLA_FILL[l]
                    (unit_tok if name == "gv" else unit_up)(U0[name] + i, JOB[name, i])
                level(l)
            pe.wait_ge(kd_ready, 1)
            for t in range(2):
                o = bank(JOB["kd", t])[:].rearrange("p a s -> p (a s)")
                for hd in range(4):
                    last = nc.tensor.transpose(o[:, hd * P:(hd + 1) * P], qk[:, 4 + hd, t * P:(t + 1) * P], ident)
                last.then_inc(job_done, 1)
            kd_tok = gtmp[:].rearrange("p (t a) s -> p t (a s)", t=2)
            pe.wait_ge(attn_acc, 6)
            pe.wait_ge(q_decayed, 1)
            for t in range(2):
                evacuated(pe, JOB["kd", t])
            for i in range(4):
                evacuated(pe, JOB["gv", i])
            for c in range(4):
                t, r = c // 2, slice(64 * (c % 2), 64 * (c % 2) + 64)
                if c:
                    evacuated(pe, JOB["state", 2 * c - 2])
                    evacuated(pe, JOB["state", 2 * c - 1])
                o = bank(JOB["gla_o", c])[:].rearrange("p a (b s) -> p (a b) s", s=64)
                for hd in range(4):
                    for dv in range(2):
                        at = slice(hd * S + dv * P, hd * S + dv * P + P)
                        if c:
                            mm(o[:, 2 * hd + dv, :], state[:, hd, dv * P:(dv + 1) * P], gqT[:, hd, c * 64:c * 64 + 64], start=True, stop=False)
                        last = mm(o[:, 2 * hd + dv, :], gv_tok[r, t, at], attnT[r, hd * 2 + t, :], start=c == 0, stop=True)
                last.then_inc(job_done, 1)
                if c < 3:
                    for i in range(2):
                        o = bank(JOB["state", 2 * c + i])
                        for n in range(2):
                            hd = 2 * i + n
                            last = mm(o[:, n, :], kd_tok[r, t, hd * P:(hd + 1) * P], gv_tok[r, t, hd * S:(hd + 1) * S], start=True, stop=True)
                        last.then_inc(job_done, 1)
                if c == 0:
                    unit_up(U0["gr"] + 3, JOB["gr", 3])
            o = bank(JOB["gla_sq", 0])
            for hd in range(4):
                pe.wait_ge(gla_squared, hd + 1)
                for b in range(2):
                    last = token_sum(o, 2 * hd, z[:, 2 * hd + b, :], hd == b == 0, hd == 3 and b == 1)
            last.then_inc(job_done, 1)
            for i in range(2):
                spread("gla", i, 2)
            ups("go", "go")
            layer_norm("ln2")
            mlp(1)

            norm("pre_mix")
            have("mix")
            pe.wait_ge(mix_loaded, 48)
            o = bank(JOB["fg", 0])
            for k in range(DB):
                last = mm(o[0:8, 0, :], narrow_f[:, k, :], z[:, k, :], start=k == 0, stop=k == DB - 1)
            last.then_inc(job_done, 1)
            for name in ("aq", "ak"):
                ups(name)
            for i in range(2):
                unit_tok(U0["av"] + i, JOB["av", i])
            for name in ("fq", "fk"):
                ups(name)
            for i in range(2):
                unit_tok(U0["fv"] + i, JOB["fv", i])
            pe.wait_ge(fc_ready, 1)
            for i in range(2):
                for name in ("aq", "ak", "av", "fq", "fk", "fv"):
                    evacuated(pe, JOB[name, i])
            fill = [("c", i) for i in range(4)] + [("s", i) for i in range(6)]
            for s, (name, i) in enumerate(fill):
                unit_up(U0[name] + i, JOB[name, i])
                att_step(s, ATT0["D"], 16)
            unit_up(U0["gate0"], JOB["gate0", 0])
            att_step(10, ATT0["D"], 16)
            pe.wait_ge(ya_squared, 2)
            o = bank(JOB["ya_sq", 0])
            for hd in range(4):
                last = token_sum(o, 2 * hd, z[:, hd, :], hd == 0, hd == 3)
            last.then_inc(job_done, 1)
            for i in range(1, 4):
                unit_up(U0["gate0"] + i, JOB["gate0", i])
                att_step(10 + i, ATT0["D"], 16)
                if i == 1:
                    spread("ya", 0, 2)
                    spread("ya", 1, 2)

            def branch(n, b, i):
                if i == 0:
                    pe.wait_ge(b_lo, 2 * n + 2)
                unit_wide(U0[f"br{b}"] + i, JOB[f"br{b}", i], (bhi, blo))

            for i in range(2):
                branch(0, 0, i)
                att_step(14 + i, ATT0["D"], 16)
            for i in range(4):
                unit_up(U0["gate3"] + i, JOB["gate3", i])
                att_step(16 + i, ATT0["D"], 16)
            for i in range(2):
                branch(1, 3, i)
            for i in range(4):
                unit_up(U0["gate1"] + i, JOB["gate1", i])
                if i == 1:
                    o = bank(JOB["conv_mean", 0])
                    pe.wait_ge(conv_done, 1)
                    for m in range(4):
                        last = mm(o[:, 0, :], ones, conv[:, m, :], start=m == 0, stop=m == 3)
                    last.then_inc(job_done, 1)
                elif i == 2:
                    square_sum("conv", 4)
                elif i == 3:
                    spread("conv")
            for i in range(2):
                branch(2, 1, i)
            ups("gate2")
            for i in range(2):
                branch(3, 2, i)
            ups("out", "out")

            norm("mem")
            square_sum("post_mix")
            unit_up(U0["xk"], JOB["xk", 0], None, "mem")
            spread("post_mix")
            unit_up(U0["xk"] + 1, JOB["xk", 1])
            unit_tok(U0["xv"], JOB["xv", 0])
            square_sum("pre_x")
            unit_tok(U0["xv"] + 1, JOB["xv", 1])
            spread("pre_x")
            ups("xq", "xq")
            for i in range(2):
                for name in ("xk", "xv", "xq"):
                    evacuated(pe, JOB[name, i])
            for s in range(4 + 3):
                att_step(s, ATT0["X"], 4)
            have("xo", 2)
            for i in range(2):
                unit_wide(U0["xo"] + i, JOB["xo", i], (xh, xl))
            norm("post_x")

            norm("pre_ffn")
            ups("fu", "ffn")
            for n in range(DB * FB):
                i, k = divmod(n, FB)
                if n % UT == 0:
                    arrived(U0["fd"] + n // UT)
                if k == 0:
                    o = bank(JOB["fd", i])
                if i == 0:
                    pe.wait_ge(ff_lo, k + 1)
                last = three(o[:, 0, :], tile(U0["fd"] + n // UT, n % UT), (gh[:, k, :], gl[:, k, :]), k == 0, k == FB - 1)
                if k == FB - 1:
                    last.then_inc(job_done, 1)
            norm("post_ffn")

        @block.scalar
        def _(act):
            f = nc.scalar.activation
            chain = Chain(act, act_step)
            eps_ln, eps_rms, one = const("ln_eps"), const("rms_eps"), const("one")

            def two(t, c):
                return t[:, 2 * c:2 * c + 2, :]

            def high_part(u, g=None, used=None):
                if u >= NU:
                    return
                act.wait_ge(raw_full[u % RING], per(16 * (u // RING + 1), g, 16))
                if u >= RING:
                    act.wait_ge(job_done, per(LAST[u - RING] + 1 if used is None else used, g, RING))
                f(whi[u % RING][:], raw[u % RING][:], ACT.Copy).then_inc(hi_ready, 1)

            def unit(name, i):
                high_part(U0[name] + i + AHEAD)
                filled(act, JOB[name, i])

            def passed(name):
                for i in range(COUNT[name]):
                    high_part(U0[name] + i + AHEAD)

            def copy(name, i, dst, scale=1.0):
                unit(name, i)
                j = JOB[name, i]
                f(dst, lin[j % RING][:], ACT.Copy, scale=scale).then_inc(evac[j % RING], 1)

            def split(event, src, ready, n=4):
                for c in range(n):
                    ready(c)
                    f(two(xh, c), two(src, c), ACT.Copy).then_inc(split_hi, 1)

            def squares(name, src, ready, n=4, bias=None):
                for c in range(n):
                    ready(c)
                    if bias is None:
                        last = f(squares_of[c][:], two(src, c), ACT.Square)
                    else:
                        for m in range(2):
                            last = f(squares_of[c][:, m, :], src[:, 2 * c + m, :], ACT.Square, bias=bias(2 * c + m))
                    last.then_inc(squared, 1)

            def deviation(name, width, eps, n=2):
                j = JOB[name + "_sq", 0]
                filled(act, j)
                if INV[name]:
                    act.wait_ge(inv_ready, INV[name])
                f(dev[:, 0:n], lin[j % RING][:, 0, 0:n], ACT.Sqrt, scale=1.0 / width, bias=eps).then_inc(evac[j % RING], 1)

            def is_scaled(name):
                return lambda c: act.wait_ge(scaled, SCALED[name] + c + 1) if c < 3 else evacuated(act, JOB[name + "_rstd", 0])

            def is_normed(name):
                return lambda c: act.wait_ge(normed, NORMED[name] + c + 1)

            def is_centered(name, n=4):
                return lambda c: act.wait_ge(centered, CENTERED[name] + c + 1) if c < n - 1 else evacuated(act, JOB[name + "_mean", 0])

            def layer_norm(name, event, bias):
                squares(name, z, is_centered(name))
                deviation(name, D, eps_ln)
                if event:
                    for c in range(4):
                        is_scaled(name)(c)
                        for m in (2 * c, 2 * c + 1):
                            last = f(xh[:, m, :], z[:, m, :], ACT.Identity, bias=bias(m))
                        last.then_inc(split_hi, 1)

            def att_exp(u):
                act.wait_ge(neg_ready, u + 1)
                if u >= 2:
                    act.wait_ge(pT_psum, u - 1)
                for m in range(2):
                    w = att_keys(u, m)
                    last = f(pr[u % 2][:, m, 0:w], lg[u % 2][:, m, 0:w], ACT.Exp, scale=-1.0, bias=nmax[:, u % 2, m:m + 1],
                             accum_out=rsum[:, u % 2, m:m + 1])
                last.then_inc(exp_done, 1)

            def att_transposed(u):
                act.wait_ge(pT_psum, u + 1)
                if u >= 2:
                    act.wait_ge(pv_psum, u - 1)
                n = len(att_blocks(u))
                f(pT[u % 2][:, 0:n, :], att[2][:, 0:n * P].rearrange("p (n q) -> p n q", q=P), ACT.Copy).then_inc(pT_sb, 1)

            def att_result(u):
                act.wait_ge(pv_psum, u + 1)
                n = 1 if UNITS_ATT[u][0] == "D" else 2
                f(att_out(u), att[3][att_rows(u), 0:n * P], ACT.Copy).then_inc(o_done, 1)

            def att_step(s, u0, n):
                if s < n:
                    att_exp(u0 + s)
                if 2 <= s < n + 2:
                    att_transposed(u0 + s - 2)
                if 3 <= s < n + 3:
                    att_result(u0 + s - 3)

            act.dma_start(consts[:], const_d).then_inc(consts_loaded, 16)
            act.dma_start(posi[:], pos_d.partition_broadcast(P)).then_inc(pos_loaded, 16)
            act.dma_start(narrow_a[:], narrow_a_d).then_inc(narrow_a_loaded, 16)
            act.dma_start(vec[:], vec_d).then_inc(vec_loaded, 16)
            split("x", h, lambda c: act.wait_ge(x_loaded, 16))
            for u in range(AHEAD):
                high_part(u)
            act.wait_ge(reduced, 2)
            f(sinT[:], sinT[:], ACT.Sin).then_inc(trig, 1)
            f(cosT[:], cosT[:], ACT.Sin).then_inc(trig, 1)
            for i in range(2):
                copy("iq", i, two(iqT, i))
            j = JOB["ik", 0]
            filled(act, j)
            f(ikT[:, 0, :], lin[j % RING][:, 0, :], ACT.Copy).then_inc(evac[j % RING], 1)
            copy("k", 0, kT[:])
            copy("v", 0, v_tok[:])
            for i in range(6):
                j = JOB["idx", i]
                filled(act, j)
                if i >= 2:
                    act.wait_ge(idx_acc, i - 1)
                f(rbuf[i % 2][:], lin[j % RING][:].rearrange("p a s -> p (a s)"), ACT.Relu, scale=64 ** -0.5).then_inc(evac[j % RING], 1)
            for i in range(4):
                copy("q", i, two(qT, i))
            for s in range(16 + 3):
                att_step(s, ATT0["A"], 16)
            split("ao", qT, lambda c: act.wait_ge(o_done, 4 * c + 4))
            passed("ao")
            layer_norm("ln0", "mlp0", lambda m: vcol("ln_mix_b", m))

            def mlp(layer):
                for half in range(2):
                    up, dn = f"up{layer}{half}", f"dn{layer}{half}"
                    base = 8 * (2 * layer + half)
                    with act.Fori(0, 2) as g:
                        for i in range(RING):
                            j = JOB[up, i]
                            high_part(U0[up] + i + AHEAD, g, j)
                            filled(act, j, g)
                            f(relu[i % 2][:], lin[j % RING][:], ACT.Relu).then_inc(evac[j % RING], 1)
                            act.wait_ge(sqr_done, per(base + i + 1, g, RING))
                            f(fh[:, bass.ds(g * 8 + 2 * i, 2), :], sqr[i % 2][:], ACT.Copy).then_inc(fhi, 1)
                    with act.Fori(0, 2) as g:
                        for i in range(RING):
                            high_part(U0[dn] + i + AHEAD, g, JOB[dn, i])
                layer_norm(f"ln{2 * layer + 1}", "gla" if layer == 0 else None, lambda m: vcol("ln_mlp_b", m))

            mlp(0)

            act.dma_start(narrow_b[:], narrow_b_d).then_inc(gla_loaded, 16)
            act.dma_start(w_a2[:], w_a2_d).then_inc(gla_loaded, 16)
            for i in range(2):
                copy("gq", i, two(gqT, i), 128 ** -0.5)
            for i in range(2):
                copy("gk", i, two(gkT, i))
            j = JOB["alow", 0]
            filled(act, j)
            f(alow[:], lin[j % RING][0:16, 0, :], ACT.Copy).then_inc(evac[j % RING], 1)
            for i in range(2):
                evacuated(act, JOB["gate_a", i])
            chain.link(f(decay[:], gtmp[:], ACT.Abs))
            chain.link(f(decay[:], decay[:], ACT.Exp, scale=-1.0))
            f(decay[:], decay[:], ACT.Ln, bias=one).then_inc(softplus, 1)
            def gla_fill(name, i):
                if name == "gv":
                    copy("gv", i, gv_tok[:, :, i * S:(i + 1) * S])
                else:
                    unit("gr", i)
                    f(two(rgate, i), lin[JOB["gr", i] % RING][:], ACT.Tanh, scale=0.5).then_inc(gr_tanh, 1)

            for i in range(2):
                gla_fill("gv", i)

            def level_decay(l):
                act.wait_ge(lvl_arg, l + 1)
                chain.link(f(decay[:], gtmp[:], ACT.Abs))
                f(decay[:], decay[:], ACT.Exp, scale=-1.0 / 16).then_inc(lvl_exp, 1)

            level_decay(0)
            for l in range(6):
                if l in GLA_FILL:
                    gla_fill(*GLA_FILL[l])
                if l < 5:
                    level_decay(l + 1)
            act.wait_ge(lvl_arg, 7)
            f(decay[:], bcum[:], ACT.Exp, scale=1.0 / 16).then_inc(lvl_exp, 1)
            f(gtmp[:], gtmp[:], ACT.Exp, scale=-1.0 / 16).then_inc(lvl_exp, 1)
            act.wait_ge(kd_ready, 1)
            kd_tok = gtmp[:].rearrange("p (t a) s -> p t (a s)", t=2)
            for t in range(2):
                j = JOB["kd", t]
                filled(act, j)
                f(kd_tok[:, t, :], lin[j % RING][:].rearrange("p a s -> p (a s)"), ACT.Copy).then_inc(evac[j % RING], 1)
            for c in range(4):
                j = JOB["gla_o", c]
                filled(act, j)
                f(qk[:, :, c * 64:(c + 1) * 64], lin[j % RING][:].rearrange("p a (b s) -> p (a b) s", s=64), ACT.Copy).then_inc(evac[j % RING], 1)
                if c == 0:
                    gla_fill("gr", 3)
            for hd in range(4):
                if hd == 0:
                    evacuated(act, JOB["gla_o", 3])
                    act.wait_ge(attn_acc, 6)
                f(two(z, hd), two(qk, hd), ACT.Square).then_inc(gla_squared, 1)
            deviation("gla", S, eps_rms, 8)
            split("go", qk, lambda c: act.wait_ge(gla_y, c + 1))
            passed("go")
            layer_norm("ln2", "mlp1", lambda m: vcol("ln_mix_b", DB + m))
            mlp(1)

            squares("pre_mix", z, is_scaled("ln3"), 4, lambda m: vcol("ln_mlp_b", DB + m))
            deviation("pre_mix", D, eps_rms)
            act.dma_start(narrow_f[:], narrow_f_d).then_inc(mix_loaded, 16)
            act.dma_start(lamv[:], lam_d.partition_broadcast(P)).then_inc(mix_loaded, 16)
            act.dma_start(bfg[:], b_fgt_d).then_inc(mix_loaded, 16)
            split("mix", z, is_scaled("pre_mix"))
            evacuated(act, JOB["fg", 0])
            chain.link(f(fc[:], fgt[:], ACT.Abs))
            chain.link(f(fc[:], fc[:], ACT.Exp, scale=-1.0))
            f(fc[:], fc[:], ACT.Ln, bias=one[0:8, :]).then_inc(fg_soft, 1)
            act.wait_ge(lam_dot, 2)
            f(lamt[:, 2:4], lamt[:, 0:2], ACT.Exp).then_inc(lam_exp, 1)
            for name, dst in (("aq", aqT), ("ak", akT)):
                for i in range(2):
                    copy(name, i, two(dst, i))
            for i in range(2):
                copy("av", i, av_tok[:, :, i * S:(i + 1) * S])
            for name, dst in (("fq", fqT), ("fk", fkT)):
                for i in range(2):
                    copy(name, i, two(dst, i))
            for i in range(2):
                copy("fv", i, fv_tok[:, :, i * S:(i + 1) * S])

            def branch_split(n, src, ready):
                for c in range(2):
                    ready(c)
                    f(two(bhi, c), two(src, c), ACT.Copy).then_inc(b_hi, 1)

            def gates(b, i):
                unit(f"gate{b}", i)
                j = JOB[f"gate{b}", i]
                for m in range(2):
                    col = b * 8 + 2 * i + m
                    last = f(gate[:, 2 * i + m, :], lin[j % RING][:, m, :], ACT.Tanh, scale=0.5, bias=hvec[:, col:col + 1])
                last.then_inc(evac[j % RING], 1)

            for s in range(10):
                if s < 4:
                    unit("c", s)
                    j = JOB["c", s]
                    if s % 2 == 0:
                        if s:
                            evacuated(act, JOB["c", s - 1])
                        for m in range(2):
                            last = f(mtmp[0][:, m, :], lin[j % RING][:, m, :], ACT.Tanh, scale=0.5, bias=hvec[:, 36 + s + m:37 + s + m])
                        last.then_inc(evac[j % RING], 1)
                else:
                    i = s - 4
                    unit("s", i)
                    j = JOB["s", i]
                    if i % 3 == 0:
                        if i:
                            evacuated(act, JOB["s", i - 2])
                        f(mtmp[1][:], lin[j % RING][:], ACT.Copy).then_inc(evac[j % RING], 1)
                    elif i % 3 == 2:
                        f(two(sgate, i // 3), lin[j % RING][:], ACT.Copy).then_inc(evac[j % RING], 1)
                att_step(s, ATT0["D"], 16)
            att_step(10, ATT0["D"], 16)
            gates(0, 0)
            deviation("ya", P, eps_rms, 8)
            for i in range(1, 4):
                gates(0, i)
                att_step(10 + i, ATT0["D"], 16)
            branch_split(0, aqT, lambda c: evacuated(act, JOB["ya_rstd", c]))
            for i in range(2):
                high_part(U0["br0"] + i + AHEAD)
                att_step(14 + i, ATT0["D"], 16)
            for i in range(4):
                if i < 2:
                    act.wait_ge(mixed, 2 * i + 2)
                gates(3, i)
                if i == 0:
                    branch_split(1, sgate, lambda c: act.wait_ge(b_y, c + 1))
                att_step(16 + i, ATT0["D"], 16)
            passed("br3")
            for i in range(4):
                if i < 2:
                    act.wait_ge(mixed, 4 + 2 * i + 2)
                gates(1, i)
                if i == 0:
                    branch_split(2, fqT, lambda c: act.wait_ge(o_done, 32))
                elif i == 1:
                    squares("conv", conv, is_centered("conv", 2), 2)
                elif i == 2:
                    deviation("conv", 512, eps_rms)
            for i in range(2):
                act.wait_ge(conv_normed, i + 1)
                if i == 0:
                    act.wait_ge(mixed, 8)
                f(mtmp[i][:], two(conv, i), ACT.Tanh, scale=0.5).then_inc(conv_tanh, 1)
            passed("br1")
            for i in range(4):
                if i < 2:
                    act.wait_ge(mixed, 8 + 2 * i + 2)
                gates(2, i)
                if i == 0:
                    branch_split(3, conv, lambda c: act.wait_ge(b_y, 2 + c + 1))
            passed("br2")
            split("out", z, lambda c: act.wait_ge(mixed, 16))
            act.dma_start(memT[:], mem_d).then_inc(mem_loaded, 16)
            for i in range(4):
                copy("out", i, two(z, i))

            squares("mem", memT, lambda c: act.wait_ge(mem_loaded, 16))
            deviation("mem", D, eps_rms)
            squares("post_mix", z, lambda c: evacuated(act, JOB["out", c]))
            split("mem", memT, is_scaled("mem"))
            deviation("post_mix", D, eps_rms)
            for i in range(2):
                copy("xk", i, two(xkT, i))
            copy("xv", 0, xv_tok[:, :, 0:S])
            squares("pre_x", h, is_normed("post_mix"))
            deviation("pre_x", D, eps_rms)
            copy("xv", 1, xv_tok[:, :, S:2 * S])
            split("xq", z, is_scaled("pre_x"))
            for i in range(2):
                copy("xq", i, two(xqT, i))
            for s in range(4 + 3):
                att_step(s, ATT0["X"], 4)
            split("xo", xqT, lambda c: act.wait_ge(o_done, ATT0["X"] + 2 * c + 2), 2)
            passed("xo")
            for c in range(4):
                j = JOB["xo", 0] + c
                filled(act, j)
                f(two(z, c), lin[j % RING][:], ACT.Copy).then_inc(evac[j % RING], 1)
            squares("post_x", z, lambda c: evacuated(act, JOB["xo", 0] + c))
            deviation("post_x", D, eps_rms)

            squares("pre_ffn", h, is_normed("post_x"))
            deviation("pre_ffn", D, eps_rms)
            split("ffn", z, is_scaled("pre_ffn"))
            for s in range(FB + 2):
                if s < FB:
                    u = s
                    unit("fu", u)
                    if u >= 2:
                        act.wait_ge(ff_conv, u - 1)
                    j = JOB["fu", u]
                    f(fpad[u % 2][:, :, 2:], lin[j % RING][:], ACT.Copy).then_inc(evac[j % RING], 1)
                if 1 <= s < FB + 1:
                    u = s - 1
                    act.wait_ge(ff_conv, u + 1)
                    if u >= 2:
                        act.wait_ge(ff_y, u - 1)
                    f(fth[:, u % 2, :], fconv[:, u % 2, 0, :], ACT.Tanh, scale=0.5).then_inc(ff_tanh, 1)
                if s >= 2:
                    u = s - 2
                    act.wait_ge(ff_y, u + 1)
                    f(gh[:, u, :], fy[:, u % 2, :], ACT.Copy).then_inc(ff_hi, 1)
            for i in range(COUNT["fd"]):
                high_part(U0["fd"] + i + AHEAD)
            squares("post_ffn", z, lambda c: evacuated(act, JOB["fd", 2 * c + 1]))
            deviation("post_ffn", D, eps_rms)

        @block.vector
        def _(dve):
            v = nc.vector
            chain = Chain(dve, dve_step)
            link = chain.link

            def two(t, c):
                return t[:, 2 * c:2 * c + 2, :]

            def over(row, n=2):
                return row[:, None, :].broadcast_to([P, n, S])

            def psum(j, g=None):
                filled(dve, j, g)
                return lin[j % RING]

            def read_out(ins, j):
                ins.then_inc(evac[j % RING], 1)

            def low(event, src, c):
                dve.wait_ge(split_hi, SPLIT[event] + c + 1)
                v.tensor_tensor(two(xl, c), two(src, c), two(xh, c).bitcast(f32), ALU.subtract).then_inc(split_lo, 1)

            def inverse(name, n=2):
                evacuated(dve, JOB[name + "_sq", 0])
                v.reciprocal(inv[:, 0:n], dev[:, 0:n]).then_inc(inv_ready, 1)

            def center(name, t, width, n=4):
                j = JOB[name + "_mean", 0]
                p = psum(j)
                for c in range(n):
                    ins = v.scalar_tensor_tensor(out=two(t, c), in0=over(p[:, 0, :]), scalar=-1.0 / width, in1=two(t, c), op0=ALU.mult, op1=ALU.add)
                    if c < n - 1:
                        ins.then_inc(centered, 1)
                    else:
                        read_out(ins, j)

            def is_centered(name, n=4):
                dve.wait_ge(centered, CENTERED[name] + n - 1)
                evacuated(dve, JOB[name + "_mean", 0])

            def scale(name, c, src, dst, g_name, i=0):
                j = JOB[name + "_rstd", 0]
                p = psum(j)
                for m in (2 * c, 2 * c + 1):
                    ins = v.scalar_tensor_tensor(out=dst[:, m, :], in0=src[:, m, :], scalar=vcol(g_name, i + m), in1=p[:, 0, :], op0=ALU.mult, op1=ALU.mult)
                if c < 3:
                    ins.then_inc(scaled, 1)
                else:
                    read_out(ins, j)

            def layer_norm(name, layer, event, g_name, b_name):
                def bias(m):
                    return vcol(b_name, DB * layer + m)

                def low_biased(c):
                    dve.wait_ge(split_hi, SPLIT[event] + c + 1)
                    for m in (2 * c, 2 * c + 1):
                        ins = v.scalar_tensor_tensor(out=xl[:, m, :], in0=z[:, m, :], scalar=bias(m), in1=xh[:, m, :].bitcast(f32), op0=ALU.add, op1=ALU.subtract)
                    ins.then_inc(split_lo, 1)

                center(name, z, D)
                link(v.memset(zsum[:], 0.0))
                inverse(name)
                is_centered(name)
                for c in range(4):
                    scale(name, c, z, z, g_name, DB * layer)
                    if event and c:
                        low_biased(c - 1)
                if event:
                    low_biased(3)
                dve.wait_ge(scaled, SCALED[name] + 3)
                evacuated(dve, JOB[name + "_rstd", 0])
                for m in range(DB):
                    ins = v.tensor_scalar(h[:, m, :], z[:, m, :], bias(m), None, ALU.add)
                    if m % 2:
                        ins.then_inc(normed, 1)
                dve.wait_ge(normed, NORMED[name] + 4)

            def rms(name, src, dst, g_name, event):
                inverse(name)
                for c in range(4):
                    scale(name, c, src, dst, g_name)
                    if c:
                        low(event, dst, c - 1)
                low(event, dst, 3)

            def rms_residual(name, g_name):
                inverse(name)
                j = JOB[name + "_rstd", 0]
                p = psum(j)
                for c in range(4):
                    for m in (2 * c, 2 * c + 1):
                        ins = v.scalar_tensor_tensor(out=z[:, m, :], in0=z[:, m, :], scalar=vcol(g_name, m), in1=p[:, 0, :], op0=ALU.mult, op1=ALU.mult)
                        if m == DB - 1:
                            read_out(ins, j)
                            evacuated(dve, j)
                        elif m % 2:
                            link(ins)
                    v.tensor_tensor(two(h, c), two(h, c), two(z, c), ALU.add).then_inc(normed, 1)
                dve.wait_ge(normed, NORMED[name] + 4)

            def add_up(m, n, g=None):
                v.tensor_tensor(zsum[:, None, :], zsum[:, None, :], z[:, m, :] if g is not None else z[:, m:m + 1, :], ALU.add).then_inc(z_summed, 1)
                dve.wait_ge(z_summed, per(n, g, RING))

            def residual(name, norm):
                for i in range(4):
                    j = JOB[name, i]
                    read_out(v.scalar_tensor_tensor(out=two(z, i), in0=two(h, i), scalar=ALPHA, in1=psum(j)[:], op0=ALU.mult, op1=ALU.add), j)
                    evacuated(dve, j)
                    for m in (2 * i, 2 * i + 1):
                        add_up(m, SUMMED[norm] + m + 1)

            def att_neg(u):
                k, i, t = UNITS_ATT[u]
                dve.wait_ge(lg_ready, u + 1)
                if u >= 2:
                    dve.wait_ge(exp_done, u - 1)
                for m in range(2):
                    w = att_keys(u, m)
                    if k == "A":
                        mask = selbias[:, m, 0:w]
                    elif k == "X":
                        mask = const("zero").broadcast_to([P, S])
                    else:
                        mask = const("chunk" if k == "D" else "causal", P * (1 - (m if t is None else t)), S)
                    last = v.tensor_tensor_reduce(out=lg[u % 2][:, m, 0:w], in0=att_scores(u, m), in1=mask, scale=-(128 if k == "X" else 64) ** -0.5,
                                                  scalar=3.0e38, op0=ALU.add, op1=ALU.min, accum_out=nmax[:, u % 2, m:m + 1])
                last.then_inc(neg_ready, 1)

            def att_scale(u):
                dve.wait_ge(exp_done, u + 1)
                if u:
                    dve.wait_ge(p_ready, u)
                link(v.reciprocal(rinv[:], rsum[:, u % 2, :]))
                p0, p1 = [pr[u % 2][:, m, 0:att_keys(u, m)] for m in range(2)]
                if UNITS_ATT[u][0] == "D":
                    link(v.tensor_tensor(rinv[:, 1:2], rinv[:, 1:2], lamt[:, 4:5], ALU.mult))
                    link(v.tensor_scalar(p1, p1, rinv[:, 1:2], None, ALU.mult))
                    last = v.scalar_tensor_tensor(out=p0, in0=p0, scalar=rinv[:, 0:1], in1=p1, op0=ALU.mult, op1=ALU.subtract)
                else:
                    v.tensor_scalar(p0, p0, rinv[:, 0:1], None, ALU.mult)
                    last = v.tensor_scalar(p1, p1, rinv[:, 1:2], None, ALU.mult)
                last.then_inc(p_ready, 1)

            def att_step(s, u0, n):
                if s < n:
                    att_neg(u0 + s)
                if 1 <= s < n + 1:
                    att_scale(u0 + s - 1)

            link(v.memset(zsum[:], 0.0))
            for c in range(4):
                low("x", h, c)
            dve.wait_ge(pos_loaded, 16)
            dve.wait_ge(consts_loaded, 16)
            link(v.tensor_copy(ang[:], posi[:]))
            link(v.tensor_scalar(ang[:], ang[:], const("inv"), None, ALU.mult))
            TURN, MAGIC = 2 * np.pi, 12582912.0
            for quarter, dst in ((0.0, sinT), (0.25, cosT)):
                link(v.tensor_scalar(turns[:], ang[:], 1 / TURN, quarter, ALU.mult, ALU.add))
                link(v.tensor_scalar(turns[:], turns[:], MAGIC, None, ALU.add))
                link(v.tensor_scalar(turns[:], turns[:], MAGIC, None, ALU.subtract))
                link(v.scalar_tensor_tensor(out=dst[:], in0=turns[:], scalar=-6.28125, in1=ang[:], op0=ALU.mult, op1=ALU.add))
                link(v.scalar_tensor_tensor(out=dst[:], in0=turns[:], scalar=-(TURN - 6.28125), in1=dst[:], op0=ALU.mult, op1=ALU.add))
                link(v.tensor_scalar(dst[:], dst[:], quarter * TURN, 3.1415925, ALU.add, ALU.min))
                v.tensor_scalar(dst[:], dst[:], -3.1415925, None, ALU.max).then_inc(reduced, 1)
            dve.wait_ge(vec_loaded, 16)
            link(v.tensor_scalar(hvec[:, 0:32], vec[:, COL["b_gate_2"]:COL["b_gate_2"] + 32], 0.5, None, ALU.mult))
            link(v.tensor_scalar(hvec[:, 32:40], vec[:, COL["b_glu_2"]:COL["b_glu_2"] + 8], 0.5, None, ALU.mult))
            link(v.tensor_scalar(hvec[:, 40:41], vcol("diff_norm_2"), 0.8, None, ALU.mult))
            dve.wait_ge(trig, 2)
            link(v.tensor_scalar(cosT[:], cosT[:], const("rot"), const("norot"), ALU.mult, ALU.add))

            def rope(r, dst):
                j = JOB["rope", r]
                n = dst.shape[1]
                p = psum(j)
                read_out(v.tensor_tensor(rtmp[:, 0:n, :], p[:, 0:n, :], over(sinT, n), ALU.mult), j)
                link(v.tensor_tensor(dst, dst, over(cosT, n), ALU.mult))
                evacuated(dve, j)
                v.tensor_tensor(dst, dst, rtmp[:, 0:n, :], ALU.add).then_inc(roped, 1)
                dve.wait_ge(roped, r + 1)

            j = JOB["iw", 0]
            read_out(v.tensor_scalar(iw[:], psum(j)[:, :, 0:8], 8 ** -0.5, None, ALU.mult), j)
            rope(0, two(iqT, 0))
            rope(1, two(iqT, 1))
            rope(2, ikT[:])
            rope(3, kT[:])
            v.tensor_copy(kswap[0:64, :, :], kT[64:128, :, :]).then_inc(kswapped, 1)
            v.tensor_copy(kswap[64:128, :, :], kT[0:64, :, :]).then_inc(kswapped, 1)
            for i in range(6):
                evacuated(dve, JOB["idx", i])
                t, heads = (0, range(i, 8, 2)) if i < 2 else (1, [(0, 2), (4, 6), (1, 3), (5, 7)][i - 2])
                w = P * (t + 1)
                for n, hd in enumerate(heads):
                    first = i in (0, 2) and n == 0
                    ins = v.scalar_tensor_tensor(out=work[:, t, 0:w], in0=rbuf[i % 2][:, n * w:(n + 1) * w], scalar=iw[:, t, hd:hd + 1],
                                                 in1=const("causal", P * (1 - t), S) if first else work[:, t, 0:w], op0=ALU.mult, op1=ALU.add)
                    if n < len(heads) - 1:
                        link(ins)
                ins.then_inc(idx_acc, 1)
                dve.wait_ge(idx_acc, i + 1)
            for t in range(2):
                w = P * (t + 1)
                for _ in range(TOPK // 8):
                    link(v.max(top8[:], work[:, t, 0:w]))
                    link(v.match_replace(work[:, t, 0:w], top8[:], work[:, t, 0:w], TAKEN))
                link(v.tensor_scalar(selbias[:, t, 0:w], work[:, t, 0:w], TAKEN, NEG, ALU.not_equal, ALU.mult))
                link(v.tensor_tensor(selbias[:, t, 0:w], selbias[:, t, 0:w], const("causal", P * (1 - t), S), ALU.add))
            for i in range(4):
                rope(4 + i, two(qT, i))
            for s in range(16 + 1):
                att_step(s, ATT0["A"], 16)
            for c in range(4):
                low("ao", qT, c)
            residual("ao", "ln0")
            layer_norm("ln0", 0, "mlp0", "ln_mix_g", "ln_mix_b")

            def mlp(layer):
                for half in range(2):
                    up, dn = f"up{layer}{half}", f"dn{layer}{half}"
                    base = 8 * (2 * layer + half)
                    with dve.Fori(0, 2) as g:
                        for i in range(RING):
                            evacuated(dve, JOB[up, i], g)
                            v.tensor_tensor(sqr[i % 2][:], relu[i % 2][:], relu[i % 2][:], ALU.mult).then_inc(sqr_done, 1)
                            dve.wait_ge(fhi, per(base + i + 1, g, RING))
                            at = bass.ds(g * 8 + 2 * i, 2)
                            v.tensor_tensor(fl[:, at, :], sqr[i % 2][:], fh[:, at, :].bitcast(f32), ALU.subtract).then_inc(flo, 1)
                    with dve.Fori(0, 2) as g:
                        for i in range(RING):
                            j = JOB[dn, i]
                            p = psum(j, g)
                            m = bass.ds(g * 4 + i, 1)
                            if half == 0:
                                ins = v.scalar_tensor_tensor(out=z[:, m, :], in0=h[:, m, :], scalar=ALPHA, in1=p[:, 0:1, :], op0=ALU.mult, op1=ALU.add)
                            else:
                                ins = v.tensor_tensor(z[:, m, :], z[:, m, :], p[:, 0:1, :], ALU.add)
                            read_out(ins, j)
                            if half:
                                evacuated(dve, j, g)
                                add_up(m, SUMMED[f"ln{2 * layer + 1}"] + i + 1, g)
                layer_norm(f"ln{2 * layer + 1}", layer, "gla" if layer == 0 else None, "ln_mlp_g", "ln_mlp_b")

            mlp(0)

            for i in range(2):
                j = JOB["gate_a", i]
                p = psum(j)
                for n in range(2):
                    ins = v.tensor_scalar(gtmp[:, 2 * i + n, :], p[:, n, :], vcol("b_b_a", 2 * i + n), None, ALU.add)
                read_out(ins, j)
            evacuated(dve, JOB["gate_a", 0])
            evacuated(dve, JOB["gate_a", 1])
            dve.wait_ge(softplus, 1)
            link(v.tensor_scalar(gtmp[:], gtmp[:], 0.0, None, ALU.min))
            link(v.tensor_tensor(gtmp[:], gtmp[:], decay[:], ALU.subtract))
            for hd in range(4):
                ins = v.tensor_tensor_scan(out=bcum[:, hd, :], data0=const("scan"), data1=gtmp[:, hd, :], initial=0.0, op0=ALU.mult, op1=ALU.add)
                link(ins)
            flat_b = bcum[:].rearrange("p a s -> p (a s)")
            flat_t = gtmp[:].rearrange("p a s -> p (a s)")
            masked = z[:, 0:2, :].rearrange("p a (b s) -> p (a b) s", s=64)

            def level_args(l):
                half = 32 >> l
                if l:
                    dve.wait_ge(lvl_exp, l)
                b = flat_b.rearrange("p (n w) -> p n w", w=2 * half)
                v.tensor_tensor(flat_t.rearrange("p (n w) -> p n w", w=2 * half), b,
                                b[:, :, half - 1:half].broadcast_to([P, 4 * S // (2 * half), 2 * half]), ALU.subtract).then_inc(lvl_arg, 1)

            def level_pairs(l):
                dve.wait_ge(lvl_exp, l + 1)
                if l:
                    filled(dve, JOB["level", l - 1])
                v.tensor_tensor(qk[:, 0:4, :], gqT[:], decay[:], ALU.mult)
                v.tensor_tensor(qk[:, 4:8, :], gkT[:], decay[:], ALU.mult).then_inc(lvl_qk, 1)

            def level_sum(l):
                j = JOB["level", l]
                p = psum(j)[:].rearrange("p a (b s) -> p (a b) s", s=64)
                mask = const("level", 64 * l, 64 * l + 64)[:, None, :].broadcast_to([P, 8, 64])
                if l == 0:
                    read_out(v.tensor_tensor(attnT[:], p, mask, ALU.mult), j)
                    evacuated(dve, j)
                    return
                read_out(v.tensor_tensor(masked, p, mask, ALU.mult), j)
                evacuated(dve, j)
                v.tensor_tensor(attnT[:], attnT[:], masked, ALU.add).then_inc(attn_acc, 1)
                dve.wait_ge(attn_acc, l)

            def gr_silu(i):
                j = JOB["gr", i]
                dve.wait_ge(gr_tanh, i + 1)
                read_out(v.scalar_tensor_tensor(out=two(rgate, i), in0=two(rgate, i), scalar=1.0, in1=lin[j % RING][:], op0=ALU.add, op1=ALU.mult), j)

            level_args(0)
            for i in range(2):
                evacuated(dve, JOB["gq", i])
                evacuated(dve, JOB["gk", i])
            for l in range(6):
                level_pairs(l)
                if l < 5:
                    level_args(l + 1)
                if l in GLA_FILL and GLA_FILL[l][0] == "gr":
                    gr_silu(GLA_FILL[l][1])
                if l:
                    level_sum(l - 1)
            level_sum(5)
            b = flat_b.rearrange("p (n w) -> p n w", w=64)
            v.tensor_tensor(flat_t.rearrange("p (n w) -> p n w", w=64), b, b[:, :, 63:64].broadcast_to([P, 16, 64]), ALU.subtract).then_inc(lvl_arg, 1)
            level_sum(6)
            dve.wait_ge(lvl_exp, 8)
            v.tensor_tensor(qk[:, 4:8, :], gkT[:], gtmp[:], ALU.mult).then_inc(kd_ready, 1)
            v.tensor_tensor(gqT[:], gqT[:], decay[:], ALU.mult).then_inc(q_decayed, 1)
            for c in range(3):
                for i in range(2):
                    j = JOB["state", 2 * c + i]
                    p = psum(j)
                    if c == 0:
                        read_out(v.tensor_copy(two(state, i), p[:]), j)
                        continue
                    evacuated(dve, JOB["state", 2 * c - 2 + i])
                    for n in range(2):
                        hd = 2 * i + n
                        ins = v.scalar_tensor_tensor(out=state[:, hd, :], in0=state[:, hd, :], scalar=decay[:, hd, c * 64 + 63:c * 64 + 64],
                                                     in1=p[:, n, :], op0=ALU.mult, op1=ALU.add)
                    read_out(ins, j)
                if c == 0:
                    gr_silu(3)
            inverse("gla", 8)
            for i in range(2):
                j = JOB["gla_rstd", i]
                p = psum(j)
                for n in range(2):
                    hd = 2 * i + n
                    for dv in range(2):
                        m = 2 * hd + dv
                        ins = v.scalar_tensor_tensor(out=qk[:, m, :], in0=qk[:, m, :], scalar=vcol("b_g_norm", dv), in1=p[:, n, :], op0=ALU.mult, op1=ALU.mult)
                    if n == 0:
                        link(ins)
                    else:
                        read_out(ins, j)
                        evacuated(dve, j)
                    v.scalar_tensor_tensor(out=two(qk, hd), in0=two(rgate, hd), scalar=0.5, in1=two(qk, hd), op0=ALU.mult, op1=ALU.mult).then_inc(gla_y, 1)
            for c in range(4):
                low("go", qk, c)
            residual("go", "ln2")
            layer_norm("ln2", 1, "mlp1", "ln_mix_g", "ln_mix_b")
            mlp(1)

            rms("pre_mix", h, z, "norm_mix_pre_2", "mix")
            dve.wait_ge(mix_loaded, 48)
            for i in range(2):
                v.tensor_tensor_reduce(out=pr[0][:, i, 0:64], in0=lamv[:, 2 * i, :], in1=lamv[:, 2 * i + 1, :], scale=1.0, scalar=0.0,
                                       op0=ALU.mult, op1=ALU.add, accum_out=lamt[:, i:i + 1]).then_inc(lam_dot, 1)
            link(v.memset(upad[:, :, 0:CPAD], 0.0))
            link(v.memset(scpad[:, :, 0:2], 0.0))
            j = JOB["fg", 0]
            read_out(v.tensor_scalar(fgt[:], psum(j)[0:8, 0, :], bfg[:], None, ALU.add), j)
            dve.wait_ge(fg_soft, 1)
            link(v.tensor_scalar(fgt[:], fgt[:], 0.0, None, ALU.min))
            link(v.tensor_tensor(fgt[:], fgt[:], fc[:], ALU.subtract))
            link(v.tensor_tensor_scan(out=fc[:], data0=const("ones")[0:8, :], data1=fgt[:], initial=0.0, op0=ALU.mult, op1=ALU.add))
            v.tensor_scalar(fc[:], fc[:], -8.0, None, ALU.mult).then_inc(fc_ready, 1)
            dve.wait_ge(lam_exp, 1)
            link(v.tensor_tensor(lamt[:, 4:5], lamt[:, 2:3], lamt[:, 3:4], ALU.subtract))
            link(v.tensor_scalar(lamt[:, 4:5], lamt[:, 4:5], 0.8 - 0.6, None, ALU.add))

            def conv_taps(n0, n1):
                for n in range(n0, min(n1, 4 * CONV_K)):
                    k, b = n // 4, n % 4
                    x, w = upad[:, b, k:k + S], vcol("conv_dw_2", 4 * k + b)
                    if k == 0:
                        ins = v.tensor_scalar(conv[:, b, :], x, w, vcol("conv_dw_b_2", b), ALU.mult, ALU.add)
                    else:
                        ins = v.scalar_tensor_tensor(out=conv[:, b, :], in0=x, scalar=w, in1=conv[:, b, :], op0=ALU.mult, op1=ALU.add)
                    if n == 4 * CONV_K - 1:
                        ins.then_inc(conv_done, 1)
                    else:
                        link(ins)

            def short_conv(i):
                evacuated(dve, JOB["s", 3 * i + 2])
                evacuated(dve, JOB["s", 3 * i + 1])
                for m in range(2):
                    b = 2 * i + m
                    acc = mtmp[1][:, m, :]
                    link(v.tensor_scalar(acc, scpad[:, m, 0:S], vcol("sc_w_2", b), None, ALU.mult))
                    for k in (1, 2):
                        link(v.scalar_tensor_tensor(out=acc, in0=scpad[:, m, k:k + S], scalar=vcol("sc_w_2", 4 * k + b), in1=acc, op0=ALU.mult, op1=ALU.add))
                v.tensor_tensor(two(sgate, i), two(sgate, i), mtmp[1][:], ALU.mult).then_inc(b_y, 1)

            def branch_low(n, src):
                for c in range(2):
                    dve.wait_ge(b_hi, 2 * n + c + 1)
                    v.tensor_tensor(two(blo, c), two(src, c), two(bhi, c).bitcast(f32), ALU.subtract).then_inc(b_lo, 1)

            def branch_sum(n, b, i):
                for c in (2 * i, 2 * i + 1):
                    j = JOB[f"br{b}", 0] + c
                    t = mtmp[c % 2]
                    read_out(v.scalar_tensor_tensor(out=t[:], in0=two(gate, c), scalar=1.0, in1=psum(j)[:], op0=ALU.add, op1=ALU.mult), j)
                    evacuated(dve, j)
                    if n == 0:
                        ins = v.tensor_scalar(two(z, c), t[:], 0.5, None, ALU.mult)
                    else:
                        ins = v.scalar_tensor_tensor(out=two(z, c), in0=t[:], scalar=0.5, in1=two(z, c), op0=ALU.mult, op1=ALU.add)
                    ins.then_inc(mixed, 1)
                    dve.wait_ge(mixed, 4 * n + c + 1)

            TAPS = 8
            for s in range(10):
                if s < 4 and s % 2:
                    j = JOB["c", s]
                    evacuated(dve, JOB["c", s - 1])
                    link(v.tensor_scalar(mtmp[0][:], mtmp[0][:], 0.5, 0.5, ALU.mult, ALU.add))
                    p = psum(j)
                    for m in range(2):
                        b = s - 1 + m
                        ins = v.scalar_tensor_tensor(out=upad[:, b, CPAD:], in0=p[:, m, :], scalar=vcol("b_glu_2", b), in1=mtmp[0][:, m, :], op0=ALU.add, op1=ALU.mult)
                    read_out(ins, j)
                elif s >= 4 and (s - 4) % 3 == 1:
                    i = s - 4
                    j = JOB["s", i]
                    evacuated(dve, JOB["s", i - 1])
                    read_out(v.tensor_tensor(scpad[:, :, 2:], mtmp[1][:], psum(j)[:], ALU.mult), j)
                elif s >= 4 and (s - 4) % 3 == 2:
                    short_conv((s - 4) // 3)
                att_step(s, ATT0["D"], 16)
                if s == 4:
                    evacuated(dve, JOB["c", 1])
                    evacuated(dve, JOB["c", 3])
                if s >= 4:
                    conv_taps(TAPS * (s - 4), TAPS * (s - 3))
            att_step(10, ATT0["D"], 16)
            dve.wait_ge(o_done, 24)
            for i in range(2):
                v.tensor_tensor(two(z, i), two(aqT, i), two(aqT, i), ALU.mult).then_inc(ya_squared, 1)
            inverse("ya", 8)
            for i in range(1, 4):
                att_step(10 + i, ATT0["D"], 16)
                conv_taps(TAPS * (5 + i), TAPS * (6 + i))
                if i == 2:
                    for c in range(2):
                        j = JOB["ya_rstd", c]
                        p = psum(j)
                        for n in range(2):
                            hd = 2 * c + n
                            ins = v.scalar_tensor_tensor(out=aqT[:, hd, :], in0=aqT[:, hd, :], scalar=hvec[:, 40:41], in1=p[:, n, :], op0=ALU.mult, op1=ALU.mult)
                        read_out(ins, j)
            branch_low(0, aqT)
            for i in range(2):
                att_step(14 + i, ATT0["D"], 16)
                branch_sum(0, 0, i)
            for i in range(4):
                att_step(16 + i, ATT0["D"], 16)
                if i == 0:
                    branch_low(1, sgate)
                conv_taps(TAPS * (9 + i), TAPS * (10 + i))
            for i in range(2):
                branch_sum(1, 3, i)
            conv_taps(TAPS * 13, 4 * CONV_K)
            branch_low(2, fqT)
            center("conv", conv, 512, 2)
            inverse("conv")
            is_centered("conv", 2)
            j = JOB["conv_rstd", 0]
            p = psum(j)
            for b in range(4):
                ins = v.scalar_tensor_tensor(out=conv[:, b, :], in0=conv[:, b, :], scalar=vcol("conv_ln_g_2", b), in1=p[:, 0, :], op0=ALU.mult, op1=ALU.mult)
                if b < 3:
                    link(ins)
                else:
                    read_out(ins, j)
                    evacuated(dve, j)
            for b in range(4):
                ins = v.tensor_scalar(conv[:, b, :], conv[:, b, :], vcol("conv_ln_b_2", b), None, ALU.add)
                if b % 2:
                    ins.then_inc(conv_normed, 1)
            for c in range(2):
                dve.wait_ge(conv_tanh, c + 1)
                link(v.tensor_scalar(mtmp[c][:], mtmp[c][:], 0.5, 0.5, ALU.mult, ALU.add))
                v.tensor_tensor(two(conv, c), two(conv, c), mtmp[c][:], ALU.mult).then_inc(b_y, 1)
            dve.wait_ge(b_y, 4)
            for i in range(2):
                branch_sum(2, 1, i)
            branch_low(3, conv)
            for i in range(2):
                branch_sum(3, 2, i)
            for c in range(4):
                low("out", z, c)

            rms("mem", memT, memT, "norm_mem_2", "mem")
            rms_residual("post_mix", "norm_mix_post_2")
            rms("pre_x", h, z, "norm_x_pre_2", "xq")
            for s in range(4 + 1):
                att_step(s, ATT0["X"], 4)
            for c in range(2):
                low("xo", xqT, c)
            rms_residual("post_x", "norm_x_post_2")

            for i in range(2):
                link(v.memset(fpad[i][:, :, 0:2], 0.0))
            rms("pre_ffn", h, z, "norm_ffn_pre_2", "ffn")
            for s in range(FB + 2):
                if s < FB:
                    u = s
                    evacuated(dve, JOB["fu", u])
                    for m in range(2):
                        x, acc, b = fpad[u % 2][:, m, :], fconv[:, u % 2, m, :], FB * m + u
                        link(v.tensor_scalar(acc, x[:, 0:S], vcol("ffn_dw_2", b), vcol("ffn_dw_b_2", b), ALU.mult, ALU.add))
                        link(v.scalar_tensor_tensor(out=acc, in0=x[:, 1:1 + S], scalar=vcol("ffn_dw_2", 2 * FB + b), in1=acc, op0=ALU.mult, op1=ALU.add))
                        ins = v.scalar_tensor_tensor(out=acc, in0=x[:, 2:2 + S], scalar=vcol("ffn_dw_2", 4 * FB + b), in1=acc, op0=ALU.mult, op1=ALU.add)
                        if m == 0:
                            link(ins)
                    ins.then_inc(ff_conv, 1)
                if 1 <= s < FB + 1:
                    u = s - 1
                    dve.wait_ge(ff_tanh, u + 1)
                    if u >= 2:
                        dve.wait_ge(ff_lo, u - 1)
                    link(v.scalar_tensor_tensor(out=fy[:, u % 2, :], in0=fth[:, u % 2, :], scalar=1.0, in1=fconv[:, u % 2, 0, :], op0=ALU.add, op1=ALU.mult))
                    v.scalar_tensor_tensor(out=fy[:, u % 2, :], in0=fy[:, u % 2, :], scalar=0.5, in1=fconv[:, u % 2, 1, :], op0=ALU.mult, op1=ALU.mult).then_inc(ff_y, 1)
                if s >= 2:
                    u = s - 2
                    dve.wait_ge(ff_hi, u + 1)
                    v.tensor_tensor(gl[:, u, :], fy[:, u % 2, :], gh[:, u, :].bitcast(f32), ALU.subtract).then_inc(ff_lo, 1)
            for i in range(DB):
                j = JOB["fd", i]
                read_out(v.tensor_copy(z[:, i, :], psum(j)[:, 0, :]), j)
            rms_residual("post_ffn", "norm_ffn_post_2")


def tiles_up(w, blocks):
    out = []
    for pair in blocks:
        cols = np.concatenate([np.arange(c, c + P) for c in pair])
        kb = w.shape[0] // P
        out.append(w[:, cols].reshape(kb, P, len(pair), P).transpose(1, 2, 0, 3).reshape(P, -1))
    return out


def pairs(start, n, step=P):
    return [(start + 2 * i * step, start + (2 * i + 1) * step) for i in range(n // 2)]


def tiles_tok(w, start, n):
    return [w[:, start + i * S:start + (i + 1) * S].reshape(DB, P, S).transpose(1, 0, 2).reshape(P, -1) for i in range(n)]


def tiles_wide(w):
    return tiles_up(w, [tuple(range(i * 512, i * 512 + 512, P)) for i in range(2)])


def tiles_down(w):
    return tiles_up(w, [(i * P,) for i in range(8)])


def weight_units(i):
    a, b, w2, br = i["a_w_in"][0], i["b_w_in"][0], i["w_in_2"][0], i["w_branch_2"][0]
    wg, up, dn = i["w_gate_2"][0], i["w_up_2"][0], i["w_down_2"][0]
    g = {"iq": tiles_up(a, pairs(1536, 4)), "k": tiles_up(a, pairs(1024, 2)), "v": tiles_tok(a, 1280, 1),
         "q": tiles_up(a, pairs(0, 8)), "ao": tiles_up(i["a_w_o"][0], pairs(0, 8)),
         "gq": tiles_up(b, pairs(0, 4)), "gk": tiles_up(b, pairs(512, 4)), "gv": tiles_tok(b, 1024, 4),
         "gr": tiles_up(b, pairs(2048, 8)), "go": tiles_up(i["b_w_o"][0], pairs(0, 8)),
         "aq": tiles_up(w2, pairs(0, 4)), "ak": tiles_up(w2, pairs(512, 4)), "av": tiles_tok(w2, 1024, 2),
         "fq": tiles_up(w2, pairs(1536, 4)), "fk": tiles_up(w2, pairs(2048, 4)), "fv": tiles_tok(w2, 2560, 2)}
    c0 = 3080
    g["c"] = tiles_up(w2, [p for n in range(2) for p in (pairs(c0 + 512 + 256 * n, 2) + pairs(c0 + 256 * n, 2))])
    s0 = c0 + 1024
    g["s"] = tiles_up(w2, [p for n in range(2) for at in (1024, 0, 512) for p in pairs(s0 + at + 256 * n, 2)])
    for layer in range(2):
        for half in range(2):
            g[f"up{layer}{half}"] = tiles_up(i["mlp_w_up"][layer], pairs(2048 * half, 16))
            g[f"dn{layer}{half}"] = tiles_down(i["mlp_w_down"][layer][2048 * half:2048 * half + 2048])
    for n in range(4):
        g[f"gate{n}"] = tiles_up(wg, pairs(D * n, 8))
        g[f"br{n}"] = tiles_wide(br[n])
    g["out"] = tiles_up(i["w_out_2"][0], pairs(0, 8))
    g["xq"] = tiles_up(i["w_xq_2"][0], pairs(0, 4))
    g["xk"] = tiles_up(i["w_xkv_2"][0], pairs(0, 4))
    g["xv"] = tiles_tok(i["w_xkv_2"][0], 512, 2)
    g["xo"] = tiles_wide(i["w_xo_2"][0])
    g["fu"] = tiles_up(up, [(P * b, P * (FB + b)) for b in range(FB)])
    g["fd"] = np.split(np.concatenate(tiles_down(dn), 1), COUNT["fd"], 1)
    return np.stack([unit for name, _ in UNITS for unit in g[name]])


def by_partition(w):
    return np.ascontiguousarray(w.reshape(-1, P, w.shape[1]).transpose(1, 0, 2))


def kernel(**inputs):
    import concourse.bacc as bacc
    from concourse.bass_utils import run_bass_kernel_spmd

    i = {k: np.asarray(v) for k, v in inputs.items()}
    a, b, w2 = i["a_w_in"][0], i["b_w_in"][0], i["w_in_2"][0]
    ik = a[:, 2048:2112]
    arrays = {
        "units": weight_units(i),
        "x": by_partition(np.ascontiguousarray(i["x"][0].T)),
        "mem": by_partition(np.ascontiguousarray(i["mem_2"][0].T)),
        "pos": np.ascontiguousarray(i["positions"][0]),
        "vectors": np.ascontiguousarray(np.concatenate([i[n].reshape(-1, P) for n, _ in VECTORS]).T),
        "consts": shape_constants(),
        "narrow_a": by_partition(np.concatenate([ik, ik, a[:, 2112:2120]], 1)),
        "narrow_b": by_partition(b[:, 3072:3088]),
        "narrow_f": by_partition(w2[:, 3072:3080]),
        "w_a2": np.ascontiguousarray(i["b_w_a2"][0]),
        "b_fgt": np.ascontiguousarray(i["b_fgt_2"][0][:, None]),
        "lam": np.ascontiguousarray(np.stack([i[n + "_2"][0] for n in ("lam_q1", "lam_k1", "lam_q2", "lam_k2")])),
    }
    nc = bacc.Bacc("TRN2", target_bir_lowering=False, num_devices=1)
    args = [nc.dram_tensor(n + "_dram", v.shape, mybir.dt.from_np(v.dtype), kind="ExternalInput").ap() for n, v in arrays.items()]
    out = nc.dram_tensor("out_dram", (P, DB, S), mybir.dt.float32, kind="ExternalOutput").ap()
    build(nc, *args, out)
    r = run_bass_kernel_spmd(nc, [{n + "_dram": v for n, v in arrays.items()}], core_ids=[0])
    y = r.results[0]["out_dram"]
    return np.ascontiguousarray(y.transpose(2, 1, 0).reshape(1, S, D))
```

```python
import numpy as np
import concourse.bass as bass
from concourse import mybir
from concourse.alu_op_type import AluOpType as ALU
from contextlib import ExitStack

P = 128
S = 256
D = 1024
DB = D // P
RING = 4
UT = 16
UW = UT * P
AHEAD = 3
NEG = -1.0e30
TAKEN = -3.0e38
TOPK = min(256, S // 4)
ALPHA = 4 ** 0.25
CONV_K = 31
CPAD = CONV_K - 1
FB = 22

VECTORS = [("ln_mix_g", 16), ("ln_mix_b", 16), ("ln_mlp_g", 16), ("ln_mlp_b", 16), ("b_b_a", 4), ("b_g_norm", 2),
           ("norm_mix_pre_2", 8), ("norm_mix_post_2", 8), ("norm_x_pre_2", 8), ("norm_x_post_2", 8),
           ("norm_mem_2", 8), ("norm_ffn_pre_2", 8), ("norm_ffn_post_2", 8), ("diff_norm_2", 1), ("b_glu_2", 8),
           ("conv_dw_b_2", 4), ("conv_ln_g_2", 4), ("conv_ln_b_2", 4), ("b_gate_2", 32), ("ffn_dw_b_2", 44),
           ("conv_dw_2", 4 * CONV_K), ("sc_w_2", 12), ("ffn_dw_2", 3 * 44)]
COL = {}
for _name, _n in VECTORS:
    COL[_name] = sum(n for m, n in VECTORS[:len(COL)])
NV = sum(n for _, n in VECTORS)

UNITS = [("iq", 2), ("k", 1), ("v", 1), ("q", 4), ("ao", 4),
         ("up00", 8), ("dn00", 8), ("up01", 8), ("dn01", 8),
         ("gq", 2), ("gk", 2), ("gv", 4), ("gr", 4), ("go", 4),
         ("up10", 8), ("dn10", 8), ("up11", 8), ("dn11", 8),
         ("aq", 2), ("ak", 2), ("av", 2), ("fq", 2), ("fk", 2), ("fv", 2),
         ("c", 4), ("s", 6), ("gate0", 4), ("br0", 2), ("gate3", 4), ("br3", 2),
         ("gate1", 4), ("br1", 2), ("gate2", 4), ("br2", 2), ("out", 4),
         ("xk", 2), ("xv", 2), ("xq", 2), ("xo", 2),
         ("fu", FB), ("fd", DB * FB // UT)]
COUNT = dict(UNITS)
U0 = {}
NU = 0
for _name, _n in UNITS:
    U0[_name] = NU
    NU += _n


GLA_FILL = {1: ("gr", 0), 3: ("gr", 1)}


def plan():
    job, last, n = {}, {}, [0]

    def add(name, i=0, unit=None, banks=1):
        job[name, i] = n[0]
        n[0] += banks
        if unit:
            last[U0[unit] + i] = n[0] - 1

    def units(name, count, banks=1):
        for i in range(count):
            add(name, i, name, banks)

    def norm(name, mean=False):
        if mean:
            add(name + "_mean")
        add(name + "_sq"); add(name + "_rstd")

    units("iq", 2); add("ik"); add("iw"); add("rope", 0); add("rope", 1); add("rope", 2)
    units("k", 1); units("v", 1); add("rope", 3)
    for i in range(6):
        add("idx", i)
    units("q", 4)
    for i in range(4):
        add("rope", 4 + i)
    units("ao", 4); norm("ln0", True)
    for layer in range(2):
        for half in range(2):
            units(f"up{layer}{half}", 8); units(f"dn{layer}{half}", 8)
        norm(f"ln{2 * layer + 1}", True)
        if layer == 0:
            units("gq", 2); units("gk", 2); add("alow"); add("gate_a", 0); add("gate_a", 1)
            units("gv", 4)
            for l in range(7):
                if l in GLA_FILL:
                    add(*GLA_FILL[l], GLA_FILL[l][0])
                add("level", l)
            add("gr", 2, "gr"); add("kd", 0); add("kd", 1); add("state", 0); add("state", 1)
            for i in range(4):
                add("gla_o", i)
            add("gr", 3, "gr")
            add("gla_sq"); add("gla_rstd", 0); add("gla_rstd", 1)
            units("go", 4); norm("ln2", True)
    norm("pre_mix")
    units("aq", 2); add("fg")
    for name in ("ak", "av", "fq", "fk", "fv", "c", "s"):
        units(name, COUNT[name])
    add("gate0", 0, "gate0"); add("gate0", 1, "gate0"); add("ya_sq"); add("gate0", 2, "gate0"); add("ya_rstd", 0); add("ya_rstd", 1)
    add("gate0", 3, "gate0"); units("br0", 2, 2); units("gate3", 4); units("br3", 2, 2)
    add("gate1", 0, "gate1"); add("gate1", 1, "gate1"); add("conv_mean"); add("gate1", 2, "gate1"); add("conv_sq")
    add("gate1", 3, "gate1"); add("conv_rstd"); units("br1", 2, 2); units("gate2", 4); units("br2", 2, 2)
    add("out", 0, "out"); add("out", 1, "out"); add("mem_sq"); add("out", 2, "out"); add("mem_rstd"); add("out", 3, "out")
    add("xk", 0, "xk"); add("post_mix_sq"); add("xk", 1, "xk"); add("post_mix_rstd"); add("xv", 0, "xv"); add("pre_x_sq"); add("xv", 1, "xv"); add("pre_x_rstd"); units("xq", 2); units("xo", 2, 2)
    norm("post_x"); norm("pre_ffn")
    units("fu", FB)
    for i in range(DB):
        add("fd", i)
    for u in range(COUNT["fd"]):
        last[U0["fd"] + u] = job["fd", (UT * u + UT - 1) // FB]
    norm("post_ffn")
    return job, last


JOB, LAST = plan()

CONSTS = [("ident", P), ("ones", S), ("causal", S), ("chunk", S), ("perm", P), ("level", 7 * 64), ("scan", S),
          ("inv", 1), ("rot", 1), ("norot", 1), ("ln_eps", 1), ("rms_eps", 1), ("one", 1), ("zero", 1)]
CC = {}
for _name, _n in CONSTS:
    CC[_name] = sum(n for m, n in CONSTS[:len(CC)])
NC = sum(n for _, n in CONSTS)


def shape_constants():
    c = np.zeros((P, NC), np.float32)

    def put(name, a):
        c[:, CC[name]:CC[name] + a.shape[1]] = a

    i = np.arange(P)
    put("ident", np.eye(P))
    put("ones", np.ones((P, S)))
    put("causal", np.concatenate([np.zeros((P, P)), np.where(i[None] <= i[:, None], 0.0, NEG)], 1))
    put("chunk", np.concatenate([np.zeros((P, P)), np.where(i[None] // 64 <= i[:, None] // 64, 0.0, NEG)], 1))
    perm = np.zeros((P, P))
    for head in range(0, P, 64):
        for d in range(8):
            perm[head + d + 8, head + d] = -1.0
            perm[head + d, head + d + 8] = 1.0
    put("perm", perm)
    j, t = i[:, None] % 64, np.arange(64)[None]
    levels = []
    for l in range(6):
        half = 32 >> l
        levels.append((j // (2 * half) == t // (2 * half)) & (j // half % 2 == 0) & (t // half % 2 == 1))
    levels.append(j == t)
    put("level", np.concatenate(levels, 1).astype(np.float32))
    put("scan", np.broadcast_to((np.arange(S) % 64 != 0).astype(np.float32), (P, S)))
    rot = (i % 64 < 16).astype(np.float32)
    inv = np.float32(500000.0) ** (-np.arange(0, 16, 2, dtype=np.float32) / np.float32(16))
    put("inv", (rot * inv[i % 8])[:, None])
    put("rot", rot[:, None])
    put("norot", 1.0 - rot[:, None])
    put("ln_eps", np.full((P, 1), 1e-5))
    put("rms_eps", np.full((P, 1), 1e-6))
    put("one", np.ones((P, 1)))
    return c


def build(nc, units_d, x_d, mem_d, pos_d, vec_d, const_d, narrow_a_d, narrow_b_d, narrow_f_d, w_a2_d, b_fgt_d, lam_d, out_d):
    f32, f32r = mybir.dt.float32, mybir.dt.float32r
    i32 = mybir.dt.int32
    ACT, AX = mybir.ActivationFunctionType, mybir.AxisListType
    ctx = ExitStack()
    with ctx:
        def sem(name):
            return ctx.enter_context(nc.semaphore(name))

        def sbuf(name, shape, dt=f32, where=ctx):
            return where.enter_context(nc.sbuf_tensor(name, shape, dt))

        raw = [sbuf(f"raw{i}", [P, UW]) for i in range(RING)]
        whi = [sbuf(f"whi{i}", [P, UW], f32r) for i in range(RING)]
        wlo = [sbuf(f"wlo{i}", [P, UW], f32r) for i in range(RING)]
        h = sbuf("h", [P, DB, S])
        z = sbuf("z", [P, DB, S])
        xh = sbuf("xh", [P, DB, S], f32r)
        xl = sbuf("xl", [P, DB, S], f32r)
        consts = sbuf("consts", [P, NC])
        vec = sbuf("vec", [P, NV])
        hvec = sbuf("hvec", [P, 32 + 8 + 1])
        zsum = sbuf("zsum", [P, S])
        dev = sbuf("dev", [P, 8])
        inv = sbuf("inv", [P, 8])

        def const(name, a=0, b=None):
            n = dict(CONSTS)[name]
            return consts[:, CC[name] + a:CC[name] + (n if b is None else b)]

        def vcol(name, i=0):
            return vec[:, COL[name] + i:COL[name] + i + 1]

        ident, ones = const("ident"), const("ones", 0, P)

        lg = [sbuf(f"lg{i}", [P, 2, S]) for i in range(2)]
        pr = [sbuf(f"pr{i}", [P, 2, S]) for i in range(2)]
        pT = [sbuf(f"pT{i}", [P, 4, P]) for i in range(2)]
        nmax = sbuf("nmax", [P, 2, 2])
        rsum = sbuf("rsum", [P, 2, 2])
        rinv = sbuf("rinv", [P, 2])
        squares_of = pr + lg

        def stage(*tensors):
            with ExitStack() as own:
                return [sbuf(t[0], t[1], t[2] if len(t) > 2 else f32, own) for t in tensors]

        (narrow_a, qT, kT, kswap, v_tok, iqT, ikT, cosT, sinT, ang, turns, posi, iw, work, selbias, rbuf0, rbuf1, rtmp,
         top8) = stage(
            ("narrow_a", [P, DB, 136]), ("qT", [P, 8, S]), ("kT", [P, 2, S]), ("kswap", [P, 2, S]),
            ("v_tok", [P, 2, S]), ("iqT", [P, 4, S]), ("ikT", [P, 1, S]), ("cosT", [P, S]), ("sinT", [P, S]),
            ("ang", [P, S]), ("turns", [P, S]), ("posi", [P, S], i32), ("iw", [P, 2, 8]), ("work", [P, 2, S]),
            ("selbias", [P, 2, S]), ("rbuf0", [P, 512]), ("rbuf1", [P, 512]), ("rtmp", [P, 2, S]), ("top8", [P, 8]))
        rbuf = [rbuf0, rbuf1]
        fh, fl, relu0, relu1, sqr0, sqr1 = stage(
            ("fh", [P, 16, S], f32r), ("fl", [P, 16, S], f32r), ("relu0", [P, 2, S]), ("relu1", [P, 2, S]),
            ("sqr0", [P, 2, S]), ("sqr1", [P, 2, S]))
        relu, sqr = [relu0, relu1], [sqr0, sqr1]
        narrow_b, w_a2, alow, gqT, gkT, gv_tok, rgate, gtmp, bcum, decay, qk, attnT, state1, state2 = stage(
            ("narrow_b", [P, DB, 16]), ("w_a2", [16, 512]), ("alow", [16, S]), ("gqT", [P, 4, S]), ("gkT", [P, 4, S]),
            ("gv_tok", [P, 2, D]), ("rgate", [P, 8, S]), ("gtmp", [P, 4, S]), ("bcum", [P, 4, S]), ("decay", [P, 4, S]),
            ("qk", [P, 8, S]), ("attnT", [P, 8, 64]), ("state1", [P, 4, S]), ("state2", [P, 4, S]))
        attnD = z[:, 4:8, :].rearrange("p a (b s) -> p (a b) s", s=P)
        state = [bcum, state1, state2]
        (narrow_f, aqT, gate, fqT, fkT, fv_tok, upad, conv, scpad, sgate, mtmp0, mtmp1, bhi, blo, lamv, lamt, fgt, fc,
         bfg) = stage(
            ("narrow_f", [P, DB, 8]), ("aqT", [P, 4, S]), ("gate", [P, 8, S]), ("fqT", [P, 4, S]), ("fkT", [P, 4, S]),
            ("fv_tok", [P, 2, 512]), ("upad", [P, 4, CPAD + S]), ("conv", [P, 4, S]), ("scpad", [P, 2, 2 + S]),
            ("sgate", [P, 4, S]), ("mtmp0", [P, 2, S]), ("mtmp1", [P, 2, S]), ("bhi", [P, 4, S], f32r),
            ("blo", [P, 4, S], f32r), ("lamv", [P, 4, 64]), ("lamt", [P, 8]), ("fgt", [8, S]), ("fc", [8, S]),
            ("bfg", [8, 1]))
        akT = gate[:, 0:4, :]
        av_tok = gate[:, 4:8, :].rearrange("p (t a) s -> p t (a s)", t=2)
        mtmp = [mtmp0, mtmp1]
        memT, xkT, xv_tok, xqT = stage(
            ("memT", [P, DB, S]), ("xkT", [P, 4, S]), ("xv_tok", [P, 2, 512]), ("xqT", [P, 4, S]))
        gh, gl, fpad0, fpad1, fconv, fth, fy = stage(
            ("gh", [P, FB, S], f32r), ("gl", [P, FB, S], f32r), ("fpad0", [P, 2, 2 + S]), ("fpad1", [P, 2, 2 + S]),
            ("fconv", [P, 2, 2, S]), ("fth", [P, 2, S]), ("fy", [P, 2, S]))
        fpad = [fpad0, fpad1]

        lin = [ctx.enter_context(nc.psum_tensor(f"lin{i}", [P, 2, S], f32)) for i in range(RING)]
        att = [ctx.enter_context(nc.psum_tensor(f"att{i}", [P, 512], f32)) for i in range(4)]

        raw_full = [sem(f"raw_full{i}") for i in range(RING)]
        hi_ready = sem("hi_ready")
        lo_ready = sem("lo_ready")
        job_done = sem("job_done")
        evac = [sem(f"evac{i}") for i in range(RING)]
        x_loaded, consts_loaded, vec_loaded = sem("x_loaded"), sem("consts_loaded"), sem("vec_loaded")
        pos_loaded, narrow_a_loaded, gla_loaded = sem("pos_loaded"), sem("narrow_a_loaded"), sem("gla_loaded")
        mix_loaded, mem_loaded, out_stored = sem("mix_loaded"), sem("mem_loaded"), sem("out_stored")
        split_hi, split_lo = sem("split_hi"), sem("split_lo")
        reduced, trig = sem("reduced"), sem("trig")
        roped, kswapped = sem("roped"), sem("kswapped")
        idx_acc = sem("idx_acc")
        lg_ready, neg_ready, exp_done, p_ready = sem("lg_ready"), sem("neg_ready"), sem("exp_done"), sem("p_ready")
        pT_psum, pT_sb, pv_psum, o_done = sem("pT_psum"), sem("pT_sb"), sem("pv_psum"), sem("o_done")
        z_summed, centered, squared, normed = sem("z_summed"), sem("centered"), sem("squared"), sem("normed")
        paired, scaled, inv_ready = sem("paired"), sem("scaled"), sem("inv_ready")
        sqr_done, fhi, flo = sem("sqr_done"), sem("fhi"), sem("flo")
        softplus = sem("softplus")
        gr_tanh, lvl_arg, lvl_exp, lvl_qk, attn_acc = sem("gr_tanh"), sem("lvl_arg"), sem("lvl_exp"), sem("lvl_qk"), sem("attn_acc")
        state_psum, state_ready = sem("state_psum"), sem("state_ready")
        kd_ready, q_decayed, gla_squared, gla_y = sem("kd_ready"), sem("q_decayed"), sem("gla_squared"), sem("gla_y")
        fg_soft, fc_ready = sem("fg_soft"), sem("fc_ready")
        lam_dot, lam_exp = sem("lam_dot"), sem("lam_exp")
        ya_squared, b_y, b_hi, b_lo = sem("ya_squared"), sem("b_y"), sem("b_hi"), sem("b_lo")
        mixed, conv_done, conv_normed, conv_tanh = sem("mixed"), sem("conv_done"), sem("conv_normed"), sem("conv_tanh")
        ff_conv, ff_tanh, ff_y, ff_hi, ff_lo = sem("ff_conv"), sem("ff_tanh"), sem("ff_y"), sem("ff_hi"), sem("ff_lo")
        dve_step, act_step = sem("dve_step"), sem("act_step")

        def counts(events):
            n, out = 0, {}
            for name, k in events:
                out[name] = n
                n += k
            return out

        SPLIT = counts([(e, 4) for e in ("x", "ao", "mlp0", "gla", "go", "mlp1", "mix", "out", "mem", "xq")] + [("xo", 2), ("ffn", 4)])
        NORMED = counts([("ln0", 4), ("ln1", 4), ("ln2", 4), ("ln3", 4), ("post_mix", 4), ("post_x", 4), ("post_ffn", 4)])
        SCALED = counts([(e, 3) for e in ("ln0", "ln1", "ln2", "ln3", "pre_mix", "mem", "pre_x", "pre_ffn")])
        CENTERED = counts([(e, 3) for e in ("ln0", "ln1", "ln2", "ln3", "conv")])
        SQUARED = counts([("ln0", 4), ("ln1", 4), ("ln2", 4), ("ln3", 4), ("pre_mix", 4), ("conv", 2), ("mem", 4),
                          ("post_mix", 4), ("pre_x", 4), ("post_x", 4), ("pre_ffn", 4), ("post_ffn", 4)])
        PAIRS = {"ln0": (2, 3), "ln1": (2, 3), "ln2": (2, 3), "ln3": (2, 3), "conv": (0, 1), "mem": range(4), "post_mix": range(4),
                 "post_x": range(4), "post_ffn": range(4)}
        PAIRED = counts([(e, len(p)) for e, p in PAIRS.items()])

        INV = counts([(e, 1) for e in ("ln0", "ln1", "gla", "ln2", "ln3", "pre_mix", "ya", "conv", "mem", "post_mix", "pre_x",
                                       "post_x", "pre_ffn", "post_ffn")])
        SUMMED = {"ln0": 0, "ln1": 8, "ln2": 16, "ln3": 24}

        def per(n, g, step):
            return n if g is None else n + g * step

        def evacuated(eng, j, g=None):
            eng.wait_ge(evac[j % RING], per(j // RING + 1, g, 1))

        def filled(eng, j, g=None):
            eng.wait_ge(job_done, per(j + 1, g, RING))

        class Chain:

            def __init__(self, eng, s):
                self.eng, self.sem, self.n, self.g, self.step = eng, s, 0, None, 0

            def link(self, ins):
                ins.then_inc(self.sem, 1)
                self.n += 1
                self.eng.wait_ge(self.sem, per(self.n, self.g, self.step))

            def enter(self, g, step):
                self.g, self.step, self.first = g, step, self.n

            def leave(self, times):
                assert self.n - self.first == self.step, (self.n - self.first, self.step)
                self.n, self.g = self.first + times * self.step, None

        UNITS_ATT = [("A", i, None) for i in range(16)] + [("D", j, t) for j in range(4) for t in range(2)] \
            + [("F", i, None) for i in range(8)] + [("X", j, None) for j in range(4)]
        ATT0 = {k: [u[0] for u in UNITS_ATT].index(k) for k in "ADFX"}

        def att_keys(u, m):
            k, i, t = UNITS_ATT[u]
            return {"X": S, "D": P * ((t or 0) + 1)}.get(k, P * (m + 1))

        def att_blocks(u):
            return [(m, b) for m in range(1 if UNITS_ATT[u][0] == "D" else 2) for b in range(att_keys(u, m) // P)]

        def att_rows(u):
            k, i, t = UNITS_ATT[u]
            return slice(64 * (i % 2), 64 * (i % 2) + 64) if k in "AF" else slice(0, P)

        def att_cols(u):
            k, i, t = UNITS_ATT[u]
            return slice(P * t, P * t + P) if k == "D" else slice(0, S)

        def att_out(u):
            k, i, t = UNITS_ATT[u]
            return {"A": qT, "D": aqT, "F": fqT, "X": xqT}[k][att_rows(u), i // 2 if k in "AF" else i, att_cols(u)]

        def att_scores(u, m):
            bank, at = (m, 0) if UNITS_ATT[u][0] == "D" else (u % 2, S * m)
            return att[bank][:, at:at + att_keys(u, m)]

        def free_after(u, kinds):
            return u - 1 if u and UNITS_ATT[u][0] in kinds and UNITS_ATT[u - 1][0] in kinds else u

        block = ctx.enter_context(nc.Block())
        @block.sync
        def _(sp):
            def load(u, g=None):
                if u >= RING:
                    sp.wait_ge(lo_ready, per(u - RING + 1, g, RING))
                sp.dma_start(raw[u % RING][:], units_d[per(u, g, RING)]).then_inc(raw_full[u % RING], 16)

            load(0)
            sp.dma_start(h[:], x_d).then_inc(x_loaded, 16)
            for u in range(1, RING):
                load(u)
            with sp.Fori(0, NU // RING - 1) as g:
                for u in range(RING, 2 * RING):
                    load(u, g)
            for u in range(NU // RING * RING, NU):
                load(u)
            for c in range(4):
                sp.wait_ge(normed, NORMED["post_ffn"] + c + 1)
                sp.dma_start(out_d[:, 2 * c:2 * c + 2, :], h[:, 2 * c:2 * c + 2, :]).then_inc(out_stored, 16)
            sp.wait_ge(out_stored, 64)

        @block.gpsimd
        def _(pool):
            def low_part(u, g=None):
                pool.wait_ge(hi_ready, per(u + 1, g, RING))
                nc.gpsimd.tensor_tensor(wlo[u % RING][:], raw[u % RING][:], whi[u % RING][:].bitcast(f32), ALU.subtract).then_inc(lo_ready, 1)

            pool.wait_ge(lo_ready, 1)
            for u in range(1, RING):
                low_part(u)
            with pool.Fori(0, NU // RING - 1) as g:
                for u in range(RING, 2 * RING):
                    low_part(u, g)
            for u in range(NU // RING * RING, NU):
                low_part(u)

        @block.tensor
        def _(pe):
            mm = nc.tensor.matmul

            def bank(j, g=None):
                if j >= RING:
                    evacuated(pe, j - RING, g)
                return lin[j % RING]

            def three(out, w, a, first, last):
                mm(out, w[0], a[0], start=first, stop=False)
                mm(out, w[0], a[1], start=False, stop=False)
                return mm(out, w[1], a[0], start=False, stop=last)

            def tile(u, i, n=1):
                return (whi[u % RING][:, i * P:(i + n) * P], wlo[u % RING][:, i * P:(i + n) * P])

            def arrived(u, g=None):
                pe.wait_ge(lo_ready, per(u + 1, g, RING))

            def unit_up(u, j, g=None):
                arrived(u, g)
                o = bank(j, g)
                for m in range(2):
                    for k in range(DB):
                        last = three(o[:, m, :], tile(u, m * DB + k), (xh[:, k, :], xl[:, k, :]), k == 0, k == DB - 1)
                last.then_inc(job_done, 1)

            def unit_first(u, j, event, g=None):
                arrived(u, g)
                o = bank(j, g)
                for c in range(4):
                    have(event, c + 1)
                    for m in range(2):
                        for k in (2 * c, 2 * c + 1):
                            last = three(o[:, m, :], tile(u, m * DB + k), (xh[:, k, :], xl[:, k, :]), m == k == 0, m == 1 and k == DB - 1)
                last.then_inc(job_done, 1)

            def unit_down(u, j, first, g=None):
                arrived(u, g)
                o = bank(j, g)
                for k in range(UT):
                    if first is not None and k % 2 == 0:
                        pe.wait_ge(flo, first + k // 2 + 1)
                    last = three(o[:, 0, :], tile(u, k), (fh[:, k, :], fl[:, k, :]), k == 0, k == UT - 1)
                last.then_inc(job_done, 1)

            def unit_tok(u, j):
                arrived(u)
                o = bank(j)
                for t in range(2):
                    for k in range(DB):
                        at = slice(t * P, (t + 1) * P)
                        last = three(o[:, t, :], (xh[:, k, at], xl[:, k, at]), tile(u, 2 * k, 2), k == 0, k == DB - 1)
                last.then_inc(job_done, 1)

            def unit_wide(u, j, a):
                arrived(u)
                for b in range(2):
                    o = bank(j + b)
                    for m in range(2):
                        for k in range(4):
                            last = three(o[:, m, :], tile(u, (2 * b + m) * 4 + k), (a[0][:, k, :], a[1][:, k, :]), k == 0, k == 3)
                    last.then_inc(job_done, 1)

            def ups(name, event=None):
                for i in range(COUNT[name]):
                    if event and i == 0:
                        unit_first(U0[name], JOB[name, 0], event)
                    else:
                        unit_up(U0[name] + i, JOB[name, i])

            def have(event, n=4):
                pe.wait_ge(split_lo, SPLIT[event] + n)

            def keep_warm(n):
                for _ in range(n):
                    mm(att[0][:, 0:P], ident, ident, start=True, stop=True)

            def token_sum(o, col, block, first, last, width=P):
                flat = o[:].rearrange("p a s -> p (a s)")
                for t in range(2):
                    ins = mm(flat[:, (col + t) * width:(col + t + 1) * width], block[:, t * P:(t + 1) * P], ones[:, 0:width],
                             start=first and t == 0, stop=last and t == 1)
                return ins

            def square_sum(name, blocks=DB):
                o = bank(JOB[name + "_sq", 0])
                for c in range(blocks // 2):
                    added = c in PAIRS.get(name, ())
                    if added:
                        pe.wait_ge(paired, PAIRED[name] + PAIRS[name].index(c) + 1)
                    else:
                        pe.wait_ge(squared, SQUARED[name] + c + 1)
                    for n in range(1 if added else 2):
                        last = token_sum(o, 0, squares_of[c][:, n, :], c == n == 0, c == blocks // 2 - 1 and (added or n == 1))
                last.then_inc(job_done, 1)

            def spread(name, i=0, heads=1):
                pe.wait_ge(inv_ready, INV[name] + 1)
                o = bank(JOB[name + "_rstd", i])
                for n in range(heads):
                    for t in range(2):
                        col = 2 * (i * heads + n) + t
                        last = mm(o[:, n, t * P:(t + 1) * P], inv[:, col:col + 1].broadcast_to([P, P]), ident, start=True, stop=True)
                last.then_inc(job_done, 1)

            def norm(name, idle=6):
                keep_warm(idle)
                square_sum(name)
                keep_warm(4)
                spread(name)
                keep_warm(11)

            def layer_norm(name):
                keep_warm(5)
                pe.wait_ge(z_summed, SUMMED[name] + DB)
                mm(bank(JOB[name + "_mean", 0])[:, 0, :], ones, zsum[:], start=True, stop=True).then_inc(job_done, 1)
                norm(name)

            def att_logits(u):
                k, i, t = UNITS_ATT[u]
                if free_after(u, "AFX"):
                    pe.wait_ge(neg_ready, free_after(u, "AFX"))
                for m in range(2):
                    o = att_scores(u, m)
                    w = att_keys(u, m)
                    q = slice((m if t is None else t) * P, (m if t is None else t) * P + P)
                    r = att_rows(u)
                    if k == "A":
                        pe.wait_ge(roped, 5 + i // 4)
                        keys = kT if i // 4 % 2 == i % 2 else kswap
                        last = mm(o, qT[r, i // 2, q], keys[r, i // 8, 0:w], start=True, stop=True)
                    elif k == "D":
                        r = slice(64 * m, 64 * m + 64)
                        last = mm(o, aqT[r, i, q], akT[r, i, 0:w], start=True, stop=True)
                    elif k == "F":
                        mm(o, fqT[r, i // 2, q], fkT[r, i // 2, 0:w], start=True, stop=False)
                        last = mm(o, ident[0:8, i:i + 1].broadcast_to([8, P]), fc[:, 0:w], start=False, stop=True)
                    else:
                        last = mm(o, xqT[:, i, q], xkT[:, i, :], start=True, stop=True)
                last.then_inc(lg_ready, 1)

            def att_transpose(u):
                pe.wait_ge(p_ready, u + 1)
                if u:
                    pe.wait_ge(pT_sb, u)
                for n, (m, b) in enumerate(att_blocks(u)):
                    last = nc.tensor.transpose(att[2][:, n * P:(n + 1) * P], pr[u % 2][:, m, b * P:(b + 1) * P], ident)
                last.then_inc(pT_psum, 1)

            def att_values(u):
                k, i, t = UNITS_ATT[u]
                pe.wait_ge(pT_sb, u + 1)
                if free_after(u, "AF"):
                    pe.wait_ge(o_done, free_after(u, "AF"))
                for n, (m, b) in enumerate(att_blocks(u)):
                    o = att[3][att_rows(u), m * P:(m + 1) * P]
                    if k == "A":
                        v = v_tok[:, b, 64 * (i // 4):64 * (i // 4) + 64]
                    elif k == "F":
                        v = fv_tok[:, b, 64 * i:64 * i + 64]
                    else:
                        v = (av_tok if k == "D" else xv_tok)[:, b, i * P:(i + 1) * P]
                    last = mm(o, v, pT[u % 2][:, n, :], start=b == 0, stop=b == att_keys(u, m) // P - 1)
                last.then_inc(pv_psum, 1)

            def att_step(s, u0, n):
                if s < n:
                    att_logits(u0 + s)
                if 2 <= s < n + 2:
                    att_transpose(u0 + s - 2)
                if 3 <= s < n + 3:
                    att_values(u0 + s - 3)

            ups("iq", "x")
            pe.wait_ge(consts_loaded, 16)
            pe.wait_ge(narrow_a_loaded, 16)
            o = bank(JOB["ik", 0])
            for k in range(DB):
                last = mm(o[:, 0, :], narrow_a[:, k, 0:P], h[:, k, :], start=k == 0, stop=k == DB - 1)
            last.then_inc(job_done, 1)
            o = bank(JOB["iw", 0])
            for t in range(2):
                for k in range(DB):
                    last = mm(o[:, t, 0:8], h[:, k, t * P:(t + 1) * P], narrow_a[:, k, P:P + 8], start=k == 0, stop=k == DB - 1)
            last.then_inc(job_done, 1)

            def rope(r, raw_jobs, src):
                for j in raw_jobs:
                    evacuated(pe, j)
                o = bank(JOB["rope", r])
                n = src.shape[1]
                mm(o[:, 0:n, :], const("perm"), src, start=True, stop=True).then_inc(job_done, 1)

            rope(0, [JOB["iq", 0]], iqT[:, 0:2, :])
            rope(1, [JOB["iq", 1]], iqT[:, 2:4, :])
            rope(2, [JOB["ik", 0]], ikT[:])
            ups("k")
            unit_tok(U0["v"], JOB["v", 0])
            rope(3, [JOB["k", 0]], kT[:])
            pe.wait_ge(roped, 3)
            for i in range(6):
                o = bank(JOB["idx", i])
                t, heads = (0, range(i, 8, 2)) if i < 2 else (1, [(0, 2), (4, 6), (1, 3), (5, 7)][i - 2])
                w = P * (t + 1)
                for n, hd in enumerate(heads):
                    r = slice(64 * (hd % 2), 64 * (hd % 2) + 64)
                    last = mm(o[:].rearrange("p a s -> p (a s)")[:, n * w:(n + 1) * w], iqT[r, hd // 2, t * P:(t + 1) * P], ikT[r, 0, 0:w], start=True, stop=True)
                last.then_inc(job_done, 1)
            ups("q")
            for i in range(4):
                rope(4 + i, [JOB["q", i]], qT[:, 2 * i:2 * i + 2, :])
            pe.wait_ge(kswapped, 2)
            evacuated(pe, JOB["v", 0])
            for s in range(16 + 3):
                att_step(s, ATT0["A"], 16)
            keep_warm(9)
            ups("ao", "ao")

            layer_norm("ln0")

            def mlp(layer):
                for half in range(2):
                    up, dn = f"up{layer}{half}", f"dn{layer}{half}"
                    with pe.Fori(0, 2) as g:
                        for i in range(RING):
                            if half == i == 0:
                                unit_first(U0[up], JOB[up, 0], f"mlp{layer}", g)
                            else:
                                unit_up(U0[up] + i, JOB[up, i], g)
                    with pe.Fori(0, 2) as g:
                        for i in range(RING):
                            unit_down(U0[dn] + i, JOB[dn, i], None if i else 8 * (2 * layer + half), g)
                layer_norm(f"ln{2 * layer + 1}")

            mlp(0)

            ups("gq", "gla")
            ups("gk")
            pe.wait_ge(gla_loaded, 32)
            pe.wait_ge(normed, NORMED["ln1"] + 4)
            o = bank(JOB["alow", 0])
            for k in range(DB):
                last = mm(o[0:16, 0, :], narrow_b[:, k, :], h[:, k, :], start=k == 0, stop=k == DB - 1)
            last.then_inc(job_done, 1)
            evacuated(pe, JOB["alow", 0])
            for i in range(2):
                o = bank(JOB["gate_a", i])
                for n in range(2):
                    hd = 2 * i + n
                    last = mm(o[:, n, :], w_a2[:, hd * P:(hd + 1) * P], alow[:], start=True, stop=True)
                last.then_inc(job_done, 1)
            for i in range(4):
                unit_tok(U0["gv"] + i, JOB["gv", i])

            def level(l):
                if l < 6:
                    pe.wait_ge(lvl_qk, l + 1)
                o = bank(JOB["level", l])[:].rearrange("p a (b s) -> p (a b) s", s=64)
                for hd in range(4):
                    for c in range(4):
                        at = slice(c * 64, c * 64 + 64)
                        both = qk[:, 4 * (l % 2) + hd, at]
                        keys, queries = (both, both) if l < 6 else (gkT[:, hd, at], gqT[:, hd, at])
                        last = mm(o[64 * (c % 2):64 * (c % 2) + 64, hd * 2 + c // 2, :], keys, queries, start=True, stop=True)
                last.then_inc(job_done, 1)

            for l in range(7):
                if l in GLA_FILL:
                    name, i = GLA_FILL[l]
                    unit_up(U0[name] + i, JOB[name, i])
                level(l)
            unit_up(U0["gr"] + 2, JOB["gr", 2])
            pe.wait_ge(kd_ready, 1)
            for t in range(2):
                o = bank(JOB["kd", t])[:].rearrange("p a s -> p (a s)")
                for hd in range(4):
                    last = nc.tensor.transpose(o[:, hd * P:(hd + 1) * P], qk[:, hd, t * P:(t + 1) * P], ident)
                last.then_inc(job_done, 1)
            kd_tok = gtmp[:].rearrange("p (t a) s -> p t (a s)", t=2)
            keep_warm(5)
            pe.wait_ge(attn_acc, 7)
            pe.wait_ge(q_decayed, 1)
            for t in range(2):
                evacuated(pe, JOB["kd", t])
            for i in range(4):
                evacuated(pe, JOB["gv", i])
            for c in range(3):
                t, r = c // 2, slice(64 * (c % 2), 64 * (c % 2) + 64)
                for i in range(2):
                    o = bank(JOB["state", i]) if c == 0 else att[2 * c - 2 + i][:].rearrange("p (a s) -> p a s", s=S)
                    for n in range(2):
                        hd = 2 * i + n
                        last = mm(o[:, n, :], kd_tok[r, t, hd * P:(hd + 1) * P], gv_tok[r, t, hd * S:(hd + 1) * S], start=True, stop=True)
                    last.then_inc(state_psum if c else job_done, 1)
            for t in range(2):
                for i in range(2):
                    o = bank(JOB["gla_o", 2 * t + i])[:].rearrange("p a (b s) -> p (a b) s", s=P)
                    if t == 0:
                        evacuated(pe, JOB["state", i])
                    else:
                        pe.wait_ge(state_ready, 2 + i + 1)
                    for n in range(2):
                        hd = 2 * i + n
                        for dv in range(2):
                            at = slice(hd * S + dv * P, hd * S + dv * P + P)
                            mm(o[:, 2 * n + dv, :], gv_tok[:, t, at], attnD[:, hd * 2 + t, :], start=True, stop=False)
                            for c in (1,) if t == 0 else (2, 3):
                                last = mm(o[:, 2 * n + dv, 64 * (c % 2):64 * (c % 2) + 64], state[c - 1][:, hd, dv * P:(dv + 1) * P],
                                          gqT[:, hd, c * 64:c * 64 + 64], start=False, stop=c != 2)
                    last.then_inc(job_done, 1)
            unit_up(U0["gr"] + 3, JOB["gr", 3])
            o = bank(JOB["gla_sq", 0])
            for hd in range(4):
                pe.wait_ge(gla_squared, hd + 1)
                for b in range(2):
                    last = token_sum(o, 2 * hd, z[:, 2 * hd + b, :], hd == b == 0, hd == 3 and b == 1, 64)
            last.then_inc(job_done, 1)
            keep_warm(3)
            for i in range(2):
                spread("gla", i, 2)
            keep_warm(9)
            ups("go", "go")
            layer_norm("ln2")
            mlp(1)

            norm("pre_mix")
            ups("aq", "mix")
            pe.wait_ge(mix_loaded, 48)
            o = bank(JOB["fg", 0])
            for k in range(DB):
                last = mm(o[0:8, 0, :], narrow_f[:, k, :], z[:, k, :], start=k == 0, stop=k == DB - 1)
            last.then_inc(job_done, 1)
            ups("ak")
            for i in range(2):
                unit_tok(U0["av"] + i, JOB["av", i])
            for name in ("fq", "fk"):
                ups(name)
            for i in range(2):
                unit_tok(U0["fv"] + i, JOB["fv", i])
            fill = [("c", i) for i in range(4)] + [("s", i) for i in range(6)]
            for s, (name, i) in enumerate(fill):
                unit_up(U0[name] + i, JOB[name, i])
                if s == 0:
                    pe.wait_ge(fc_ready, 1)
                    for n in range(2):
                        for name in ("aq", "ak", "av", "fq", "fk", "fv"):
                            evacuated(pe, JOB[name, n])
                att_step(s, ATT0["D"], 16)
            unit_up(U0["gate0"], JOB["gate0", 0])
            att_step(10, ATT0["D"], 16)
            for i in range(1, 4):
                unit_up(U0["gate0"] + i, JOB["gate0", i])
                att_step(10 + i, ATT0["D"], 16)
                if i == 1:
                    pe.wait_ge(ya_squared, 2)
                    o = bank(JOB["ya_sq", 0])
                    for hd in range(4):
                        last = token_sum(o, 2 * hd, z[:, hd, :], hd == 0, hd == 3, 64)
                    last.then_inc(job_done, 1)
                elif i == 2:
                    spread("ya", 0, 2)
                    spread("ya", 1, 2)

            def branch(n, b, i):
                if i == 0:
                    pe.wait_ge(b_lo, 2 * n + 2)
                unit_wide(U0[f"br{b}"] + i, JOB[f"br{b}", i], (bhi, blo))

            for i in range(2):
                branch(0, 0, i)
                att_step(14 + i, ATT0["D"], 16)
            for i in range(4):
                unit_up(U0["gate3"] + i, JOB["gate3", i])
                att_step(16 + i, ATT0["D"], 16)
            for i in range(2):
                branch(1, 3, i)
            for i in range(4):
                unit_up(U0["gate1"] + i, JOB["gate1", i])
                if i == 1:
                    o = bank(JOB["conv_mean", 0])
                    pe.wait_ge(conv_done, 1)
                    for m in range(4):
                        last = mm(o[:, 0, :], ones, conv[:, m, :], start=m == 0, stop=m == 3)
                    last.then_inc(job_done, 1)
                elif i == 2:
                    square_sum("conv", 4)
                elif i == 3:
                    spread("conv")
            for i in range(2):
                branch(2, 1, i)
            ups("gate2")
            for i in range(2):
                branch(3, 2, i)
            for i in range(4):
                if i == 0:
                    unit_first(U0["out"], JOB["out", 0], "out")
                else:
                    unit_up(U0["out"] + i, JOB["out", i])
                if i == 1:
                    square_sum("mem")
                elif i == 2:
                    spread("mem")

            keep_warm(10)
            unit_first(U0["xk"], JOB["xk", 0], "mem")
            square_sum("post_mix")
            unit_up(U0["xk"] + 1, JOB["xk", 1])
            spread("post_mix")
            unit_tok(U0["xv"], JOB["xv", 0])
            square_sum("pre_x")
            unit_tok(U0["xv"] + 1, JOB["xv", 1])
            spread("pre_x")
            keep_warm(12)
            unit_first(U0["xq"], JOB["xq", 0], "xq")
            for i in range(2):
                for name in ("xk", "xv"):
                    evacuated(pe, JOB[name, i])
            evacuated(pe, JOB["xq", 0])
            att_step(0, ATT0["X"], 4)
            unit_up(U0["xq"] + 1, JOB["xq", 1])
            evacuated(pe, JOB["xq", 1])
            for s in range(1, 4 + 3):
                att_step(s, ATT0["X"], 4)
            keep_warm(8)
            arrived(U0["xo"])
            banks = [bank(JOB["xo", 0] + b) for b in range(2)]
            for c in range(2):
                have("xo", c + 1)
                for b in range(2):
                    for m in range(2):
                        for k in (2 * c, 2 * c + 1):
                            last = three(banks[b][:, m, :], tile(U0["xo"], (2 * b + m) * 4 + k), (xh[:, k, :], xl[:, k, :]), m == k == 0, m == 1 and k == 3)
                    if c:
                        last.then_inc(job_done, 1)
            unit_wide(U0["xo"] + 1, JOB["xo", 1], (xh, xl))
            norm("post_x", 0)

            norm("pre_ffn")
            unit_first(U0["fu"], JOB["fu", 0], "ffn")
            unit_up(U0["fu"] + 1, JOB["fu", 1])
            with pe.Fori(0, (FB - 2) // RING) as g:
                for i in range(2, 2 + RING):
                    unit_up(U0["fu"] + i, JOB["fu", i], g)
            for n in range(DB * FB):
                i, k = divmod(n, FB)
                if n % UT == 0:
                    arrived(U0["fd"] + n // UT)
                if k == 0:
                    o = bank(JOB["fd", i])
                if i == 0:
                    pe.wait_ge(ff_lo, k + 1)
                last = three(o[:, 0, :], tile(U0["fd"] + n // UT, n % UT), (gh[:, k, :], gl[:, k, :]), k == 0, k == FB - 1)
                if k == FB - 1:
                    last.then_inc(job_done, 1)
            norm("post_ffn", 0)

        @block.scalar
        def _(act):
            f = nc.scalar.activation
            chain = Chain(act, act_step)
            eps_ln, eps_rms, one = const("ln_eps"), const("rms_eps"), const("one")

            def two(t, c):
                return t[:, 2 * c:2 * c + 2, :]

            def high_part(u, g=None, used=None):
                if u >= NU:
                    return
                act.wait_ge(raw_full[u % RING], per(16 * (u // RING + 1), g, 16))
                if u >= RING:
                    act.wait_ge(job_done, per(LAST[u - RING] + 1 if used is None else used, g, RING))
                f(whi[u % RING][:], raw[u % RING][:], ACT.Copy).then_inc(hi_ready, 1)

            def unit(name, i):
                high_part(U0[name] + i + AHEAD)
                filled(act, JOB[name, i])

            def passed(name):
                for i in range(COUNT[name]):
                    high_part(U0[name] + i + AHEAD)

            def copy(name, i, dst, scale=1.0):
                unit(name, i)
                j = JOB[name, i]
                f(dst, lin[j % RING][:], ACT.Copy, scale=scale).then_inc(evac[j % RING], 1)

            def split(event, src, ready, n=4):
                for c in range(n):
                    ready(c)
                    f(two(xh, c), two(src, c), ACT.Copy).then_inc(split_hi, 1)

            def squares(name, src, ready, n=4, bias=None):
                for c in range(n):
                    ready(c)
                    if bias is None:
                        last = f(squares_of[c][:], two(src, c), ACT.Square)
                    else:
                        for m in range(2):
                            last = f(squares_of[c][:, m, :], src[:, 2 * c + m, :], ACT.Square, bias=bias(2 * c + m))
                    last.then_inc(squared, 1)

            def deviation(name, over, eps, n=2):
                width = P if n == 2 else 64
                j = JOB[name + "_sq", 0]
                filled(act, j)
                if INV[name]:
                    act.wait_ge(inv_ready, INV[name])
                sums = lin[j % RING][:].rearrange("p a s -> p (a s)")[:, 0:n * width].rearrange("p (n w) -> p n w", w=width)[:, :, 0]
                f(dev[:, 0:n], sums, ACT.Sqrt, scale=1.0 / over, bias=eps).then_inc(evac[j % RING], 1)

            def is_scaled(name):
                return lambda c: act.wait_ge(scaled, SCALED[name] + c + 1) if c < 3 else evacuated(act, JOB[name + "_rstd", 0])

            def is_normed(name):
                return lambda c: act.wait_ge(normed, NORMED[name] + c + 1)

            def is_centered(name, n=4):
                return lambda c: act.wait_ge(centered, CENTERED[name] + c + 1) if c < n - 1 else evacuated(act, JOB[name + "_mean", 0])

            def layer_norm(name, event, bias):
                squares(name, z, is_centered(name))
                deviation(name, D, eps_ln)
                if event:
                    for c in range(4):
                        is_scaled(name)(c)
                        for m in (2 * c, 2 * c + 1):
                            last = f(xh[:, m, :], z[:, m, :], ACT.Identity, bias=bias(m))
                        last.then_inc(split_hi, 1)

            def att_exp(u):
                act.wait_ge(neg_ready, u + 1)
                if u >= 2:
                    act.wait_ge(pT_psum, u - 1)
                for m in range(2):
                    w = att_keys(u, m)
                    last = f(pr[u % 2][:, m, 0:w], lg[u % 2][:, m, 0:w], ACT.Exp, scale=-1.0, bias=nmax[:, u % 2, m:m + 1],
                             accum_out=rsum[:, u % 2, m:m + 1])
                last.then_inc(exp_done, 1)

            def att_transposed(u):
                act.wait_ge(pT_psum, u + 1)
                if u >= 2:
                    act.wait_ge(pv_psum, u - 1)
                n = len(att_blocks(u))
                f(pT[u % 2][:, 0:n, :], att[2][:, 0:n * P].rearrange("p (n q) -> p n q", q=P), ACT.Copy).then_inc(pT_sb, 1)

            def att_result(u):
                act.wait_ge(pv_psum, u + 1)
                n = 1 if UNITS_ATT[u][0] == "D" else 2
                f(att_out(u), att[3][att_rows(u), 0:n * P], ACT.Copy).then_inc(o_done, 1)

            def att_step(s, u0, n):
                if 2 <= s < n + 2:
                    att_transposed(u0 + s - 2)
                if s < n:
                    att_exp(u0 + s)
                if 3 <= s < n + 3:
                    att_result(u0 + s - 3)

            act.wait_ge(dve_step, 1)
            chain.link(f(dev[:], zsum[:, 0:8], ACT.Copy))
            high_part(0)
            act.dma_start(posi[:], pos_d.partition_broadcast(P)).then_inc(pos_loaded, 16)
            act.dma_start(consts[:], const_d).then_inc(consts_loaded, 16)
            split("x", h, lambda c: act.wait_ge(x_loaded, 16))
            act.dma_start(narrow_a[:], narrow_a_d).then_inc(narrow_a_loaded, 16)
            act.dma_start(vec[:], vec_d).then_inc(vec_loaded, 16)
            for u in range(1, AHEAD):
                high_part(u)
            act.wait_ge(reduced, 2)
            f(sinT[:], sinT[:], ACT.Sin).then_inc(trig, 1)
            f(cosT[:], cosT[:], ACT.Sin).then_inc(trig, 1)
            for i in range(2):
                copy("iq", i, two(iqT, i))
            j = JOB["ik", 0]
            filled(act, j)
            f(ikT[:, 0, :], lin[j % RING][:, 0, :], ACT.Copy).then_inc(evac[j % RING], 1)
            copy("k", 0, kT[:])
            copy("v", 0, v_tok[:])
            for i in range(6):
                j = JOB["idx", i]
                filled(act, j)
                if i >= 2:
                    act.wait_ge(idx_acc, i - 1)
                f(rbuf[i % 2][:], lin[j % RING][:].rearrange("p a s -> p (a s)"), ACT.Relu, scale=64 ** -0.5).then_inc(evac[j % RING], 1)
            for i in range(4):
                copy("q", i, two(qT, i))
            for s in range(16 + 3):
                att_step(s, ATT0["A"], 16)
            split("ao", qT, lambda c: act.wait_ge(o_done, 4 * c + 4))
            passed("ao")
            layer_norm("ln0", "mlp0", lambda m: vcol("ln_mix_b", m))

            def mlp(layer):
                for half in range(2):
                    up, dn = f"up{layer}{half}", f"dn{layer}{half}"
                    base = 8 * (2 * layer + half)
                    with act.Fori(0, 2) as g:
                        for i in range(RING):
                            j = JOB[up, i]
                            high_part(U0[up] + i + AHEAD, g, j)
                            filled(act, j, g)
                            f(relu[i % 2][:], lin[j % RING][:], ACT.Relu).then_inc(evac[j % RING], 1)
                            act.wait_ge(sqr_done, per(base + i + 1, g, RING))
                            f(fh[:, bass.ds(g * 8 + 2 * i, 2), :], sqr[i % 2][:], ACT.Copy).then_inc(fhi, 1)
                    with act.Fori(0, 2) as g:
                        for i in range(RING):
                            high_part(U0[dn] + i + AHEAD, g, JOB[dn, i])
                layer_norm(f"ln{2 * layer + 1}", "gla" if layer == 0 else None, lambda m: vcol("ln_mlp_b", m))

            mlp(0)

            act.dma_start(narrow_b[:], narrow_b_d).then_inc(gla_loaded, 16)
            act.dma_start(w_a2[:], w_a2_d).then_inc(gla_loaded, 16)
            for i in range(2):
                copy("gq", i, two(gqT, i), 128 ** -0.5)
            for i in range(2):
                copy("gk", i, two(gkT, i))
            j = JOB["alow", 0]
            filled(act, j)
            f(alow[:], lin[j % RING][0:16, 0, :], ACT.Copy).then_inc(evac[j % RING], 1)
            for i in range(2):
                evacuated(act, JOB["gate_a", i])
            chain.link(f(decay[:], gtmp[:], ACT.Abs))
            chain.link(f(decay[:], decay[:], ACT.Exp, scale=-1.0))
            f(decay[:], decay[:], ACT.Ln, bias=one).then_inc(softplus, 1)
            def gla_fill(name, i):
                unit(name, i)
                f(two(rgate, i), lin[JOB[name, i] % RING][:], ACT.Tanh, scale=0.5).then_inc(gr_tanh, 1)

            def level_decay(l):
                act.wait_ge(lvl_arg, l + 1)
                f(decay[:], gtmp[:], ACT.Exp, scale=1.0 / 16).then_inc(lvl_exp, 1)

            for i in range(4):
                copy("gv", i, gv_tok[:, :, i * S:(i + 1) * S])
                if i == 1:
                    level_decay(0)
            for l in range(6):
                if l < 5:
                    level_decay(l + 1)
                if l in GLA_FILL:
                    gla_fill(*GLA_FILL[l])
            act.wait_ge(lvl_arg, 7)
            f(decay[:], bcum[:], ACT.Exp, scale=1.0 / 16).then_inc(lvl_exp, 1)
            f(gtmp[:], gtmp[:], ACT.Exp, scale=-1.0 / 16).then_inc(lvl_exp, 1)
            gla_fill("gr", 2)
            act.wait_ge(kd_ready, 1)
            kd_tok = gtmp[:].rearrange("p (t a) s -> p t (a s)", t=2)
            for t in range(2):
                j = JOB["kd", t]
                filled(act, j)
                f(kd_tok[:, t, :], lin[j % RING][:].rearrange("p a s -> p (a s)"), ACT.Copy).then_inc(evac[j % RING], 1)
            for t in range(2):
                for i in range(2):
                    j = JOB["gla_o", 2 * t + i]
                    filled(act, j)
                    f(qk[:, 4 * i:4 * i + 4, t * P:(t + 1) * P], lin[j % RING][:].rearrange("p a (b s) -> p (a b) s", s=P), ACT.Copy).then_inc(evac[j % RING], 1)
            for hd in range(4):
                if hd % 2 == 0:
                    evacuated(act, JOB["gla_o", 2 + hd // 2])
                if hd == 2:
                    evacuated(act, JOB["gla_o", 3])
                f(two(z, hd), two(qk, hd), ACT.Square).then_inc(gla_squared, 1)
            gla_fill("gr", 3)
            deviation("gla", S, eps_rms, 8)
            split("go", qk, lambda c: evacuated(act, JOB["gla_rstd", c // 2]) if c % 2 else act.wait_ge(gla_y, c // 2 + 1))
            passed("go")
            layer_norm("ln2", "mlp1", lambda m: vcol("ln_mix_b", DB + m))
            mlp(1)

            squares("pre_mix", z, is_scaled("ln3"), 4, lambda m: vcol("ln_mlp_b", DB + m))
            deviation("pre_mix", D, eps_rms)
            act.dma_start(narrow_f[:], narrow_f_d).then_inc(mix_loaded, 16)
            act.dma_start(lamv[:], lam_d.partition_broadcast(P)).then_inc(mix_loaded, 16)
            act.dma_start(bfg[:], b_fgt_d).then_inc(mix_loaded, 16)
            split("mix", z, is_scaled("pre_mix"))
            for i in range(2):
                copy("aq", i, two(aqT, i))
            evacuated(act, JOB["fg", 0])
            chain.link(f(fc[:], fgt[:], ACT.Abs))
            chain.link(f(fc[:], fc[:], ACT.Exp, scale=-1.0))
            f(fc[:], fc[:], ACT.Ln, bias=one[0:8, :]).then_inc(fg_soft, 1)
            act.wait_ge(lam_dot, 2)
            f(lamt[:, 2:4], lamt[:, 0:2], ACT.Exp).then_inc(lam_exp, 1)
            for i in range(2):
                copy("ak", i, two(akT, i))
            for i in range(2):
                copy("av", i, av_tok[:, :, i * S:(i + 1) * S])
            for name, dst in (("fq", fqT), ("fk", fkT)):
                for i in range(2):
                    copy(name, i, two(dst, i))
            for i in range(2):
                copy("fv", i, fv_tok[:, :, i * S:(i + 1) * S])

            def branch_split(n, src, ready):
                for c in range(2):
                    ready(c)
                    f(two(bhi, c), two(src, c), ACT.Copy).then_inc(b_hi, 1)

            def gates(b, i):
                unit(f"gate{b}", i)
                j = JOB[f"gate{b}", i]
                for m in range(2):
                    col = b * 8 + 2 * i + m
                    last = f(gate[:, 2 * i + m, :], lin[j % RING][:, m, :], ACT.Tanh, scale=0.5, bias=hvec[:, col:col + 1])
                last.then_inc(evac[j % RING], 1)

            for s in range(10):
                if s < 4:
                    unit("c", s)
                    j = JOB["c", s]
                    if s % 2 == 0:
                        if s:
                            evacuated(act, JOB["c", s - 1])
                        for m in range(2):
                            last = f(mtmp[0][:, m, :], lin[j % RING][:, m, :], ACT.Tanh, scale=0.5, bias=hvec[:, 36 + s + m:37 + s + m])
                        last.then_inc(evac[j % RING], 1)
                else:
                    i = s - 4
                    unit("s", i)
                    j = JOB["s", i]
                    if i % 3 == 0:
                        if i:
                            evacuated(act, JOB["s", i - 2])
                        f(mtmp[1][:], lin[j % RING][:], ACT.Copy).then_inc(evac[j % RING], 1)
                    elif i % 3 == 2:
                        f(two(sgate, i // 3), lin[j % RING][:], ACT.Copy).then_inc(evac[j % RING], 1)
                att_step(s, ATT0["D"], 16)
            att_step(10, ATT0["D"], 16)
            gates(0, 0)
            act.wait_ge(o_done, 24)
            for i in range(2):
                f(two(z, i), two(aqT, i), ACT.Square).then_inc(ya_squared, 1)
            for i in range(1, 4):
                if i == 3:
                    branch_split(0, aqT, lambda c: evacuated(act, JOB["ya_rstd", c]))
                gates(0, i)
                att_step(10 + i, ATT0["D"], 16)
                if i == 1:
                    deviation("ya", P, eps_rms, 8)
            for i in range(2):
                high_part(U0["br0"] + i + AHEAD)
                att_step(14 + i, ATT0["D"], 16)
            for i in range(4):
                if i < 2:
                    act.wait_ge(mixed, 2 * i + 2)
                gates(3, i)
                if i == 0:
                    branch_split(1, sgate, lambda c: act.wait_ge(b_y, c + 1))
                att_step(16 + i, ATT0["D"], 16)
            passed("br3")
            for i in range(4):
                if i < 2:
                    act.wait_ge(mixed, 4 + 2 * i + 2)
                gates(1, i)
                if i == 0:
                    branch_split(2, fqT, lambda c: act.wait_ge(o_done, 32))
                elif i == 1:
                    squares("conv", conv, is_centered("conv", 2), 2)
                elif i == 2:
                    deviation("conv", 512, eps_rms)
            for i in range(2):
                act.wait_ge(conv_normed, i + 1)
                if i == 0:
                    act.wait_ge(mixed, 8)
                f(mtmp[i][:], two(conv, i), ACT.Tanh, scale=0.5).then_inc(conv_tanh, 1)
            passed("br1")
            for i in range(4):
                if i < 2:
                    act.wait_ge(mixed, 8 + 2 * i + 2)
                gates(2, i)
                if i == 0:
                    branch_split(3, conv, lambda c: act.wait_ge(b_y, 2 + c + 1))
            passed("br2")
            split("out", z, lambda c: act.wait_ge(mixed, 12 + c + 1))
            act.dma_start(memT[:], mem_d).then_inc(mem_loaded, 16)
            for i in range(4):
                if i == 2:
                    deviation("mem", D, eps_rms)
                copy("out", i, two(z, i))
                if i == 0:
                    squares("mem", memT, lambda c: act.wait_ge(mem_loaded, 16))

            split("mem", memT, is_scaled("mem"))
            squares("post_mix", z, lambda c: evacuated(act, JOB["out", c]))
            copy("xk", 0, two(xkT, 0))
            deviation("post_mix", D, eps_rms)
            copy("xk", 1, two(xkT, 1))
            copy("xv", 0, xv_tok[:, :, 0:S])
            squares("pre_x", h, is_normed("post_mix"))
            deviation("pre_x", D, eps_rms)
            copy("xv", 1, xv_tok[:, :, S:2 * S])
            split("xq", z, is_scaled("pre_x"))
            copy("xq", 0, two(xqT, 0))
            att_step(0, ATT0["X"], 4)
            copy("xq", 1, two(xqT, 1))
            for s in range(1, 4 + 3):
                att_step(s, ATT0["X"], 4)
            split("xo", xqT, lambda c: act.wait_ge(o_done, ATT0["X"] + 2 * c + 2), 2)
            passed("xo")
            for c in range(4):
                j = JOB["xo", 0] + c
                filled(act, j)
                f(two(z, c), lin[j % RING][:], ACT.Copy).then_inc(evac[j % RING], 1)
                evacuated(act, j)
                f(squares_of[c][:], two(z, c), ACT.Square).then_inc(squared, 1)
            deviation("post_x", D, eps_rms)

            squares("pre_ffn", h, is_normed("post_x"))
            deviation("pre_ffn", D, eps_rms)
            split("ffn", z, is_scaled("pre_ffn"))
            for s in range(FB + 2):
                if s < FB:
                    u = s
                    unit("fu", u)
                    if u >= 2:
                        act.wait_ge(ff_conv, u - 1)
                    j = JOB["fu", u]
                    f(fpad[u % 2][:, :, 2:], lin[j % RING][:], ACT.Copy).then_inc(evac[j % RING], 1)
                if 1 <= s < FB + 1:
                    u = s - 1
                    act.wait_ge(ff_conv, u + 1)
                    if u >= 2:
                        act.wait_ge(ff_y, u - 1)
                    f(fth[:, u % 2, :], fconv[:, u % 2, 0, :], ACT.Tanh, scale=0.5).then_inc(ff_tanh, 1)
                if s >= 2:
                    u = s - 2
                    act.wait_ge(ff_y, u + 1)
                    f(gh[:, u, :], fy[:, u % 2, :], ACT.Copy).then_inc(ff_hi, 1)
            for i in range(COUNT["fd"]):
                high_part(U0["fd"] + i + AHEAD)
            squares("post_ffn", z, lambda c: evacuated(act, JOB["fd", 2 * c + 1]))
            deviation("post_ffn", D, eps_rms)

        @block.vector
        def _(dve):
            v = nc.vector
            chain = Chain(dve, dve_step)
            link = chain.link

            def two(t, c):
                return t[:, 2 * c:2 * c + 2, :]

            def over(row, n=2):
                return row[:, None, :].broadcast_to([P, n, S])

            def psum(j, g=None):
                filled(dve, j, g)
                return lin[j % RING]

            def read_out(ins, j):
                ins.then_inc(evac[j % RING], 1)

            def low(event, src, c):
                dve.wait_ge(split_hi, SPLIT[event] + c + 1)
                v.tensor_tensor(two(xl, c), two(src, c), two(xh, c).bitcast(f32), ALU.subtract).then_inc(split_lo, 1)

            def inverse(name, n=2):
                for c in PAIRS.get(name, ()):
                    dve.wait_ge(squared, SQUARED[name] + c + 1)
                    sq = squares_of[c]
                    v.tensor_tensor(sq[:, 0, :], sq[:, 0, :], sq[:, 1, :], ALU.add).then_inc(paired, 1)
                evacuated(dve, JOB[name + "_sq", 0])
                v.reciprocal(inv[:, 0:n], dev[:, 0:n]).then_inc(inv_ready, 1)

            def center(name, t, width, n=4):
                j = JOB[name + "_mean", 0]
                p = psum(j)
                for c in range(n):
                    ins = v.scalar_tensor_tensor(out=two(t, c), in0=over(p[:, 0, :]), scalar=-1.0 / width, in1=two(t, c), op0=ALU.mult, op1=ALU.add)
                    if c < n - 1:
                        ins.then_inc(centered, 1)
                    else:
                        read_out(ins, j)

            def is_centered(name, n=4):
                dve.wait_ge(centered, CENTERED[name] + n - 1)
                evacuated(dve, JOB[name + "_mean", 0])

            def scale(name, c, src, dst, g_name, i=0):
                j = JOB[name + "_rstd", 0]
                p = psum(j)
                for m in (2 * c, 2 * c + 1):
                    ins = v.scalar_tensor_tensor(out=dst[:, m, :], in0=src[:, m, :], scalar=vcol(g_name, i + m), in1=p[:, 0, :], op0=ALU.mult, op1=ALU.mult)
                if c < 3:
                    ins.then_inc(scaled, 1)
                else:
                    read_out(ins, j)

            def layer_norm(name, layer, event, g_name, b_name):
                def bias(m):
                    return vcol(b_name, DB * layer + m)

                def low_biased(c):
                    dve.wait_ge(split_hi, SPLIT[event] + c + 1)
                    for m in (2 * c, 2 * c + 1):
                        ins = v.scalar_tensor_tensor(out=xl[:, m, :], in0=z[:, m, :], scalar=bias(m), in1=xh[:, m, :].bitcast(f32), op0=ALU.add, op1=ALU.subtract)
                    ins.then_inc(split_lo, 1)

                center(name, z, D)
                inverse(name)
                link(v.memset(zsum[:], 0.0))
                is_centered(name)
                for c in range(4):
                    scale(name, c, z, z, g_name, DB * layer)
                    if event and c:
                        low_biased(c - 1)
                if event:
                    low_biased(3)
                dve.wait_ge(scaled, SCALED[name] + 3)
                evacuated(dve, JOB[name + "_rstd", 0])
                for m in range(DB):
                    ins = v.tensor_scalar(h[:, m, :], z[:, m, :], bias(m), None, ALU.add)
                    if m % 2:
                        ins.then_inc(normed, 1)
                dve.wait_ge(normed, NORMED[name] + 4)

            def rms(name, src, dst, g_name, event):
                inverse(name)
                for c in range(4):
                    scale(name, c, src, dst, g_name)
                    if c:
                        low(event, dst, c - 1)
                low(event, dst, 3)

            def rms_residual(name, g_name):
                inverse(name)
                j = JOB[name + "_rstd", 0]
                p = psum(j)
                for c in range(4):
                    for m in (2 * c, 2 * c + 1):
                        ins = v.scalar_tensor_tensor(out=z[:, m, :], in0=z[:, m, :], scalar=vcol(g_name, m), in1=p[:, 0, :], op0=ALU.mult, op1=ALU.mult)
                        if m == DB - 1:
                            read_out(ins, j)
                            evacuated(dve, j)
                        elif m % 2:
                            link(ins)
                    v.tensor_tensor(two(h, c), two(h, c), two(z, c), ALU.add).then_inc(normed, 1)
                dve.wait_ge(normed, NORMED[name] + 4)

            def add_up(m, n, g=None):
                v.tensor_tensor(zsum[:, None, :], zsum[:, None, :], z[:, m, :] if g is not None else z[:, m:m + 1, :], ALU.add).then_inc(z_summed, 1)
                dve.wait_ge(z_summed, per(n, g, RING))

            def residual(name, norm):
                for i in range(4):
                    j = JOB[name, i]
                    read_out(v.scalar_tensor_tensor(out=two(z, i), in0=two(h, i), scalar=ALPHA, in1=psum(j)[:], op0=ALU.mult, op1=ALU.add), j)
                    evacuated(dve, j)
                    for m in (2 * i, 2 * i + 1):
                        add_up(m, SUMMED[norm] + m + 1)

            def att_neg(u):
                k, i, t = UNITS_ATT[u]
                dve.wait_ge(lg_ready, u + 1)
                if u >= 2:
                    dve.wait_ge(exp_done, u - 1)
                for m in range(2):
                    w = att_keys(u, m)
                    if k == "A":
                        mask = selbias[:, m, 0:w]
                    elif k == "X":
                        mask = const("zero").broadcast_to([P, S])
                    else:
                        mask = const("chunk" if k == "D" else "causal", P * (1 - (m if t is None else t)), S)
                    last = v.tensor_tensor_reduce(out=lg[u % 2][:, m, 0:w], in0=att_scores(u, m), in1=mask, scale=-(128 if k == "X" else 64) ** -0.5,
                                                  scalar=3.0e38, op0=ALU.add, op1=ALU.min, accum_out=nmax[:, u % 2, m:m + 1])
                last.then_inc(neg_ready, 1)

            def att_scale(u):
                dve.wait_ge(exp_done, u + 1)
                if u:
                    dve.wait_ge(p_ready, u)
                link(v.reciprocal(rinv[:], rsum[:, u % 2, :]))
                p0, p1 = [pr[u % 2][:, m, 0:att_keys(u, m)] for m in range(2)]
                if UNITS_ATT[u][0] == "D":
                    link(v.tensor_tensor(rinv[:, 1:2], rinv[:, 1:2], lamt[:, 4:5], ALU.mult))
                    link(v.tensor_scalar(p1, p1, rinv[:, 1:2], None, ALU.mult))
                    last = v.scalar_tensor_tensor(out=p0, in0=p0, scalar=rinv[:, 0:1], in1=p1, op0=ALU.mult, op1=ALU.subtract)
                else:
                    v.tensor_scalar(p0, p0, rinv[:, 0:1], None, ALU.mult)
                    last = v.tensor_scalar(p1, p1, rinv[:, 1:2], None, ALU.mult)
                last.then_inc(p_ready, 1)

            def att_step(s, u0, n):
                if s < n:
                    att_neg(u0 + s)
                if 1 <= s < n + 1:
                    att_scale(u0 + s - 1)

            link(v.memset(zsum[:], 0.0))
            dve.wait_ge(hi_ready, 1)
            v.tensor_tensor(wlo[0][:], raw[0][:], whi[0][:].bitcast(f32), ALU.subtract).then_inc(lo_ready, 1)
            for c in range(4):
                low("x", h, c)
            dve.wait_ge(pos_loaded, 16)
            dve.wait_ge(consts_loaded, 16)
            link(v.tensor_copy(ang[:], posi[:]))
            link(v.tensor_scalar(ang[:], ang[:], const("inv"), None, ALU.mult))
            TURN, MAGIC = 2 * np.pi, 12582912.0
            for quarter, dst in ((0.0, sinT), (0.25, cosT)):
                link(v.tensor_scalar(turns[:], ang[:], 1 / TURN, quarter, ALU.mult, ALU.add))
                link(v.tensor_scalar(turns[:], turns[:], MAGIC, None, ALU.add))
                link(v.tensor_scalar(turns[:], turns[:], MAGIC, None, ALU.subtract))
                link(v.scalar_tensor_tensor(out=dst[:], in0=turns[:], scalar=-6.28125, in1=ang[:], op0=ALU.mult, op1=ALU.add))
                link(v.scalar_tensor_tensor(out=dst[:], in0=turns[:], scalar=-(TURN - 6.28125), in1=dst[:], op0=ALU.mult, op1=ALU.add))
                link(v.tensor_scalar(dst[:], dst[:], quarter * TURN, 3.1415925, ALU.add, ALU.min))
                v.tensor_scalar(dst[:], dst[:], -3.1415925, None, ALU.max).then_inc(reduced, 1)
            dve.wait_ge(vec_loaded, 16)
            link(v.tensor_scalar(hvec[:, 0:32], vec[:, COL["b_gate_2"]:COL["b_gate_2"] + 32], 0.5, None, ALU.mult))
            link(v.tensor_scalar(hvec[:, 32:40], vec[:, COL["b_glu_2"]:COL["b_glu_2"] + 8], 0.5, None, ALU.mult))
            link(v.tensor_scalar(hvec[:, 40:41], vcol("diff_norm_2"), 0.8, None, ALU.mult))
            dve.wait_ge(trig, 2)
            link(v.tensor_scalar(cosT[:], cosT[:], const("rot"), const("norot"), ALU.mult, ALU.add))

            def rope(r, dst):
                j = JOB["rope", r]
                n = dst.shape[1]
                p = psum(j)
                read_out(v.tensor_tensor(rtmp[:, 0:n, :], p[:, 0:n, :], over(sinT, n), ALU.mult), j)
                link(v.tensor_tensor(dst, dst, over(cosT, n), ALU.mult))
                evacuated(dve, j)
                v.tensor_tensor(dst, dst, rtmp[:, 0:n, :], ALU.add).then_inc(roped, 1)
                dve.wait_ge(roped, r + 1)

            j = JOB["iw", 0]
            read_out(v.tensor_scalar(iw[:], psum(j)[:, :, 0:8], 8 ** -0.5, None, ALU.mult), j)
            rope(0, two(iqT, 0))
            rope(1, two(iqT, 1))
            rope(2, ikT[:])
            rope(3, kT[:])
            v.tensor_copy(kswap[0:64, :, :], kT[64:128, :, :]).then_inc(kswapped, 1)
            v.tensor_copy(kswap[64:128, :, :], kT[0:64, :, :]).then_inc(kswapped, 1)
            for i in range(6):
                evacuated(dve, JOB["idx", i])
                t, heads = (0, range(i, 8, 2)) if i < 2 else (1, [(0, 2), (4, 6), (1, 3), (5, 7)][i - 2])
                w = P * (t + 1)
                for n, hd in enumerate(heads):
                    first = i in (0, 2) and n == 0
                    ins = v.scalar_tensor_tensor(out=work[:, t, 0:w], in0=rbuf[i % 2][:, n * w:(n + 1) * w], scalar=iw[:, t, hd:hd + 1],
                                                 in1=const("causal", P * (1 - t), S) if first else work[:, t, 0:w], op0=ALU.mult, op1=ALU.add)
                    if n < len(heads) - 1:
                        link(ins)
                ins.then_inc(idx_acc, 1)
                dve.wait_ge(idx_acc, i + 1)
            for t in range(2):
                w = P * (t + 1)
                for _ in range(TOPK // 8):
                    link(v.max(top8[:], work[:, t, 0:w]))
                    link(v.match_replace(work[:, t, 0:w], top8[:], work[:, t, 0:w], TAKEN))
                link(v.tensor_scalar(selbias[:, t, 0:w], work[:, t, 0:w], TAKEN, NEG, ALU.not_equal, ALU.mult))
                link(v.tensor_tensor(selbias[:, t, 0:w], selbias[:, t, 0:w], const("causal", P * (1 - t), S), ALU.add))
            rope(4, two(qT, 0))
            for s in range(16 + 1):
                att_step(s, ATT0["A"], 16)
                if s < 3:
                    rope(5 + s, two(qT, 1 + s))
            for c in range(4):
                low("ao", qT, c)
            residual("ao", "ln0")
            layer_norm("ln0", 0, "mlp0", "ln_mix_g", "ln_mix_b")

            def mlp(layer):
                for half in range(2):
                    up, dn = f"up{layer}{half}", f"dn{layer}{half}"
                    base = 8 * (2 * layer + half)
                    with dve.Fori(0, 2) as g:
                        for i in range(RING):
                            evacuated(dve, JOB[up, i], g)
                            v.tensor_tensor(sqr[i % 2][:], relu[i % 2][:], relu[i % 2][:], ALU.mult).then_inc(sqr_done, 1)
                            dve.wait_ge(fhi, per(base + i + 1, g, RING))
                            at = bass.ds(g * 8 + 2 * i, 2)
                            v.tensor_tensor(fl[:, at, :], sqr[i % 2][:], fh[:, at, :].bitcast(f32), ALU.subtract).then_inc(flo, 1)
                    with dve.Fori(0, 2) as g:
                        for i in range(RING):
                            j = JOB[dn, i]
                            p = psum(j, g)
                            m = bass.ds(g * 4 + i, 1)
                            if half == 0:
                                ins = v.scalar_tensor_tensor(out=z[:, m, :], in0=h[:, m, :], scalar=ALPHA, in1=p[:, 0:1, :], op0=ALU.mult, op1=ALU.add)
                            else:
                                ins = v.tensor_tensor(z[:, m, :], z[:, m, :], p[:, 0:1, :], ALU.add)
                            read_out(ins, j)
                            if half:
                                evacuated(dve, j, g)
                                add_up(m, SUMMED[f"ln{2 * layer + 1}"] + i + 1, g)
                layer_norm(f"ln{2 * layer + 1}", layer, "gla" if layer == 0 else None, "ln_mlp_g", "ln_mlp_b")

            mlp(0)

            for i in range(2):
                j = JOB["gate_a", i]
                p = psum(j)
                for n in range(2):
                    ins = v.tensor_scalar(gtmp[:, 2 * i + n, :], p[:, n, :], vcol("b_b_a", 2 * i + n), None, ALU.add)
                read_out(ins, j)
            evacuated(dve, JOB["gate_a", 0])
            evacuated(dve, JOB["gate_a", 1])
            dve.wait_ge(softplus, 1)
            link(v.tensor_scalar(gtmp[:], gtmp[:], 0.0, None, ALU.min))
            link(v.tensor_tensor(gtmp[:], gtmp[:], decay[:], ALU.subtract))
            for hd in range(4):
                ins = v.tensor_tensor_scan(out=bcum[:, hd, :], data0=const("scan"), data1=gtmp[:, hd, :], initial=0.0, op0=ALU.mult, op1=ALU.add)
                link(ins)
            flat_b = bcum[:].rearrange("p a s -> p (a s)")
            flat_t = gtmp[:].rearrange("p a s -> p (a s)")
            masked = z[:, 0:2, :].rearrange("p a (b s) -> p (a b) s", s=64)

            def level_args(l):
                half = 32 >> l
                if l:
                    dve.wait_ge(lvl_exp, l)
                b, out = [x.rearrange("p (n two w) -> p n two w", two=2, w=half) for x in (flat_b, flat_t)]
                r = b[:, :, 0, half - 1:half].broadcast_to([P, 4 * S // (2 * half), half])
                v.tensor_tensor(out[:, :, 0, :], r, b[:, :, 0, :], ALU.subtract)
                v.tensor_tensor(out[:, :, 1, :], b[:, :, 1, :], r, ALU.subtract).then_inc(lvl_arg, 1)

            def level_pairs(l):
                half = 32 >> l
                dve.wait_ge(lvl_exp, l + 1)
                if l >= 2:
                    filled(dve, JOB["level", l - 2])
                for side, src in ((0, gkT), (1, gqT)):
                    part = [t.rearrange("p a (n two w) -> p (a n) two w", two=2, w=half)[:, :, side, :] for t in (qk[:, 4 * (l % 2):4 * (l % 2) + 4, :], src[:], decay[:])]
                    ins = v.tensor_tensor(part[0], part[1], part[2], ALU.mult)
                ins.then_inc(lvl_qk, 1)

            def level_sum(l):
                j = JOB["level", l]
                p = psum(j)[:].rearrange("p a (b s) -> p (a b) s", s=64)
                mask = const("level", 64 * l, 64 * l + 64)[:, None, :].broadcast_to([P, 8, 64])
                if l == 0:
                    read_out(v.tensor_tensor(attnT[:], p, mask, ALU.mult), j)
                    evacuated(dve, j)
                    return
                read_out(v.tensor_tensor(masked, p, mask, ALU.mult), j)
                evacuated(dve, j)
                if l < 6:
                    v.tensor_tensor(attnT[:], attnT[:], masked, ALU.add).then_inc(attn_acc, 1)
                    dve.wait_ge(attn_acc, l)
                    return
                for r in (0, 64):
                    v.tensor_tensor(attnD[r:r + 64, :, r:r + 64], attnT[r:r + 64], masked[r:r + 64], ALU.add).then_inc(attn_acc, 1)

            def gr_silu(i):
                j = JOB["gr", i]
                dve.wait_ge(gr_tanh, i + 1)
                read_out(v.scalar_tensor_tensor(out=two(rgate, i), in0=two(rgate, i), scalar=1.0, in1=lin[j % RING][:], op0=ALU.add, op1=ALU.mult), j)

            level_args(0)
            link(v.memset(attnD[:], 0.0))
            for i in range(2):
                evacuated(dve, JOB["gq", i])
                evacuated(dve, JOB["gk", i])
            for l in range(6):
                level_pairs(l)
                if l < 5:
                    level_args(l + 1)
                else:
                    dve.wait_ge(lvl_exp, 6)
                    b = flat_b.rearrange("p (n w) -> p n w", w=64)
                    v.tensor_tensor(flat_t.rearrange("p (n w) -> p n w", w=64), b, b[:, :, 63:64].broadcast_to([P, 16, 64]), ALU.subtract).then_inc(lvl_arg, 1)
                if l - 1 in GLA_FILL:
                    gr_silu(GLA_FILL[l - 1][1])
                if l:
                    level_sum(l - 1)
            level_sum(5)
            dve.wait_ge(lvl_exp, 8)
            v.tensor_tensor(qk[:, 0:4, :], gkT[:], gtmp[:], ALU.mult).then_inc(kd_ready, 1)
            level_sum(6)
            v.tensor_tensor(gqT[:], gqT[:], decay[:], ALU.mult).then_inc(q_decayed, 1)
            gr_silu(2)
            for i in range(2):
                j = JOB["state", i]
                read_out(v.tensor_copy(two(state[0], i), psum(j)[:]), j)
                evacuated(dve, j)
            for c in (1, 2):
                for i in range(2):
                    dve.wait_ge(state_psum, 2 * c - 1 + i)
                    if c == 2:
                        dve.wait_ge(state_ready, i + 1)
                    for n in range(2):
                        hd = 2 * i + n
                        ins = v.scalar_tensor_tensor(out=state[c][:, hd, :], in0=state[c - 1][:, hd, :], scalar=decay[:, hd, c * 64 + 63:c * 64 + 64],
                                                     in1=att[2 * c - 2 + i][:, n * S:(n + 1) * S], op0=ALU.mult, op1=ALU.add)
                    ins.then_inc(state_ready, 1)
            def gated(hd):
                evacuated(dve, JOB["gla_o", hd // 2])
                evacuated(dve, JOB["gla_o", 2 + hd // 2])
                for dv in range(2):
                    m = 2 * hd + dv
                    ins = v.scalar_tensor_tensor(out=rgate[:, m, :], in0=rgate[:, m, :], scalar=vcol("b_g_norm", dv), in1=qk[:, m, :], op0=ALU.mult, op1=ALU.mult)
                link(ins)

            for i in range(3):
                evacuated(dve, JOB["gr", i])
                gated(i)
            gr_silu(3)
            evacuated(dve, JOB["gr", 3])
            gated(3)
            inverse("gla", 8)
            for hd in range(4):
                j = JOB["gla_rstd", hd // 2]
                p = psum(j)
                if hd % 2:
                    ins = v.scalar_tensor_tensor(out=two(qk, hd), in0=two(rgate, hd), scalar=0.5, in1=over(p[:, 1, :]), op0=ALU.mult, op1=ALU.mult)
                    read_out(ins, j)
                else:
                    ins = v.scalar_tensor_tensor(out=two(qk, hd), in0=two(rgate, hd), scalar=0.5, in1=over(p[:, 0, :]), op0=ALU.mult, op1=ALU.mult)
                    ins.then_inc(gla_y, 1)
                if hd:
                    low("go", qk, hd - 1)
            low("go", qk, 3)
            residual("go", "ln2")
            layer_norm("ln2", 1, "mlp1", "ln_mix_g", "ln_mix_b")
            mlp(1)

            rms("pre_mix", h, z, "norm_mix_pre_2", "mix")
            dve.wait_ge(mix_loaded, 48)
            for i in range(2):
                v.tensor_tensor_reduce(out=pr[0][:, i, 0:64], in0=lamv[:, 2 * i, :], in1=lamv[:, 2 * i + 1, :], scale=1.0, scalar=0.0,
                                       op0=ALU.mult, op1=ALU.add, accum_out=lamt[:, i:i + 1]).then_inc(lam_dot, 1)
            link(v.memset(upad[:, :, 0:CPAD], 0.0))
            link(v.memset(scpad[:, :, 0:2], 0.0))
            j = JOB["fg", 0]
            read_out(v.tensor_scalar(fgt[:], psum(j)[0:8, 0, :], bfg[:], None, ALU.add), j)
            dve.wait_ge(fg_soft, 1)
            link(v.tensor_scalar(fgt[:], fgt[:], 0.0, None, ALU.min))
            link(v.tensor_tensor(fgt[:], fgt[:], fc[:], ALU.subtract))
            link(v.tensor_tensor_scan(out=fc[:], data0=const("ones")[0:8, :], data1=fgt[:], initial=0.0, op0=ALU.mult, op1=ALU.add))
            v.tensor_scalar(fc[:], fc[:], -8.0, None, ALU.mult).then_inc(fc_ready, 1)
            dve.wait_ge(lam_exp, 1)
            link(v.tensor_tensor(lamt[:, 4:5], lamt[:, 2:3], lamt[:, 3:4], ALU.subtract))
            link(v.tensor_scalar(lamt[:, 4:5], lamt[:, 4:5], 0.8 - 0.6, None, ALU.add))

            def conv_taps(n0, n1):
                for n in range(n0, min(n1, 4 * CONV_K)):
                    k, b = n // 4, n % 4
                    x, w = upad[:, b, k:k + S], vcol("conv_dw_2", 4 * k + b)
                    if k == 0:
                        ins = v.tensor_scalar(conv[:, b, :], x, w, vcol("conv_dw_b_2", b), ALU.mult, ALU.add)
                    else:
                        ins = v.scalar_tensor_tensor(out=conv[:, b, :], in0=x, scalar=w, in1=conv[:, b, :], op0=ALU.mult, op1=ALU.add)
                    if n == 4 * CONV_K - 1:
                        ins.then_inc(conv_done, 1)
                    else:
                        link(ins)

            def short_conv(i):
                evacuated(dve, JOB["s", 3 * i + 2])
                evacuated(dve, JOB["s", 3 * i + 1])
                for m in range(2):
                    b = 2 * i + m
                    acc = mtmp[1][:, m, :]
                    link(v.tensor_scalar(acc, scpad[:, m, 0:S], vcol("sc_w_2", b), None, ALU.mult))
                    for k in (1, 2):
                        link(v.scalar_tensor_tensor(out=acc, in0=scpad[:, m, k:k + S], scalar=vcol("sc_w_2", 4 * k + b), in1=acc, op0=ALU.mult, op1=ALU.add))
                v.tensor_tensor(two(sgate, i), two(sgate, i), mtmp[1][:], ALU.mult).then_inc(b_y, 1)

            def branch_low(n, src):
                for c in range(2):
                    dve.wait_ge(b_hi, 2 * n + c + 1)
                    v.tensor_tensor(two(blo, c), two(src, c), two(bhi, c).bitcast(f32), ALU.subtract).then_inc(b_lo, 1)

            def branch_sum(n, b, i, event=None):
                for c in (2 * i, 2 * i + 1):
                    j = JOB[f"br{b}", 0] + c
                    t = mtmp[c % 2]
                    read_out(v.scalar_tensor_tensor(out=t[:], in0=two(gate, c), scalar=1.0, in1=psum(j)[:], op0=ALU.add, op1=ALU.mult), j)
                    evacuated(dve, j)
                    if n == 0:
                        ins = v.tensor_scalar(two(z, c), t[:], 0.5, None, ALU.mult)
                    else:
                        ins = v.scalar_tensor_tensor(out=two(z, c), in0=t[:], scalar=0.5, in1=two(z, c), op0=ALU.mult, op1=ALU.add)
                    ins.then_inc(mixed, 1)
                    dve.wait_ge(mixed, 4 * n + c + 1)
                    if event and c:
                        low(event, z, c - 1)

            TAPS = 8
            for s in range(10):
                if s < 4 and s % 2:
                    j = JOB["c", s]
                    evacuated(dve, JOB["c", s - 1])
                    link(v.tensor_scalar(mtmp[0][:], mtmp[0][:], 0.5, 0.5, ALU.mult, ALU.add))
                    p = psum(j)
                    for m in range(2):
                        b = s - 1 + m
                        ins = v.scalar_tensor_tensor(out=upad[:, b, CPAD:], in0=p[:, m, :], scalar=vcol("b_glu_2", b), in1=mtmp[0][:, m, :], op0=ALU.add, op1=ALU.mult)
                    read_out(ins, j)
                elif s >= 4 and (s - 4) % 3 == 1:
                    i = s - 4
                    j = JOB["s", i]
                    evacuated(dve, JOB["s", i - 1])
                    read_out(v.tensor_tensor(scpad[:, :, 2:], mtmp[1][:], psum(j)[:], ALU.mult), j)
                elif s >= 4 and (s - 4) % 3 == 2:
                    short_conv((s - 4) // 3)
                att_step(s, ATT0["D"], 16)
                if s == 4:
                    evacuated(dve, JOB["c", 1])
                    evacuated(dve, JOB["c", 3])
                if s >= 4:
                    conv_taps(TAPS * (s - 4), TAPS * (s - 3))
            att_step(10, ATT0["D"], 16)
            for i in range(1, 4):
                if i == 2:
                    inverse("ya", 8)
                elif i == 3:
                    for c in range(2):
                        j = JOB["ya_rstd", c]
                        p = psum(j)
                        for n in range(2):
                            hd = 2 * c + n
                            ins = v.scalar_tensor_tensor(out=aqT[:, hd, :], in0=aqT[:, hd, :], scalar=hvec[:, 40:41], in1=p[:, n, :], op0=ALU.mult, op1=ALU.mult)
                        read_out(ins, j)
                    branch_low(0, aqT)
                att_step(10 + i, ATT0["D"], 16)
                conv_taps(TAPS * (5 + i), TAPS * (6 + i))
            for i in range(2):
                att_step(14 + i, ATT0["D"], 16)
                branch_sum(0, 0, i)
            for i in range(4):
                att_step(16 + i, ATT0["D"], 16)
                if i == 0:
                    branch_low(1, sgate)
                conv_taps(TAPS * (9 + i), TAPS * (10 + i))
            for i in range(2):
                branch_sum(1, 3, i)
            conv_taps(TAPS * 13, 4 * CONV_K)
            branch_low(2, fqT)
            center("conv", conv, 512, 2)
            inverse("conv")
            is_centered("conv", 2)
            j = JOB["conv_rstd", 0]
            p = psum(j)
            for b in range(4):
                ins = v.scalar_tensor_tensor(out=conv[:, b, :], in0=conv[:, b, :], scalar=vcol("conv_ln_g_2", b), in1=p[:, 0, :], op0=ALU.mult, op1=ALU.mult)
                if b < 3:
                    link(ins)
                else:
                    read_out(ins, j)
                    evacuated(dve, j)
            for b in range(4):
                ins = v.tensor_scalar(conv[:, b, :], conv[:, b, :], vcol("conv_ln_b_2", b), None, ALU.add)
                if b % 2:
                    ins.then_inc(conv_normed, 1)
            for c in range(2):
                dve.wait_ge(conv_tanh, c + 1)
                link(v.tensor_scalar(mtmp[c][:], mtmp[c][:], 0.5, 0.5, ALU.mult, ALU.add))
                v.tensor_tensor(two(conv, c), two(conv, c), mtmp[c][:], ALU.mult).then_inc(b_y, 1)
            dve.wait_ge(b_y, 4)
            for i in range(2):
                branch_sum(2, 1, i)
            branch_low(3, conv)
            for i in range(2):
                branch_sum(3, 2, i, "out")
            low("out", z, 3)

            inverse("mem")
            for c in range(4):
                scale("mem", c, memT, memT, "norm_mem_2")
            for c in range(4):
                low("mem", memT, c)
            rms_residual("post_mix", "norm_mix_post_2")
            rms("pre_x", h, z, "norm_x_pre_2", "xq")
            for s in range(4 + 1):
                att_step(s, ATT0["X"], 4)
            for c in range(2):
                low("xo", xqT, c)
            rms_residual("post_x", "norm_x_post_2")

            for i in range(2):
                link(v.memset(fpad[i][:, :, 0:2], 0.0))
            rms("pre_ffn", h, z, "norm_ffn_pre_2", "ffn")
            for s in range(FB + 2):
                if s < FB:
                    u = s
                    evacuated(dve, JOB["fu", u])
                    for m in range(2):
                        x, acc, b = fpad[u % 2][:, m, :], fconv[:, u % 2, m, :], FB * m + u
                        link(v.tensor_scalar(acc, x[:, 0:S], vcol("ffn_dw_2", b), vcol("ffn_dw_b_2", b), ALU.mult, ALU.add))
                        link(v.scalar_tensor_tensor(out=acc, in0=x[:, 1:1 + S], scalar=vcol("ffn_dw_2", 2 * FB + b), in1=acc, op0=ALU.mult, op1=ALU.add))
                        ins = v.scalar_tensor_tensor(out=acc, in0=x[:, 2:2 + S], scalar=vcol("ffn_dw_2", 4 * FB + b), in1=acc, op0=ALU.mult, op1=ALU.add)
                        if m == 0:
                            link(ins)
                    ins.then_inc(ff_conv, 1)
                if 1 <= s < FB + 1:
                    u = s - 1
                    dve.wait_ge(ff_tanh, u + 1)
                    if u >= 2:
                        dve.wait_ge(ff_lo, u - 1)
                    link(v.scalar_tensor_tensor(out=fy[:, u % 2, :], in0=fth[:, u % 2, :], scalar=1.0, in1=fconv[:, u % 2, 0, :], op0=ALU.add, op1=ALU.mult))
                    v.scalar_tensor_tensor(out=fy[:, u % 2, :], in0=fy[:, u % 2, :], scalar=0.5, in1=fconv[:, u % 2, 1, :], op0=ALU.mult, op1=ALU.mult).then_inc(ff_y, 1)
                if s >= 2:
                    u = s - 2
                    dve.wait_ge(ff_hi, u + 1)
                    v.tensor_tensor(gl[:, u, :], fy[:, u % 2, :], gh[:, u, :].bitcast(f32), ALU.subtract).then_inc(ff_lo, 1)
            for i in range(DB):
                j = JOB["fd", i]
                read_out(v.tensor_copy(z[:, i, :], psum(j)[:, 0, :]), j)
            rms_residual("post_ffn", "norm_ffn_post_2")


def tiles_up(w, blocks):
    out = []
    for pair in blocks:
        cols = np.concatenate([np.arange(c, c + P) for c in pair])
        kb = w.shape[0] // P
        out.append(w[:, cols].reshape(kb, P, len(pair), P).transpose(1, 2, 0, 3).reshape(P, -1))
    return out


def pairs(start, n, step=P):
    return [(start + 2 * i * step, start + (2 * i + 1) * step) for i in range(n // 2)]


def tiles_tok(w, start, n):
    return [w[:, start + i * S:start + (i + 1) * S].reshape(DB, P, S).transpose(1, 0, 2).reshape(P, -1) for i in range(n)]


def tiles_wide(w):
    return tiles_up(w, [tuple(range(i * 512, i * 512 + 512, P)) for i in range(2)])


def tiles_down(w):
    return tiles_up(w, [(i * P,) for i in range(8)])


def weight_units(i):
    a, b, w2, br = i["a_w_in"][0], i["b_w_in"][0], i["w_in_2"][0], i["w_branch_2"][0]
    wg, up, dn = i["w_gate_2"][0], i["w_up_2"][0], i["w_down_2"][0]
    g = {"iq": tiles_up(a, pairs(1536, 4)), "k": tiles_up(a, pairs(1024, 2)), "v": tiles_tok(a, 1280, 1),
         "q": tiles_up(a, pairs(0, 8)), "ao": tiles_up(i["a_w_o"][0], pairs(0, 8)),
         "gq": tiles_up(b, pairs(0, 4)), "gk": tiles_up(b, pairs(512, 4)), "gv": tiles_tok(b, 1024, 4),
         "gr": tiles_up(b, pairs(2048, 8)), "go": tiles_up(i["b_w_o"][0], pairs(0, 8)),
         "aq": tiles_up(w2, pairs(0, 4)), "ak": tiles_up(w2, pairs(512, 4)), "av": tiles_tok(w2, 1024, 2),
         "fq": tiles_up(w2, pairs(1536, 4)), "fk": tiles_up(w2, pairs(2048, 4)), "fv": tiles_tok(w2, 2560, 2)}
    c0 = 3080
    g["c"] = tiles_up(w2, [p for n in range(2) for p in (pairs(c0 + 512 + 256 * n, 2) + pairs(c0 + 256 * n, 2))])
    s0 = c0 + 1024
    g["s"] = tiles_up(w2, [p for n in range(2) for at in (1024, 0, 512) for p in pairs(s0 + at + 256 * n, 2)])
    for layer in range(2):
        for half in range(2):
            g[f"up{layer}{half}"] = tiles_up(i["mlp_w_up"][layer], pairs(2048 * half, 16))
            g[f"dn{layer}{half}"] = tiles_down(i["mlp_w_down"][layer][2048 * half:2048 * half + 2048])
    for n in range(4):
        g[f"gate{n}"] = tiles_up(wg, pairs(D * n, 8))
        g[f"br{n}"] = tiles_wide(br[n])
    g["out"] = tiles_up(i["w_out_2"][0], pairs(0, 8))
    g["xq"] = tiles_up(i["w_xq_2"][0], pairs(0, 4))
    g["xk"] = tiles_up(i["w_xkv_2"][0], pairs(0, 4))
    g["xv"] = tiles_tok(i["w_xkv_2"][0], 512, 2)
    g["xo"] = tiles_wide(i["w_xo_2"][0])
    g["fu"] = tiles_up(up, [(P * b, P * (FB + b)) for b in range(FB)])
    g["fd"] = np.split(np.concatenate(tiles_down(dn), 1), COUNT["fd"], 1)
    return np.stack([unit for name, _ in UNITS for unit in g[name]])


def by_partition(w):
    return np.ascontiguousarray(w.reshape(-1, P, w.shape[1]).transpose(1, 0, 2))


def kernel(**inputs):
    import concourse.bacc as bacc
    from concourse.bass_utils import run_bass_kernel_spmd

    i = {k: np.asarray(v) for k, v in inputs.items()}
    a, b, w2 = i["a_w_in"][0], i["b_w_in"][0], i["w_in_2"][0]
    ik = a[:, 2048:2112]
    arrays = {
        "units": weight_units(i),
        "x": by_partition(np.ascontiguousarray(i["x"][0].T)),
        "mem": by_partition(np.ascontiguousarray(i["mem_2"][0].T)),
        "pos": np.ascontiguousarray(i["positions"][0]),
        "vectors": np.ascontiguousarray(np.concatenate([i[n].reshape(-1, P) for n, _ in VECTORS]).T),
        "consts": shape_constants(),
        "narrow_a": by_partition(np.concatenate([ik, ik, a[:, 2112:2120]], 1)),
        "narrow_b": by_partition(b[:, 3072:3088]),
        "narrow_f": by_partition(w2[:, 3072:3080]),
        "w_a2": np.ascontiguousarray(i["b_w_a2"][0]),
        "b_fgt": np.ascontiguousarray(i["b_fgt_2"][0][:, None]),
        "lam": np.ascontiguousarray(np.stack([i[n + "_2"][0] for n in ("lam_q1", "lam_k1", "lam_q2", "lam_k2")])),
    }
    nc = bacc.Bacc("TRN2", target_bir_lowering=False, num_devices=1)
    args = [nc.dram_tensor(n + "_dram", v.shape, mybir.dt.from_np(v.dtype), kind="ExternalInput").ap() for n, v in arrays.items()]
    out = nc.dram_tensor("out_dram", (P, DB, S), mybir.dt.float32, kind="ExternalOutput").ap()
    build(nc, *args, out)
    r = run_bass_kernel_spmd(nc, [{n + "_dram": v for n, v in arrays.items()}], core_ids=[0])
    y = r.results[0]["out_dram"]
    return np.ascontiguousarray(y.transpose(2, 1, 0).reshape(1, S, D))
```
